# Optimizing a Trainium2 kernel written in Bass

```python
import math
import jax, jax.numpy as jnp
from jax import lax
import numpy as np

D_MODEL = 1024
BATCH = 1
SEQ = 512
DEPTH = 1
DEC_BATCH = 8
DEC_SEQ = 8
PAST_LEN = 4096
PAGE_SIZE = 128

D_INNER = 2 * D_MODEL
SSD_HEAD_DIM = 64
SSD_HEADS = D_INNER // SSD_HEAD_DIM
SSD_GROUPS = 4
HEADS_PER_GROUP = SSD_HEADS // SSD_GROUPS
D_STATE = 128
D_CONV = 4
CONV_DIM = D_INNER + 2 * SSD_GROUPS * D_STATE
SSD_CHUNK = 128
MLA_HEADS = 8
Q_LORA = D_MODEL // 4
KV_LORA = D_MODEL // 4
QK_NOPE = 128
ROPE_DIM = 64
V_HEAD = 128
ROPE_THETA = 10000.0
ATTN_SCALE = (QK_NOPE + ROPE_DIM) ** -0.5
Q_BLOCK = 128
N_EXPERTS = 32
TOP_K = 4
D_FF = D_MODEL
SWIGLU_ALPHA = 1.702
SWIGLU_LIMIT = 7.0
MOE_BLOCK = 128
DN_ALPHA = (2 * DEPTH) ** 0.25
DN_BETA = (8 * DEPTH) ** -0.25
LN_EPS = 1e-5
RMS_EPS = 1e-6
IN_SIZES = (Q_LORA, KV_LORA, ROPE_DIM, D_INNER, CONV_DIM, SSD_HEADS, D_MODEL, D_MODEL)
IN_SPLITS = tuple(int(s) for s in np.cumsum(IN_SIZES)[:-1])
D_IN_TOTAL = int(sum(IN_SIZES))

kernel_name = 'hybrid_ssd_mla_moe_deepnorm_step'

def layer_norm(x, g, b):
    xf = x.astype(jnp.float32)
    mu = jnp.mean(xf, axis=-1, keepdims=True)
    var = jnp.mean(jnp.square(xf - mu), axis=-1, keepdims=True)
    out = (xf - mu) * lax.rsqrt(var + LN_EPS) * g.astype(jnp.float32) + b.astype(jnp.float32)
    return out.astype(x.dtype)

def rms_norm(x, g):
    xf = x.astype(jnp.float32)
    out = xf * lax.rsqrt(jnp.mean(xf * xf, axis=-1, keepdims=True) + RMS_EPS) * g.astype(jnp.float32)
    return out.astype(x.dtype)

def rope(x, pos):
    half = ROPE_DIM // 2
    inv = ROPE_THETA ** (-jnp.arange(half, dtype=jnp.float32) / half)
    ang = pos.astype(jnp.float32)[:, None] * inv[None, :]
    ang = ang.reshape((ang.shape[0],) + (1,) * (x.ndim - 3) + (half,))
    cos, sin = jnp.cos(ang), jnp.sin(ang)
    x1 = x[..., :half].astype(jnp.float32)
    x2 = x[..., half:].astype(jnp.float32)
    return jnp.concatenate([x1 * cos - x2 * sin, x2 * cos + x1 * sin], axis=-1).astype(x.dtype)

def causal_conv(xbc, conv_state, w, b):
    t = xbc.shape[1]
    full = jnp.concatenate([conv_state.astype(xbc.dtype), xbc], axis=1)
    out = b
    for k in range(D_CONV):
        out = out + full[:, k:k + t] * w[k]
    return jax.nn.silu(out), full[:, t:]

def ssd_scan(x, dt, a, bm, cm, h0):
    b, t = x.shape[:2]
    ln = SSD_CHUNK if t % SSD_CHUNK == 0 else t
    nc = t // ln
    f32 = jnp.float32
    x = x.astype(f32).reshape((b, nc, ln) + x.shape[2:])
    dt = dt.astype(f32).reshape((b, nc, ln) + dt.shape[2:])
    bm = bm.astype(f32).reshape((b, nc, ln) + bm.shape[2:])
    cm = cm.astype(f32).reshape((b, nc, ln) + cm.shape[2:])
    a_cs = jnp.cumsum(dt * a, axis=2)
    causal = jnp.tril(jnp.ones((ln, ln), dtype=bool))
    seg = a_cs[:, :, :, None] - a_cs[:, :, None, :]
    decay_ls = jnp.exp(jnp.where(causal[:, :, None, None], seg, -jnp.inf))
    cb = jnp.einsum('bclgn,bcsgn->bclsg', cm, bm)
    w_ls = cb[..., None] * decay_ls * dt[:, :, None]
    y_diag = jnp.einsum('bclsgh,bcsghp->bclghp', w_ls, x)
    decay_end = jnp.exp(a_cs[:, :, -1:] - a_cs)
    states = jnp.einsum('bclgn,bclgh,bclghp->bcghpn', bm, decay_end * dt, x)
    chunk_decay = jnp.exp(a_cs[:, :, -1])

    def step(h, inp):
        s_c, d_c = inp
        return d_c[..., None, None] * h + s_c, h

    h_final, h_prev = lax.scan(step, h0.astype(f32),
                               (jnp.moveaxis(states, 1, 0), jnp.moveaxis(chunk_decay, 1, 0)))
    h_prev = jnp.moveaxis(h_prev, 0, 1)
    y_off = jnp.einsum('bclgn,bcghpn->bclghp', cm, h_prev) * jnp.exp(a_cs)[..., None]
    y = (y_diag + y_off).reshape((b, t) + y_diag.shape[3:])
    return y, h_final

def latent_attention(q_lat, q_rope, c, kr, q_pos, k_pos):
    s = (jnp.einsum('bqhr,bkr->bhqk', q_lat, c)
         + jnp.einsum('bqhp,bkp->bhqk', q_rope, kr)).astype(jnp.float32) * ATTN_SCALE
    s = jnp.where(k_pos[None, :] <= q_pos[:, None], s, -jnp.inf)
    pr = jax.nn.softmax(s, axis=-1).astype(c.dtype)
    return jnp.einsum('bhqk,bkr->bqhr', pr, c)

def blocked_attention(q_lat, q_rope, c, kr, q_pos, k_pos):
    b, t, h, r = q_lat.shape
    qb = Q_BLOCK if t % Q_BLOCK == 0 else t
    nb = t // qb
    ql = jnp.moveaxis(q_lat.reshape(b, nb, qb, h, r), 1, 0)
    qr = jnp.moveaxis(q_rope.reshape(b, nb, qb, h, ROPE_DIM), 1, 0)
    qp = q_pos.reshape(nb, qb)
    o = lax.map(lambda arg: latent_attention(arg[0], arg[1], c, kr, arg[2], k_pos), (ql, qr, qp))
    return jnp.moveaxis(o, 0, 1).reshape(b, t, h, r)

def token_mixers(x, conv_state, ssm_state, c_past, kr_past, pos0, p):
    b, t, _ = x.shape
    proj = x @ p['w_in']
    q_a, kv_a, kr_raw, z, xbc, dt_raw, g_a, g_b = jnp.split(proj, IN_SPLITS, axis=-1)
    pos = pos0 + jnp.arange(t, dtype=jnp.int32)
    xbc, new_conv = causal_conv(xbc, conv_state, p['ssd_conv_w'], p['ssd_conv_b'])
    xs, bm, cm = jnp.split(xbc, [D_INNER, D_INNER + SSD_GROUPS * D_STATE], axis=-1)
    xs = xs.reshape(b, t, SSD_GROUPS, HEADS_PER_GROUP, SSD_HEAD_DIM)
    bm = bm.reshape(b, t, SSD_GROUPS, D_STATE)
    cm = cm.reshape(b, t, SSD_GROUPS, D_STATE)
    dt = jax.nn.softplus(dt_raw.astype(jnp.float32) + p['ssd_dt_bias'].astype(jnp.float32))
    dt = dt.reshape(b, t, SSD_GROUPS, HEADS_PER_GROUP)
    a = -jnp.exp(p['ssd_a_log'].astype(jnp.float32)).reshape(SSD_GROUPS, HEADS_PER_GROUP)
    h0 = ssm_state.reshape(b, SSD_GROUPS, HEADS_PER_GROUP, SSD_HEAD_DIM, D_STATE)
    y, h_final = ssd_scan(xs, dt, a, bm, cm, h0)
    y = y + p['ssd_d'].astype(jnp.float32).reshape(SSD_GROUPS, HEADS_PER_GROUP)[:, :, None] * xs.astype(jnp.float32)
    y = y.reshape(b, t, D_INNER) * jax.nn.silu(z.astype(jnp.float32))
    y = rms_norm(y.reshape(b, t, SSD_GROUPS, D_INNER // SSD_GROUPS),
                 p['ssd_norm_g'].reshape(SSD_GROUPS, D_INNER // SSD_GROUPS))
    y_a = y.reshape(b, t, D_INNER).astype(x.dtype) @ p['w_branch_a']
    q = (rms_norm(q_a, p['mla_q_norm_g']) @ p['w_q_b']).reshape(b, t, MLA_HEADS, QK_NOPE + ROPE_DIM)
    q_nope = q[..., :QK_NOPE]
    q_rope = rope(q[..., QK_NOPE:], pos)
    c_new = rms_norm(kv_a, p['mla_kv_norm_g'])
    kr_new = rope(kr_raw, pos)
    w_kv = p['w_kv_b'].reshape(KV_LORA, MLA_HEADS, QK_NOPE + V_HEAD)
    q_lat = jnp.einsum('bthn,rhn->bthr', q_nope, w_kv[..., :QK_NOPE])
    if c_past is None:
        c_all, kr_all, k_pos = c_new, kr_new, pos
    else:
        c_all = jnp.concatenate([c_past.astype(c_new.dtype), c_new], axis=1)
        kr_all = jnp.concatenate([kr_past.astype(kr_new.dtype), kr_new], axis=1)
        k_pos = jnp.arange(c_all.shape[1], dtype=jnp.int32)
    o_lat = blocked_attention(q_lat, q_rope, c_all, kr_all, pos, k_pos)
    o = jnp.einsum('bthr,rhv->bthv', o_lat, w_kv[..., QK_NOPE:]).reshape(b, t, MLA_HEADS * V_HEAD)
    y_b = o @ p['w_branch_b']
    merged = jax.nn.sigmoid(g_a) * y_a + jax.nn.sigmoid(g_b) * y_b
    out = merged @ p['w_out']
    new_ssm = h_final.reshape(b, SSD_HEADS, SSD_HEAD_DIM, D_STATE).astype(x.dtype)
    return out, c_new, kr_new, new_ssm, new_conv

def moe(x, p):
    n, d = x.shape
    logits = (x @ p['router_w'] + p['router_b']).astype(jnp.float32)
    top_v, top_i = lax.top_k(logits, TOP_K)
    gate = jax.nn.softmax(top_v, axis=-1)
    nk = n * TOP_K
    flat_e = top_i.reshape(-1)
    flat_t = jnp.repeat(jnp.arange(n, dtype=jnp.int32), TOP_K)
    flat_w = gate.reshape(-1)
    order = jnp.argsort(flat_e)
    se = flat_e[order]
    counts = jnp.bincount(flat_e, length=N_EXPERTS)
    padded = (counts + MOE_BLOCK - 1) // MOE_BLOCK * MOE_BLOCK
    start = jnp.cumsum(counts) - counts
    pend = jnp.cumsum(padded)
    pstart = pend - padded
    dest = pstart[se] + jnp.arange(nk, dtype=jnp.int32) - start[se]
    n_blocks = -(-(nk + N_EXPERTS * (MOE_BLOCK - 1)) // MOE_BLOCK)
    cap = n_blocks * MOE_BLOCK
    row_tok = jnp.full((cap,), n, dtype=jnp.int32).at[dest].set(flat_t[order])
    row_w = jnp.zeros((cap,), jnp.float32).at[dest].set(flat_w[order])
    blk_e = jnp.minimum(jnp.searchsorted(pend, jnp.arange(n_blocks, dtype=jnp.int32) * MOE_BLOCK, side='right'),
                        N_EXPERTS - 1)
    xpad = jnp.concatenate([x, jnp.zeros((1, d), x.dtype)], axis=0)
    xr = xpad[row_tok].reshape(n_blocks, MOE_BLOCK, d)
    w_gu, b_gu, w_dn, b_dn = p['exp_w_gu'], p['exp_b_gu'], p['exp_w_down'], p['exp_b_down']

    def expert_block(arg):
        xb, e = arg
        gu = xb @ w_gu[e] + b_gu[e]
        g = jnp.minimum(gu[:, ::2], SWIGLU_LIMIT)
        u = jnp.clip(gu[:, 1::2], -SWIGLU_LIMIT, SWIGLU_LIMIT)
        h = (u + 1.0) * (g * jax.nn.sigmoid(SWIGLU_ALPHA * g))
        return h @ w_dn[e] + b_dn[e]

    out = lax.map(expert_block, (xr, blk_e)).reshape(cap, d)
    y = jnp.zeros_like(xpad).at[row_tok].add(out * row_w[:, None].astype(out.dtype))
    return y[:n]

def setup_inputs(seed: int = 0) -> dict:
    key = jax.random.key(seed)
    ks = iter(jax.random.split(key, 40))

    def nrm(shape, scale):
        return jax.random.normal(next(ks), shape, jnp.float32) * scale

    n_pages = PAST_LEN // PAGE_SIZE
    n_used = DEC_BATCH * n_pages
    n_phys = n_used + n_used // 4
    L = DEPTH
    x_prompt = nrm((BATCH, SEQ, D_MODEL), 1.0)
    x_sample = nrm((DEC_BATCH, DEC_SEQ, D_MODEL), 1.0)
    cache_kv_latent = nrm((L, n_phys, PAGE_SIZE, KV_LORA), 1.0)
    cache_k_rope = nrm((L, n_phys, PAGE_SIZE, ROPE_DIM), 1.0)
    state_ssm = nrm((L, DEC_BATCH, SSD_HEADS, SSD_HEAD_DIM, D_STATE), 0.5)
    state_conv = nrm((L, DEC_BATCH, D_CONV - 1, CONV_DIM), 1.0)
    page_table = jax.random.permutation(next(ks), n_phys)[:n_used].reshape(DEC_BATCH, n_pages).astype(jnp.int32)
    w_in = nrm((L, D_MODEL, D_IN_TOTAL), D_MODEL ** -0.5)
    ssd_conv_w = nrm((L, D_CONV, CONV_DIM), D_CONV ** -0.5)
    ssd_conv_b = nrm((L, CONV_DIM), 0.01)
    dt0 = jnp.exp(jax.random.uniform(next(ks), (L, SSD_HEADS), jnp.float32,
                                     minval=math.log(1e-3), maxval=math.log(1e-1)))
    ssd_dt_bias = dt0 + jnp.log(-jnp.expm1(-dt0))
    ssd_a_log = jnp.log(jax.random.uniform(next(ks), (L, SSD_HEADS), jnp.float32, minval=1.0, maxval=16.0))
    ssd_d = 1.0 + nrm((L, SSD_HEADS), 0.1)
    ssd_norm_g = 1.0 + nrm((L, D_INNER), 0.02)
    mla_q_norm_g = 1.0 + nrm((L, Q_LORA), 0.02)
    w_q_b = nrm((L, Q_LORA, MLA_HEADS * (QK_NOPE + ROPE_DIM)), Q_LORA ** -0.5)
    mla_kv_norm_g = 1.0 + nrm((L, KV_LORA), 0.02)
    w_kv_b = nrm((L, KV_LORA, MLA_HEADS * (QK_NOPE + V_HEAD)), KV_LORA ** -0.5)
    w_branch_a = nrm((L, D_INNER, D_MODEL), D_INNER ** -0.5 * DN_BETA)
    w_branch_b = nrm((L, MLA_HEADS * V_HEAD, D_MODEL), (MLA_HEADS * V_HEAD) ** -0.5 * DN_BETA)
    w_out = nrm((L, D_MODEL, D_MODEL), D_MODEL ** -0.5 * DN_BETA)
    ln1_g = 1.0 + nrm((L, D_MODEL), 0.02)
    ln1_b = nrm((L, D_MODEL), 0.02)
    router_w = nrm((L, D_MODEL, N_EXPERTS), D_MODEL ** -0.5)
    router_b = nrm((L, N_EXPERTS), 0.01)
    exp_w_gu = nrm((L, N_EXPERTS, D_MODEL, 2 * D_FF), D_MODEL ** -0.5)
    exp_b_gu = nrm((L, N_EXPERTS, 2 * D_FF), 0.01)
    exp_w_down = nrm((L, N_EXPERTS, D_FF, D_MODEL), D_FF ** -0.5 * DN_BETA)
    exp_b_down = nrm((L, N_EXPERTS, D_MODEL), 0.01)
    ln2_g = 1.0 + nrm((L, D_MODEL), 0.02)
    ln2_b = nrm((L, D_MODEL), 0.02)
    return {'x_prompt': x_prompt, 'x_sample': x_sample,
            'cache_kv_latent': cache_kv_latent, 'cache_k_rope': cache_k_rope,
            'state_ssm': state_ssm, 'state_conv': state_conv, 'page_table': page_table,
            'w_in': w_in, 'ssd_conv_w': ssd_conv_w, 'ssd_conv_b': ssd_conv_b,
            'ssd_dt_bias': ssd_dt_bias, 'ssd_a_log': ssd_a_log, 'ssd_d': ssd_d, 'ssd_norm_g': ssd_norm_g,
            'mla_q_norm_g': mla_q_norm_g, 'w_q_b': w_q_b, 'mla_kv_norm_g': mla_kv_norm_g, 'w_kv_b': w_kv_b,
            'w_branch_a': w_branch_a, 'w_branch_b': w_branch_b, 'w_out': w_out,
            'ln1_g': ln1_g, 'ln1_b': ln1_b, 'router_w': router_w, 'router_b': router_b,
            'exp_w_gu': exp_w_gu, 'exp_b_gu': exp_b_gu, 'exp_w_down': exp_w_down, 'exp_b_down': exp_b_down,
            'ln2_g': ln2_g, 'ln2_b': ln2_b}

def reference(x_prompt, x_sample, cache_kv_latent, cache_k_rope, state_ssm, state_conv, page_table,
              w_in, ssd_conv_w, ssd_conv_b, ssd_dt_bias, ssd_a_log, ssd_d, ssd_norm_g,
              mla_q_norm_g, w_q_b, mla_kv_norm_g, w_kv_b, w_branch_a, w_branch_b, w_out,
              ln1_g, ln1_b, router_w, router_b, exp_w_gu, exp_b_gu, exp_w_down, exp_b_down,
              ln2_g, ln2_b):
    b_p, t_p, _ = x_prompt.shape
    b_s, t_s, _ = x_sample.shape
    n_pages = page_table.shape[1]
    past_len = n_pages * cache_kv_latent.shape[2]
    hp, hs = x_prompt, x_sample
    c_p_l, kr_p_l, ssm_p_l, conv_p_l = [], [], [], []
    c_s_l, kr_s_l, ssm_s_l, conv_s_l = [], [], [], []
    for l in range(DEPTH):
        p = {'w_in': w_in[l], 'ssd_conv_w': ssd_conv_w[l], 'ssd_conv_b': ssd_conv_b[l],
             'ssd_dt_bias': ssd_dt_bias[l], 'ssd_a_log': ssd_a_log[l], 'ssd_d': ssd_d[l],
             'ssd_norm_g': ssd_norm_g[l], 'mla_q_norm_g': mla_q_norm_g[l], 'w_q_b': w_q_b[l],
             'mla_kv_norm_g': mla_kv_norm_g[l], 'w_kv_b': w_kv_b[l], 'w_branch_a': w_branch_a[l],
             'w_branch_b': w_branch_b[l], 'w_out': w_out[l], 'router_w': router_w[l],
             'router_b': router_b[l], 'exp_w_gu': exp_w_gu[l], 'exp_b_gu': exp_b_gu[l],
             'exp_w_down': exp_w_down[l], 'exp_b_down': exp_b_down[l]}
        conv0 = jnp.zeros((b_p, D_CONV - 1, CONV_DIM), hp.dtype)
        ssm0 = jnp.zeros((b_p, SSD_HEADS, SSD_HEAD_DIM, D_STATE), hp.dtype)
        mp, c_p, kr_p, ssm_p, conv_p = token_mixers(hp, conv0, ssm0, None, None, 0, p)
        c_past = cache_kv_latent[l][page_table].reshape(b_s, past_len, KV_LORA)
        kr_past = cache_k_rope[l][page_table].reshape(b_s, past_len, ROPE_DIM)
        ms, c_s, kr_s, ssm_s, conv_s = token_mixers(hs, state_conv[l], state_ssm[l], c_past, kr_past, past_len, p)
        hp = layer_norm(DN_ALPHA * hp + mp, ln1_g[l], ln1_b[l])
        hs = layer_norm(DN_ALPHA * hs + ms, ln1_g[l], ln1_b[l])
        flat = jnp.concatenate([hp.reshape(-1, D_MODEL), hs.reshape(-1, D_MODEL)], axis=0)
        flat = layer_norm(DN_ALPHA * flat + moe(flat, p), ln2_g[l], ln2_b[l])
        hp = flat[:b_p * t_p].reshape(b_p, t_p, D_MODEL)
        hs = flat[b_p * t_p:].reshape(b_s, t_s, D_MODEL)
        c_p_l.append(c_p); kr_p_l.append(kr_p); ssm_p_l.append(ssm_p); conv_p_l.append(conv_p)
        c_s_l.append(c_s); kr_s_l.append(kr_s); ssm_s_l.append(ssm_s); conv_s_l.append(conv_s)
    kv_latent_prompt = jnp.stack(c_p_l)
    k_rope_prompt = jnp.stack(kr_p_l)
    ssm_prompt = jnp.stack(ssm_p_l)
    conv_prompt = jnp.stack(conv_p_l)
    kv_latent_sample = jnp.stack(c_s_l)
    k_rope_sample = jnp.stack(kr_s_l)
    ssm_sample = jnp.stack(ssm_s_l)
    conv_sample = jnp.stack(conv_s_l)
    return (hp, hs, kv_latent_prompt, k_rope_prompt, ssm_prompt, conv_prompt,
            kv_latent_sample, k_rope_sample, ssm_sample, conv_sample)


_drawn_inputs = setup_inputs


def setup_inputs(seed=0):
    import zlib

    import numpy as np

    out = dict(_drawn_inputs(seed))
    spreads = {}
    factors = {'cache_kv_latent': 4.385,
     'cache_k_rope': 3.561,
     'ssd_conv_b': 2.864,
     'ssd_d': 3.041,
     'ssd_norm_g': 5.952,
     'mla_q_norm_g': 8.0,
     'mla_kv_norm_g': 2.735,
     'router_b': 3.029,
     'exp_b_gu': 8.0,
     'exp_b_down': 8.0,
     'ln2_g': 2.931,
     'ln2_b': 2.769}
    for name, (base, spread) in spreads.items():
        noise = np.random.default_rng([zlib.crc32(name.encode()), seed]).standard_normal(out[name].shape)
        drawn = base * np.exp(spread * noise) if base else spread * noise
        out[name] = __import__('jax').numpy.asarray(drawn.astype(out[name].dtype))
    for name, factor in factors.items():
        out[name] = (out[name] * factor).astype(out[name].dtype)
    return out
```

```python
from contextlib import ExitStack, contextmanager

import numpy as np

import concourse.bass as bass
from concourse import mybir

F32 = mybir.dt.float32
I32 = mybir.dt.int32
U32 = mybir.dt.uint32
ALU = mybir.AluOpType
ACT = mybir.ActivationFunctionType
AX = mybir.AxisListType.X

P = 128
D = 1024
SEQ = 512
NSEQ, TS = 8, 8
NS = NSEQ * TS
T = SEQ + NS
NT = 5
ROWS = [P, P, P, P, NS]
KD = D // P
PAST, PAGE = 4096, 128
NPAGE = PAST // PAGE
NPHYS = 320
HEADS, NOPE, ROPE, VH = 8, 128, 64, 128
QL = KVL = 256
QH = NOPE + ROPE
DI = 2048
G, HG, PD, NST = 4, 8, 64, 128
SH = G * HG
GW = HG * PD
CONV = DI + 2 * G * NST
KC = 4
NCT = CONV // P
FF = 1024
E = 32
TOPK = 4
CAP = 640
ITEMS = E + (T * TOPK - 1) // P
NOVF = ITEMS - E
ATT_SCALE = (NOPE + ROPE) ** -0.5
ALPHA = 2 ** 0.25
LN_EPS, RMS_EPS = 1e-5, 1e-6
SW_ALPHA, SW_LIMIT = 1.702, 7.0
MASKED = -1e30
H2 = T // 2

C_Q, C_KV, C_KR, C_Z = 0, QL, QL + KVL, QL + KVL + ROPE
C_X = C_Z + DI
C_DT = C_X + CONV
C_GA = C_DT + SH
C_GB = C_GA + D
C_ALL = C_GB + D

K_ID = 0
K_TRI = K_ID + P
K_STRICT = K_TRI + P
K_ONE = K_STRICT + P
K_CAUS = K_ONE + P
K_BTRI = K_CAUS + P
K_BALL = K_BTRI + NS
K_BEND = K_BALL + NS
K_BROW = K_BEND + NSEQ
K_BCOL = K_BROW + NSEQ
K_NEW = K_BCOL + NSEQ * NS
K_PAIR = K_NEW + TS
K_BASE = K_PAIR + 2 * (NT * TOPK + 1)
K_CODE = K_BASE + E
K_ITEM = K_CODE + 4 * E
K_EXP = K_ITEM + NOVF + 1
K_W = K_EXP + 4 * E


def constants():
    c = np.zeros((P, K_W), np.float32)
    r = np.arange(P)[:, None]
    q = np.arange(P)[None, :]
    c[:, K_ID:K_ID + P] = r == q
    c[:, K_TRI:K_TRI + P] = r <= q
    c[:, K_STRICT:K_STRICT + P] = r < q
    c[:, K_ONE:K_ONE + P] = 1
    c[:, K_CAUS:K_CAUS + P] = np.where(q <= r, 0, MASKED)
    l = np.arange(NS)
    same = l[:, None] // TS == l[None, :] // TS
    c[:NS, K_BTRI:K_BTRI + NS] = same & (l[:, None] <= l[None, :])
    c[:NS, K_BALL:K_BALL + NS] = same
    s = np.arange(NSEQ)
    c[:NS, K_BEND:K_BEND + NSEQ] = l[:, None] == s[None, :] * TS + TS - 1
    c[:NS, K_BROW:K_BROW + NSEQ] = l[:, None] // TS == s[None, :]
    c[:, K_BCOL:K_BCOL + NSEQ * NS] = (s[:, None] == l[None, :] // TS).reshape(1, -1)
    t = np.arange(TS)
    c[:HEADS * TS, K_NEW:K_NEW + TS] = np.where(t[None, :] <= np.tile(t, HEADS)[:, None], 0, MASKED)
    pair = np.zeros((P, NT * TOPK + 1, 2))
    token = np.repeat(r + P * np.arange(NT)[None, :], TOPK, axis=1)
    pair[:, :-1, 0] = token
    pair[:, :-1, 1] = token * TOPK + np.tile(np.arange(TOPK), NT)[None, :]
    pair[:, -1, 1] = T * TOPK
    c[:, K_PAIR:K_BASE] = pair.reshape(P, -1)
    c[:, K_BASE:K_BASE + E] = CAP * np.arange(E)
    c[0, K_CODE:K_CODE + 4 * E] = (CAP * np.arange(E)[None, :] + P * np.arange(1, 5)[:, None]).reshape(-1)
    c[0, K_ITEM:K_ITEM + NOVF + 1] = np.arange(1, NOVF + 2)
    c[0, K_EXP:K_EXP + 4 * E] = np.tile(np.arange(E), 4)
    return c


def rope_tables():
    half = ROPE // 2
    inv = np.float32(10000.0) ** (-np.arange(half, dtype=np.float32) / np.float32(half))
    pos = np.concatenate([np.arange(SEQ), np.tile(PAST + np.arange(TS), NSEQ)]).astype(np.float32)
    ang = np.zeros((NT * P, half), np.float32)
    ang[:T] = pos[:, None] * inv[None, :]
    both = np.stack([np.cos(ang), np.sin(ang)]).astype(np.float32)
    return np.ascontiguousarray(both.reshape(2, NT, P, half).transpose(2, 0, 1, 3))


@contextmanager
def signals(nc, stage):
    made = []

    def make(name):
        made.append(nc.alloc_semaphore(f"{stage}_{name}"))
        return made[-1]

    yield make
    nc.clear_and_free_semaphores(made)
    nc.all_engine_barrier()


def token_dram(prompt, sample, i):
    return prompt[P * i:P * (i + 1), :] if i < NT - 1 else sample


def stage_latents(nc, io, sb):
    with ExitStack() as ctx:
        sem = ctx.enter_context(signals(nc, "latents"))
        buf = lambda n, s: ctx.enter_context(nc.sbuf_tensor(n, s, F32))
        x_tok = buf("x_tok", [P, NT, D])
        w_lat = buf("w_lat", [P, KD, C_Z])
        w_dt = buf("w_dt", [P, KD, SH])
        lat = buf("lat", [P, NT, C_Z])
        qn = buf("qn", [P, NT, QL])
        gq = buf("gq", [P, QL])
        gkv = buf("gkv", [P, KVL])
        junk = buf("junk", [P, QL])
        ssq = buf("ssq", [P, 2, NT])
        rt = [buf(f"rt{i}", [P, NT, ROPE // 2]) for i in range(4)]
        banks = ctx.enter_context(nc.psum_tensor("banks", [P, 8, 512], F32))
        const_in, w_in_, g_in = sem("const_in"), sem("w_in_"), sem("g_in")
        x_in = [sem(f"x_in{i}") for i in range(NT)]
        turned, turned_out = sem("turned"), sem("turned_out")
        lat_ready, lat_out = sem("lat_ready"), sem("lat_out")
        zeroed, squared, rooted, vec = sem("zeroed"), sem("squared"), sem("rooted"), sem("vec")
        lat_done, lat_turned, stored = sem("lat_done"), sem("lat_turned"), sem("stored")
        K = sb.const
        w_view = io.w_in.rearrange("(k p) n -> p k n", p=P)

        with nc.Block() as block:
            @block.sync
            def _(sp):
                sp.dma_start(K[:], io.consts).then_inc(const_in, 16)
                for i in range(NT):
                    sp.dma_start(x_tok[0:ROWS[i], i, :], token_dram(io.xp, io.xs, i)).then_inc(x_in[i], 16)
                sp.dma_start(w_lat[:], w_view[:, :, 0:C_Z]).then_inc(w_in_, 16)
                sp.dma_start(w_dt[:], w_view[:, :, C_DT:C_GA]).then_inc(w_in_, 16)
                sp.dma_start(sb.rope[:], io.rope).then_inc(g_in, 16)
                sp.dma_start(gq[:], io.gq.broadcast_to((P, QL))).then_inc(g_in, 16)
                sp.dma_start(gkv[:], io.gkv.broadcast_to((P, KVL))).then_inc(g_in, 16)
                sp.wait_ge(lat_done, 2)
                for i in range(NT):
                    sp.dma_start(token_dram(io.o_cp, io.o_cs, i), sb.c_tok[0:ROWS[i], i, :]).then_inc(stored, 16)
                    sp.dma_start(token_dram(io.o_krp, io.o_krs, i), sb.kr_tok[0:ROWS[i], i, :]).then_inc(stored, 16)
                sp.wait_ge(stored, 16 * 2 * NT)

            @block.gpsimd
            def _(pool):
                pool.memset(lat[NS:P, NT - 1, :], 0.0).then_inc(zeroed, 1)
                pool.memset(sb.dt[NS:P, NT - 1, :], 0.0).then_inc(zeroed, 1)

            @block.tensor
            def _(pe):
                pe.wait_ge(const_in, 16)
                for i in range(NT):
                    n = ROWS[i]
                    pe.wait_ge(x_in[i], 16)
                    for h in range(2):
                        u = 2 * i + h
                        if u >= 4:
                            pe.wait_ge(turned_out, u - 3)
                        for k in range(4):
                            mm = pe.transpose(banks[:, u % 4, k * n:(k + 1) * n],
                                              x_tok[0:n, i, (4 * h + k) * P:(4 * h + k + 1) * P], K[0:n, K_ID:K_ID + n])
                        mm.then_inc(turned, 1)
                pe.wait_ge(w_in_, 32)
                pe.wait_ge(turned_out, 2 * NT)
                for i in range(NT):
                    n, b = ROWS[i], 4 + 2 * (i % 2)
                    if i >= 2:
                        pe.wait_ge(lat_out, i - 1)
                    xs = [sb.xT[:, k, P * i:P * i + n] for k in range(KD)]
                    for k in range(KD):
                        pe.matmul(banks[0:n, b, :], xs[k], w_lat[:, k, 0:512], start=(k == 0), stop=(k == KD - 1))
                    for k in range(KD):
                        pe.matmul(banks[0:n, b + 1, 0:ROPE], xs[k], w_lat[:, k, 512:C_Z], start=(k == 0), stop=(k == KD - 1))
                    for k in range(KD):
                        mm = pe.matmul(banks[0:n, b + 1, ROPE:ROPE + SH], xs[k], w_dt[:, k, :], start=(k == 0), stop=(k == KD - 1))
                    mm.then_inc(lat_ready, 1)
                pe.wait_ge(lat_done, 3)
                for i in range(NT):
                    n = ROWS[i]
                    if i >= 4:
                        pe.wait_ge(lat_turned, i - 3)
                    for c in range(2):
                        pe.transpose(banks[:, i % 4, c * n:(c + 1) * n], qn[0:n, i, c * P:(c + 1) * P], K[0:n, K_ID:K_ID + n])
                    for c in range(2):
                        pe.transpose(banks[:, 4 + i % 4, c * n:(c + 1) * n], sb.c_tok[0:n, i, c * P:(c + 1) * P], K[0:n, K_ID:K_ID + n])
                    pe.transpose(banks[0:ROPE, 4 + i % 4, 2 * n:3 * n], sb.kr_tok[0:n, i, :], K[0:n, K_ID:K_ID + n]).then_inc(turned, 1)

            @block.scalar
            def _(act):
                for i in range(NT):
                    n, b = ROWS[i], 4 + 2 * (i % 2)
                    act.wait_ge(lat_ready, i + 1)
                    act.activation(lat[0:n, i, 0:512], banks[0:n, b, :], ACT.Copy)
                    act.activation(lat[0:n, i, 512:C_Z], banks[0:n, b + 1, 0:ROPE], ACT.Copy)
                    act.activation(sb.dt[0:n, i, :], banks[0:n, b + 1, ROPE:ROPE + SH], ACT.Copy).then_inc(lat_out, 1)
                act.wait_ge(zeroed, 2)
                act.wait_ge(lat_out, NT)
                for j in range(2):
                    for i in range(NT):
                        if j or i:
                            act.wait_ge(squared, j * NT + i)
                        act.activation(junk[:], lat[:, i, j * QL:(j + 1) * QL], ACT.Square,
                                       accum_out=ssq[:, j, i:i + 1]).then_inc(squared, 1)
                act.wait_ge(vec, 1)
                act.activation(ssq[:], ssq[:], ACT.Sqrt).then_inc(rooted, 1)

            @block.vector
            def _(dve):
                for u in range(2 * NT):
                    i, h = divmod(u, 2)
                    n = ROWS[i]
                    dve.wait_ge(turned, u + 1)
                    dve.tensor_copy(sb.xT[:, 4 * h:4 * h + 4, P * i:P * i + n],
                                    banks[:, u % 4, 0:4 * n].rearrange("p (k n) -> p k n", k=4)).then_inc(turned_out, 1)
                dve.wait_ge(squared, 2 * NT)
                dve.tensor_scalar(ssq[:], ssq[:], 1.0 / QL, RMS_EPS, ALU.mult, ALU.add).then_inc(vec, 1)
                dve.wait_ge(g_in, 48)
                c, s = sb.rope[:, 0], sb.rope[:, 1]
                half = ROPE // 2
                k1, k2 = lat[:, :, 512:512 + half], lat[:, :, 512 + half:C_Z]
                for o, a, b in ((0, k1, c), (1, k2, s), (2, k2, c), (3, k1, s)):
                    ins = dve.tensor_tensor(rt[o][:], a, b, ALU.mult)
                ins.then_inc(vec, 1)
                dve.wait_ge(vec, 2)
                dve.tensor_tensor(sb.kr_tok[:, :, 0:half], rt[0][:], rt[1][:], ALU.subtract)
                dve.tensor_tensor(sb.kr_tok[:, :, half:ROPE], rt[2][:], rt[3][:], ALU.add).then_inc(lat_done, 1)
                dve.wait_ge(rooted, 1)
                dve.reciprocal(ssq[:], ssq[:]).then_inc(vec, 1)
                dve.wait_ge(vec, 3)
                for i in range(NT):
                    ins = dve.scalar_tensor_tensor(out=sb.c_tok[:, i, :], in0=lat[:, i, QL:QL + KVL], scalar=ssq[:, 1, i:i + 1],
                                                   in1=gkv[:], op0=ALU.mult, op1=ALU.mult)
                ins.then_inc(lat_done, 1)
                for i in range(NT):
                    ins = dve.scalar_tensor_tensor(out=qn[:, i, :], in0=lat[:, i, 0:QL], scalar=ssq[:, 0, i:i + 1],
                                                   in1=gq[:], op0=ALU.mult, op1=ALU.mult)
                ins.then_inc(lat_done, 1)
                for i in range(NT):
                    n = ROWS[i]
                    dve.wait_ge(turned, 2 * NT + i + 1)
                    dve.tensor_copy(sb.qnT[:, :, P * i:P * i + n], banks[:, i % 4, 0:2 * n].rearrange("p (c n) -> p c n", c=2))
                    dve.tensor_copy(sb.cT[:, :, P * i:P * i + n], banks[:, 4 + i % 4, 0:2 * n].rearrange("p (c n) -> p c n", c=2))
                    dve.tensor_copy(sb.krT[:, P * i:P * i + n], banks[0:ROPE, 4 + i % 4, 2 * n:3 * n]).then_inc(lat_turned, 1)


def stage_prompt_attention(nc, io, sb):
    with ExitStack() as ctx:
        sem = ctx.enter_context(signals(nc, "prompt_attention"))
        buf = lambda n, s: ctx.enter_context(nc.sbuf_tensor(n, s, F32))
        wq = buf("wq", [P, 2, HEADS * QH])
        wkT = buf("wkT", [P, HEADS, KVL])
        q_rot = buf("q_rot", [P, NT, HEADS, ROPE])
        rt = [buf(f"qrt{i}", [P, HEADS, ROPE // 2]) for i in range(4)]
        qn_h = buf("qn_h", [P, T])
        ql_h = buf("ql_h", [P, 2, 2, SEQ])
        qr_h = buf("qr_h", [ROPE, 2, SEQ])
        prob = buf("prob", [P, 2, SEQ])
        probT = buf("probT", [P, 2, 4, P])
        olT = buf("olT", [P, 2, 2, P])
        mx = buf("mx", [P, 2])
        neg = buf("neg", [P, 2])
        den = buf("den", [P, 2])
        banks = ctx.enter_context(nc.psum_tensor("banks2", [P, 8, 512], F32))
        K = sb.const
        wq_in, wkv_in = sem("wq_in"), sem("wkv_in")
        wk_ready, wk_out, rot_ready, rot_out, rot_vec = sem("wk_ready"), sem("wk_out"), sem("rot_ready"), sem("rot_out"), sem("rot_vec")
        prep_ready, prep_out = sem("prep_ready"), sem("prep_out")
        scored, maxed, vec, expd, normed = sem("scored"), sem("maxed"), sem("vec2"), sem("expd"), sem("normed")
        pt_ready, pt_out, pv_ready, pv_out, o_ready, o_out = (sem(n) for n in ("pt_ready", "pt_out", "pv_ready", "pv_out", "o_ready", "o_out"))
        wq_rot = wq[:].rearrange("p k (h d) -> p k h d", h=HEADS)[:, :, :, NOPE:QH]
        n_steps = HEADS * 4
        step = lambda i: divmod(i, 4)

        with nc.Block() as block:
            @block.sync
            def _(sp):
                sp.dma_start(wq[:], io.wq.rearrange("(k p) n -> p k n", p=P)).then_inc(wq_in, 16)
                sp.dma_start(sb.wkv[:], io.wkv.rearrange("(k p) n -> p k n", p=P)).then_inc(wkv_in, 16)

            @block.tensor
            def _(pe):
                pe.wait_ge(wq_in, 16)
                for i in range(NT):
                    n = ROWS[i]
                    if i >= 2:
                        pe.wait_ge(rot_out, i - 1)
                    for k in range(2):
                        mm = pe.matmul(banks[0:n, i % 2, :], sb.qnT[:, k, P * i:P * i + n], wq_rot[:, k], start=(k == 0), stop=(k == 1))
                    mm.then_inc(rot_ready, 1)
                pe.wait_ge(wkv_in, 16)
                for u in range(4):
                    for v in range(4):
                        h, r = 2 * u + v // 2, v % 2
                        mm = pe.transpose(banks[:, 2 + u, v * P:(v + 1) * P], sb.wkv[:, r, h * 256:h * 256 + NOPE], K[:, K_ID:K_ID + P])
                    mm.then_inc(wk_ready, 1)

                def prep(h, part):
                    m = 4 * h + part
                    if m >= 1:
                        pe.wait_ge(prep_out, m)
                    if part == 0:
                        for piece, b in ((0, 0), (1, 1)):
                            for k in range(2):
                                mm = pe.matmul(banks[:, b, 0:H2], wq[:, k, h * QH:h * QH + NOPE],
                                               sb.qnT[:, k, piece * H2:(piece + 1) * H2], start=(k == 0), stop=(k == 1))
                    elif part < 3:
                        r = part - 1
                        for piece in range(2):
                            mm = pe.matmul(banks[:, piece, 0:H2], wkT[:, h, r * P:(r + 1) * P],
                                           qn_h[:, piece * H2:(piece + 1) * H2], start=True, stop=True)
                    else:
                        for i in range(NT):
                            n = ROWS[i]
                            o = banks[0:ROPE, 0, P * i:P * i + n] if i < 4 else banks[0:ROPE, 1, 0:n]
                            mm = pe.transpose(o, q_rot[0:n, i, h, :], K[0:n, K_ID:K_ID + n])
                    mm.then_inc(prep_ready, 1)

                pe.wait_ge(rot_out, NT)
                pe.wait_ge(wk_out, 4)
                for part in range(4):
                    prep(0, part)
                for i in range(n_steps + 3):
                    if i < n_steps:
                        h, q = step(i)
                        pe.wait_ge(prep_out, 4 * h + 4)
                        if i >= 2:
                            pe.wait_ge(expd, i - 1)
                        n = (q + 1) * P
                        o = banks[:, 2 + i % 2, 0:n]
                        for r in range(2):
                            pe.matmul(o, ql_h[:, h % 2, r, q * P:(q + 1) * P], sb.cT[:, r, 0:n], start=(r == 0), stop=False)
                        pe.matmul(o, qr_h[:, h % 2, q * P:(q + 1) * P], sb.krT[:, 0:n], start=False, stop=True).then_inc(scored, 1)
                    if 1 <= i <= n_steps:
                        j = i - 1
                        pe.wait_ge(normed, j + 1)
                        if j >= 2:
                            pe.wait_ge(pt_out, j - 1)
                        for k in range(step(j)[1] + 1):
                            mm = pe.transpose(banks[:, 4 + 3 * (j % 2), k * P:(k + 1) * P], prob[:, j % 2, k * P:(k + 1) * P], K[:, K_ID:K_ID + P])
                        mm.then_inc(pt_ready, 1)
                    if 2 <= i <= n_steps + 1:
                        j = i - 2
                        pe.wait_ge(pt_out, j + 1)
                        if j >= 1:
                            pe.wait_ge(pv_out, j)
                        q = step(j)[1]
                        for r in range(2):
                            for k in range(q + 1):
                                mm = pe.matmul(banks[:, 5, r * P:(r + 1) * P], sb.c_tok[:, k, r * P:(r + 1) * P], probT[:, j % 2, k, :],
                                               start=(k == 0), stop=(k == q))
                        mm.then_inc(pv_ready, 1)
                    if 3 <= i:
                        j = i - 3
                        h = step(j)[0]
                        pe.wait_ge(pv_out, j + 1)
                        if j >= 1:
                            pe.wait_ge(o_out, j)
                        for r in range(2):
                            mm = pe.matmul(banks[:, 6, 0:P], sb.wkv[:, r, h * 256 + NOPE:(h + 1) * 256], olT[:, j % 2, r, :],
                                           start=(r == 0), stop=(r == 1))
                        mm.then_inc(o_ready, 1)
                    if i < n_steps and step(i)[0] + 1 < HEADS:
                        prep(step(i)[0] + 1, step(i)[1])

            @block.scalar
            def _(act):
                def prep_copy(h, part):
                    m = 4 * h + part
                    act.wait_ge(prep_ready, m + 1)
                    S1 = SEQ - H2
                    if part == 0:
                        act.activation(qn_h[:, 0:H2], banks[:, 0, 0:H2], ACT.Copy)
                        ins = act.activation(qn_h[:, H2:T], banks[:, 1, 0:H2], ACT.Copy)
                    elif part < 3:
                        r = part - 1
                        if h >= 2:
                            act.wait_ge(scored, 4 * h - 4)
                        act.activation(ql_h[:, h % 2, r, 0:H2], banks[:, 0, 0:H2], ACT.Copy)
                        act.activation(ql_h[:, h % 2, r, H2:SEQ], banks[:, 1, 0:S1], ACT.Copy)
                        ins = act.activation(sb.qlS[:, r, h, :], banks[:, 1, S1:H2], ACT.Copy)
                    else:
                        act.activation(qr_h[:, h % 2, :], banks[0:ROPE, 0, :], ACT.Copy)
                        ins = act.activation(sb.qrS[:, h, :], banks[0:ROPE, 1, 0:NS], ACT.Copy)
                    ins.then_inc(prep_out, 1)

                for part in range(4):
                    prep_copy(0, part)
                for i in range(n_steps + 1):
                    if i >= 1:
                        j = i - 1
                        n = step(j)[1] + 1
                        act.wait_ge(pt_ready, j + 1)
                        if j >= 2:
                            act.wait_ge(pv_ready, j - 1)
                        act.activation(probT[:, j % 2, 0:n, :], banks[:, 4 + 3 * (j % 2), 0:n * P].rearrange("p (k n) -> p k n", n=P),
                                       ACT.Copy).then_inc(pt_out, 1)
                    if i < n_steps:
                        h, q = step(i)
                        n = (q + 1) * P
                        act.wait_ge(maxed, i + 1)
                        if i >= 2:
                            act.wait_ge(pt_ready, i - 1)
                        act.activation(prob[:, i % 2, 0:n], banks[:, 2 + i % 2, 0:n], ACT.Exp, bias=neg[:, i % 2:i % 2 + 1],
                                       scale=ATT_SCALE, accum_out=den[:, i % 2:i % 2 + 1]).then_inc(expd, 1)
                        if h + 1 < HEADS:
                            prep_copy(h + 1, q)

            @block.vector
            def _(dve):
                half = ROPE // 2
                for i in range(NT):
                    n = ROWS[i]
                    dve.wait_ge(rot_ready, i + 1)
                    x = banks[0:n, i % 2, :].rearrange("p (h d) -> p h d", h=HEADS)
                    c = sb.rope[0:n, 0, i, :].unsqueeze(1).broadcast_to((n, HEADS, half))
                    s = sb.rope[0:n, 1, i, :].unsqueeze(1).broadcast_to((n, HEADS, half))
                    x1, x2 = x[:, :, 0:half], x[:, :, half:ROPE]
                    if i >= 1:
                        dve.wait_ge(rot_out, i)
                    for o, a, b in ((0, x1, c), (1, x2, s), (2, x2, c), (3, x1, s)):
                        ins = dve.tensor_tensor(rt[o][0:n], a, b, ALU.mult)
                    ins.then_inc(rot_vec, 1)
                    dve.wait_ge(rot_vec, i + 1)
                    dve.tensor_tensor(q_rot[0:n, i, :, 0:half], rt[0][0:n], rt[1][0:n], ALU.subtract)
                    dve.tensor_tensor(q_rot[0:n, i, :, half:ROPE], rt[2][0:n], rt[3][0:n], ALU.add).then_inc(rot_out, 1)
                for u in range(4):
                    dve.wait_ge(wk_ready, u + 1)
                    dve.tensor_copy(wkT[:, 2 * u:2 * u + 2, :], banks[:, 2 + u, :].rearrange("p (h r) -> p h r", h=2)).then_inc(wk_out, 1)
                for i in range(n_steps + 3):
                    if 1 <= i <= n_steps:
                        j = i - 1
                        n = (step(j)[1] + 1) * P
                        dve.wait_ge(expd, j + 1)
                        dve.reciprocal(den[:, j % 2:j % 2 + 1], den[:, j % 2:j % 2 + 1]).then_inc(vec, 1)
                        dve.wait_ge(vec, 3 * j + 3)
                        dve.tensor_scalar(prob[:, j % 2, 0:n], prob[:, j % 2, 0:n], den[:, j % 2:j % 2 + 1], None, ALU.mult).then_inc(normed, 1)
                    if i < n_steps:
                        q = step(i)[1]
                        dve.wait_ge(scored, i + 1)
                        diag = banks[:, 2 + i % 2, q * P:(q + 1) * P]
                        dve.tensor_tensor(diag, diag, K[:, K_CAUS:K_CAUS + P], ALU.add).then_inc(vec, 1)
                        dve.wait_ge(vec, 3 * i + 1)
                        dve.reduce_max(mx[:, i % 2:i % 2 + 1], banks[:, 2 + i % 2, 0:(q + 1) * P], AX).then_inc(vec, 1)
                        dve.wait_ge(vec, 3 * i + 2)
                        dve.tensor_scalar(neg[:, i % 2:i % 2 + 1], mx[:, i % 2:i % 2 + 1], -ATT_SCALE, None, ALU.mult).then_inc(maxed, 1)
                    if 2 <= i <= n_steps + 1:
                        j = i - 2
                        dve.wait_ge(pv_ready, j + 1)
                        if j >= 2:
                            dve.wait_ge(o_ready, j - 1)
                        dve.tensor_copy(olT[:, j % 2, :, :], banks[:, 5, 0:2 * P].rearrange("p (r n) -> p r n", r=2)).then_inc(pv_out, 1)
                    if 3 <= i:
                        j = i - 3
                        h, q = step(j)
                        dve.wait_ge(o_ready, j + 1)
                        dve.tensor_copy(sb.oT[:, h, q * P:(q + 1) * P], banks[:, 6, 0:P]).then_inc(o_out, 1)


def stage_sample_attention(nc, io, sb):
    NQ = HEADS * TS
    NKEY = PAST + TS
    NCH = 8
    with ExitStack() as ctx:
        sem = ctx.enter_context(signals(nc, "sample_attention"))
        buf = lambda n, s: ctx.enter_context(nc.sbuf_tensor(n, s, F32))
        page = ctx.enter_context(nc.sbuf_tensor("page", [1, NSEQ * NPAGE], I32))
        rows = buf("rows", [P, 2, NPAGE, KVL])
        rots = buf("rots", [P, 2, NPAGE, ROPE])
        spare = sb.mergedT[:].rearrange("p k t -> p (k t)")
        spare2 = sb.xT[:].rearrange("p k t -> p (k t)")
        keyT = spare[:, 0:3072].rearrange("p (a j n) -> p a j n", a=2, j=3)
        q_b = spare[:, 3072:3328].rearrange("p (a r n) -> p a r n", a=2, r=2)
        qr_b = spare[0:ROPE, 3328:3456].rearrange("p (a n) -> p a n", a=2)
        new_b = spare[0:TS, 3456:3968].rearrange("p (a r) -> p a r", a=2)
        score = buf("score", [NQ, 2, NKEY])
        mx = buf("mx3", [NQ, 2, NCH + 1])
        stat = buf("stat", [NQ, 2, 3])
        cT_b = spare[:, 3968:4000].rearrange("p (a r t) -> p a r t", a=2, r=2)
        krT_b = spare[0:ROPE, 4000:4016].rearrange("p (a t) -> p a t", a=2)
        probT = spare2[:, 0:NPAGE * NQ].rearrange("p (k n) -> p k n", k=NPAGE)
        probT_new = buf("probT_new", [TS, NQ])
        olS = spare2[:, NPAGE * NQ:NPAGE * NQ + 2 * HEADS * NS].rearrange("p (r h n) -> p r h n", r=2, h=HEADS)
        banks = ctx.enter_context(nc.psum_tensor("banks3", [P, 8, 512], F32))
        K = sb.const
        carried = sem("carried")
        page_in, new_in = sem("page_in"), [sem("new_in0"), sem("new_in1")]
        chunk_in = [[sem(f"chunk_in{p}{c}") for c in range(NCH)] for p in range(2)]
        rows_free, q_ready, q_free = sem("rows_free"), sem("q_ready"), sem("q_free")
        bank_full = [sem(f"bank_full{i}") for i in range(4)]
        bank_free = [sem(f"bank_free{i}") for i in range(4)]
        keys_v, keys_a, scored = sem("keys_v"), sem("keys_a"), sem("scored3")
        read_v, read_a, masked, maxed, negd, expd, vec = (sem(n) for n in ("read_v", "read_a", "masked", "maxed3", "negd", "expd3", "vec3"))
        scaled, new_scored, newT, newT_out, probs_out, pv_ready, pv_out = (sem(n) for n in (
            "scaled", "new_scored", "newT", "newT_out", "probs_out", "pv_ready3", "pv_out3"))
        o_ready, o_out = sem("o_ready3"), sem("o_out3")
        def key_use(b, u):
            return u // 4 if isinstance(b, int) and b == 0 else b * 7 + (u // 4 - 1)

        def prob_use(b):
            return b * 7 + 12 if not (isinstance(b, int) and b == NSEQ - 1) else b * 7 + 6

        with nc.Block() as block:
            def over(eng, head, body, tail):
                head()
                with eng.Fori(0, NSEQ // 2 - 1) as i:
                    body(i * 2 + 1, 1)
                    body(i * 2 + 2, 0)
                tail(NSEQ - 1, 1)

            @block.sync
            def _(sp):
                sp.dma_start(page[:], io.pages.rearrange("(a b) n -> a (b n)", a=1)).then_inc(page_in, 16)
                sp.wait_ge(page_in, 16)

                def load(b, par):
                    sp.wait_ge(rows_free, b + 1)
                    for j in range(NPAGE):
                        n = sp.value_load(page[0:1, bass.ds(b * NPAGE + j, 1)], min_val=0, max_val=NPHYS - 1)
                        s = chunk_in[par][j // 4]
                        sp.dma_start(rows[:, par, j, :], io.cache_c[bass.ds(n, 1)].rearrange("a p r -> (a p) r")).then_inc(s, 16)
                        sp.dma_start(rots[:, par, j, :], io.cache_r[bass.ds(n, 1)].rearrange("a p r -> (a p) r")).then_inc(s, 16)

                with sp.Fori(0, NSEQ // 2) as i:
                    load(i * 2, 0)
                    load(i * 2 + 1, 1)

            @block.gpsimd
            def _(pool):
                def stage(b, par):
                    pool.wait_ge(q_free, b + 1)
                    pool.dma_start(new_b[:, par, :], io.o_cs[bass.ds(b * TS, TS), :]).then_inc(new_in[par], 16)
                    at, fresh = bass.ds(b * TS, TS), bass.ds(b * TS + SEQ, TS)
                    pool.tensor_copy(cT_b[:, par], sb.cT[:, :, fresh])
                    pool.tensor_copy(krT_b[:, par, :], sb.krT[:, fresh])
                    for r in range(2):
                        pool.tensor_copy(q_b[:, par, r, :].rearrange("p (h t) -> p h t", h=HEADS), sb.qlS[:, r, :, at])
                    pool.tensor_copy(qr_b[:, par, :].rearrange("p (h t) -> p h t", h=HEADS), sb.qrS[:, :, at]).then_inc(q_ready, 1)

                with pool.Fori(0, NSEQ // 2) as i:
                    stage(i * 2, 0)
                    stage(i * 2 + 1, 1)

            @block.tensor
            def _(pe):
                pe.sem_inc(rows_free, 2)
                pe.sem_inc(q_free, 2)

                def settle():
                    pe.sem_inc(carried, 1)

                def turn_keys(b, par, c):
                    for j in range(3):
                        u = 3 * c + j
                        if j == 0:
                            pe.wait_ge(chunk_in[par][c], (b - par) * 64 + 128)
                        pe.wait_ge(bank_free[u % 4], key_use(b, u) + 1)
                        if j == 2:
                            settle()
                        for k in range(4):
                            src = rows[:, par, 4 * c + k, j * P:(j + 1) * P] if j < 2 else rots[:, par, 4 * c + k, :]
                            mm = pe.transpose(banks[0:P if j < 2 else ROPE, u % 4, k * P:(k + 1) * P], src, K[:, K_ID:K_ID + P])
                        mm.then_inc(bank_full[u % 4], 1)

                def score_chunk(b, par, c):
                    pe.wait_ge(keys_v, b * NCH + c + 1)
                    pe.wait_ge(keys_a, b * NCH + c + 1)
                    pe.wait_ge(read_a, b * NCH + c + 1)
                    o = banks[0:NQ, 4 + c % 2, :]
                    for r in range(2):
                        pe.matmul(o, q_b[:, par, r, :], keyT[:, c % 2, r, :], start=(r == 0), stop=False)
                    pe.matmul(o, qr_b[:, par, :], keyT[0:ROPE, c % 2, 2, :], start=False, stop=True).then_inc(scored, 1)

                def scores(b, par):
                    pe.wait_ge(q_ready, b + 1)
                    turn_keys(b, par, 0)
                    for c in range(NCH):
                        if c + 1 < NCH:
                            turn_keys(b, par, c + 1)
                        score_chunk(b, par, c)
                    pe.wait_ge(masked, b + 1)
                    o = banks[0:NQ, 7, 0:TS]
                    for r in range(2):
                        pe.matmul(o, q_b[:, par, r, :], cT_b[:, par, r, :], start=(r == 0), stop=False)
                    pe.matmul(o, qr_b[:, par, :], krT_b[:, par, :], start=False, stop=True).then_inc(new_scored, 1)

                def values(b, par):
                    pe.wait_ge(scaled, b + 1)
                    for m in range(4):
                        u = 3 * NCH + m
                        pe.wait_ge(bank_free[u % 4], prob_use(b) + 1)
                        settle()
                        for k in range(8):
                            mm = pe.transpose(banks[:, u % 4, k * NQ:(k + 1) * NQ], score[:, par, (8 * m + k) * P:(8 * m + k + 1) * P], K[0:NQ, K_ID:K_ID + NQ])
                        mm.then_inc(bank_full[u % 4], 1)
                    pe.wait_ge(newT_out, b + 1)
                    pe.wait_ge(masked, b + (2 if isinstance(b, int) and b == NSEQ - 1 else 3))
                    settle()
                    pe.transpose(banks[0:TS, 7, 128:128 + NQ], score[:, par, PAST:NKEY], K[0:NQ, K_ID:K_ID + NQ]).then_inc(newT, 1)
                    pe.wait_ge(probs_out, b * 4 + 4)
                    pe.wait_ge(newT_out, b + 2)
                    pe.wait_ge(new_in[par], (b - par) * 8 + 16)
                    pe.wait_ge(pv_out, b + 1)
                    for r in range(2):
                        o = banks[:, 6, r * NQ:(r + 1) * NQ]
                        for k in range(NPAGE):
                            pe.matmul(o, rows[:, par, k, r * P:(r + 1) * P], probT[:, k, :], start=(k == 0), stop=False)
                        mm = pe.matmul(o, new_b[:, par, r * P:(r + 1) * P], probT_new[:], start=False, stop=True)
                    mm.then_inc(pv_ready, 1)
                    pe.wait_ge(pv_ready, b + 1)
                    pe.sem_inc(rows_free, 1)
                    pe.sem_inc(q_free, 1)

                def body(b, par):
                    scores(b, par)
                    values(b - 1, 1 - par)

                def tail(b, par):
                    body(b, par)
                    values(b, par)

                over(pe, lambda: scores(0, 0), body, tail)
                pe.wait_ge(pv_out, NSEQ + 1)
                for h in range(HEADS):
                    if h >= 2:
                        pe.wait_ge(o_out, h - 1)
                    for r in range(2):
                        mm = pe.matmul(banks[:, 4 + h % 2, 0:NS], sb.wkv[:, r, h * 256 + NOPE:(h + 1) * 256], olS[:, r, h, :],
                                       start=(r == 0), stop=(r == 1))
                    mm.then_inc(o_ready, 1)

            @block.scalar
            def _(act):
                act.sem_inc(read_a, 2)

                def chunk(b, par, c):
                    u = 3 * c + 1
                    act.wait_ge(bank_full[u % 4], key_use(b, u) + 1)
                    act.wait_ge(scored, b * NCH + c + 1)
                    act.activation(keyT[:, c % 2, 1, :], banks[:, u % 4, :], ACT.Copy).then_inc(keys_a, 1)
                    act.wait_ge(keys_a, b * NCH + c + 1)
                    act.sem_inc(bank_free[u % 4], 1)

                def copy_scores(b, par, c):
                    act.wait_ge(scored, b * NCH + c + 3)
                    act.activation(score[:, par, c * 512:(c + 1) * 512], banks[0:NQ, 4 + c % 2, :], ACT.Copy).then_inc(read_a, 1)

                def chunks(b, par):
                    act.wait_ge(newT, b)
                    chunk(b, par, 0)
                    for c in range(NCH):
                        if c + 1 < NCH:
                            chunk(b, par, c + 1)
                        copy_scores(b, par, c)
                    act.wait_ge(negd, b + 1)
                    act.wait_ge(read_a, (b + 1) * NCH + 2)
                    act.activation(score[:, par, :], score[:, par, :], ACT.Exp, bias=stat[:, par, 1:2], scale=ATT_SCALE,
                                   accum_out=stat[:, par, 2:3]).then_inc(expd, 1)

                over(act, lambda: chunks(0, 0), chunks, chunks)

            @block.vector
            def _(dve):
                dve.sem_inc(scored, 2)
                dve.sem_inc(masked, 1)
                dve.sem_inc(newT_out, 1)
                dve.sem_inc(newT, 1)
                dve.sem_inc(pv_out, 1)
                for s in bank_free:
                    dve.sem_inc(s, 1)

                def keys(b, par, c):
                    for j in (0, 2):
                        u = 3 * c + j
                        n = P if j < 2 else ROPE
                        dve.wait_ge(bank_full[u % 4], key_use(b, u) + 1)
                        if j == 0:
                            dve.wait_ge(scored, b * NCH + c + 1)
                        ins = dve.tensor_copy(keyT[0:n, c % 2, j, :], banks[0:n, u % 4, :])
                        if j == 0:
                            ins.then_inc(bank_free[u % 4], 1)
                        else:
                            ins.then_inc(keys_v, 1)
                            dve.wait_ge(keys_v, b * NCH + c + 1)
                            dve.sem_inc(bank_free[u % 4], 1)

                def chunk_max(b, par, c):
                    dve.wait_ge(read_a, b * NCH + c + 3)
                    dve.reduce_max(mx[:, par, c:c + 1], score[:, par, c * 512:(c + 1) * 512], AX).then_inc(read_v, 1)

                def chunks(b, par, between):
                    keys(b, par, 0)
                    for c in range(NCH):
                        if c + 1 < NCH:
                            keys(b, par, c + 1)
                        chunk_max(b, par, c)
                        if c == 1:
                            between()
                    dve.wait_ge(new_scored, b + 1)
                    fresh = score[:, par, PAST:NKEY]
                    dve.tensor_tensor(fresh, banks[0:NQ, 7, 0:TS], K[0:NQ, K_NEW:K_NEW + TS], ALU.add).then_inc(masked, 1)
                    dve.wait_ge(masked, b + 2)
                    dve.reduce_max(mx[:, par, NCH:NCH + 1], fresh, AX).then_inc(vec, 1)
                    dve.wait_ge(vec, b * 3 + 1)
                    dve.wait_ge(read_v, (b + 1) * NCH)
                    dve.reduce_max(stat[:, par, 0:1], mx[:, par, :], AX).then_inc(vec, 1)
                    dve.wait_ge(vec, b * 3 + 2)
                    dve.tensor_scalar(stat[:, par, 1:2], stat[:, par, 0:1], -ATT_SCALE, None, ALU.mult).then_inc(negd, 1)

                def scale(b, par):
                    dve.wait_ge(expd, b + 1)
                    dve.reciprocal(stat[:, par, 2:3], stat[:, par, 2:3]).then_inc(vec, 1)
                    dve.wait_ge(vec, b * 3 + 3)
                    dve.tensor_scalar(score[:, par, :], score[:, par, :], stat[:, par, 2:3], None, ALU.mult).then_inc(scaled, 1)

                def out(b, par):
                    for m in range(4):
                        u = 3 * NCH + m
                        dve.wait_ge(bank_full[u % 4], prob_use(b) + 1)
                        dve.tensor_copy(probT[:, 8 * m:8 * m + 8, :], banks[:, u % 4, :].rearrange("p (k n) -> p k n", k=8)).then_inc(probs_out, 1)
                        dve.wait_ge(probs_out, b * 4 + m + 1)
                        dve.sem_inc(bank_free[u % 4], 1)
                    dve.wait_ge(newT, b + 2)
                    dve.tensor_copy(probT_new[:], banks[0:TS, 7, 128:128 + NQ]).then_inc(newT_out, 1)
                    dve.wait_ge(pv_ready, b + 1)
                    dve.tensor_copy(olS[:, :, :, bass.ds(b * TS, TS)],
                                    banks[:, 6, 0:2 * NQ].rearrange("p (r h t) -> p r h t", r=2, h=HEADS)).then_inc(pv_out, 1)

                def body(b, par):
                    chunks(b, par, lambda: scale(b - 1, 1 - par))
                    out(b - 1, 1 - par)

                def tail(b, par):
                    body(b, par)
                    scale(b, par)
                    out(b, par)

                over(dve, lambda: chunks(0, 0, lambda: None), body, tail)
                for h in range(HEADS):
                    dve.wait_ge(o_ready, h + 1)
                    dve.tensor_copy(sb.oT[:, h, SEQ:T], banks[:, 4 + h % 2, 0:NS]).then_inc(o_out, 1)


def stage_turn_x(nc, io, sb):
    with ExitStack() as ctx:
        sem = ctx.enter_context(signals(nc, "turn_x"))
        x_tok = ctx.enter_context(nc.sbuf_tensor("x_tok4", [P, NT, D], F32))
        banks = ctx.enter_context(nc.psum_tensor("banks4x", [P, 8, 512], F32))
        x_in = [sem(f"x_in4{i}") for i in range(NT)]
        turned, turned_out = sem("turned4"), sem("turned_out4")
        with nc.Block() as block:
            @block.sync
            def _(sp):
                for i in range(NT):
                    sp.dma_start(x_tok[0:ROWS[i], i, :], token_dram(io.xp, io.xs, i)).then_inc(x_in[i], 16)

            @block.tensor
            def _(pe):
                for i in range(NT):
                    n = ROWS[i]
                    pe.wait_ge(x_in[i], 16)
                    for h in range(2):
                        u = 2 * i + h
                        if u >= 8:
                            pe.wait_ge(turned_out, u - 7)
                        for k in range(4):
                            mm = pe.transpose(banks[:, u % 8, k * n:(k + 1) * n],
                                              x_tok[0:n, i, (4 * h + k) * P:(4 * h + k + 1) * P], sb.const[0:n, K_ID:K_ID + n])
                        mm.then_inc(turned, 1)

            @block.vector
            def _(dve):
                for u in range(2 * NT):
                    i, h = divmod(u, 2)
                    n = ROWS[i]
                    dve.wait_ge(turned, u + 1)
                    dve.tensor_copy(sb.xT[:, 4 * h:4 * h + 4, P * i:P * i + n],
                                    banks[:, u % 8, 0:4 * n].rearrange("p (k n) -> p k n", k=4)).then_inc(turned_out, 1)


def stage_merge(nc, io, sb, gate_col, w, x_of, nk, first, tag):
    with ExitStack() as ctx:
        sem = ctx.enter_context(signals(nc, "merge" + tag))
        buf = lambda n, s: ctx.enter_context(nc.sbuf_tensor(n + tag, s, F32))
        CW = 256
        w_gate = buf("w_gate", [P, 2, KD, CW])
        w_br = buf("w_br", [P, 2, nk, CW])
        sig = buf("sig", [P, 2, T])
        prod = buf("prod", [P, 2, T])
        banks = ctx.enter_context(nc.psum_tensor("banks" + tag, [P, 8, 512], F32))
        w_in_ = [sem(f"w_in{i}") for i in range(2)]
        gate_ready, y_ready, sig_out, prod_out, merged = sem("gate_ready"), sem("y_ready"), sem("sig_out"), sem("prod_out"), sem("merged")
        n_m, n_c = D // P, D // CW
        gate_view = io.w_in.rearrange("(k p) n -> p k n", p=P)
        w_view = w.rearrange("(k p) n -> p k n", p=P)

        with nc.Block() as block:
            @block.sync
            def _(sp):
                for c in range(n_c):
                    if c >= 2:
                        sp.wait_ge(y_ready, 2 * c - 2)
                    sp.dma_start(w_gate[:, c % 2], gate_view[:, :, gate_col + c * CW:gate_col + (c + 1) * CW]).then_inc(w_in_[c % 2], 16)
                    sp.dma_start(w_br[:, c % 2], w_view[:, :, c * CW:(c + 1) * CW]).then_inc(w_in_[c % 2], 16)

            @block.tensor
            def _(pe):
                for m in range(n_m):
                    c, at = m // 2, (m % 2) * P
                    b = 4 * (m % 2)
                    pe.wait_ge(w_in_[c % 2], 32 * (c // 2 + 1))
                    if m >= 2:
                        pe.wait_ge(sig_out, m - 1)
                        pe.wait_ge(prod_out, m - 1)
                    for piece in range(2):
                        for k in range(KD):
                            mm = pe.matmul(banks[:, b + piece, 0:H2], w_gate[:, c % 2, k, at:at + P],
                                           sb.xT[:, k, piece * H2:(piece + 1) * H2], start=(k == 0), stop=(k == KD - 1))
                    mm.then_inc(gate_ready, 1)
                    for piece in range(2):
                        for k in range(nk):
                            mm = pe.matmul(banks[:, b + 2 + piece, 0:H2], w_br[:, c % 2, k, at:at + P],
                                           x_of(k)[:, piece * H2:(piece + 1) * H2], start=(k == 0), stop=(k == nk - 1))
                    mm.then_inc(y_ready, 1)

            @block.scalar
            def _(act):
                for m in range(n_m):
                    b = 4 * (m % 2)
                    act.wait_ge(gate_ready, m + 1)
                    if m >= 2:
                        act.wait_ge(prod_out, m - 1)
                    act.activation(sig[:, m % 2, :].rearrange("p (a n) -> p a n", a=2), banks[:, b:b + 2, 0:H2], ACT.Sigmoid).then_inc(sig_out, 1)

            @block.vector
            def _(dve):
                for m in range(n_m):
                    b = 4 * (m % 2)
                    dve.wait_ge(y_ready, m + 1)
                    dve.wait_ge(sig_out, m + 1)
                    if not first and m >= 2:
                        dve.wait_ge(merged, m - 1)
                    o = sb.mergedT[:, m, :] if first else prod[:, m % 2, :]
                    dve.tensor_tensor(o.rearrange("p (a n) -> p a n", a=2), banks[:, b + 2:b + 4, 0:H2],
                                      sig[:, m % 2, :].rearrange("p (a n) -> p a n", a=2), ALU.mult).then_inc(prod_out, 1)
                    if not first:
                        dve.wait_ge(prod_out, m + 1)
                        dve.tensor_tensor(sb.mergedT[:, m, :], sb.mergedT[:, m, :], prod[:, m % 2, :], ALU.add).then_inc(merged, 1)


def stage_conv(nc, io, sb):
    NR = NSEQ * (KC - 1) + KC + 1
    NO = (KC - 1) * (1 + NSEQ)
    LP = SEQ + KC - 1
    LS = TS + KC - 1
    with ExitStack() as ctx:
        sem = ctx.enter_context(signals(nc, "conv"))
        buf = lambda n, s: ctx.enter_context(nc.sbuf_tensor(n, s, F32))
        w = buf("w_x", [P, 2, KD, 512])
        small = buf("small", [NR, CONV])
        smallT = buf("smallT", [P, NCT, NR])
        pre = buf("pre", [P, 3, LP + NSEQ * LS])
        acc = buf("acc", [P, 2, T])
        lastT = buf("lastT", [P, NCT, NO])
        last = buf("last", [NO, CONV])
        banks = ctx.enter_context(nc.psum_tensor("banks5", [P, 8, 512], F32))
        small_in, w_in_ = sem("small_in"), [sem("w_x_in0"), sem("w_x_in1")]
        small_ready, small_out, zeroed = sem("small_ready"), sem("small_out"), sem("zeroed5")
        ready, copied, state_put, tap, conved, done = (sem(n) for n in ("x_ready", "x_copied", "state_put", "tap", "conved", "silu_done"))
        last_ready, last_out, stored, kept = sem("last_ready"), sem("last_out"), sem("stored5"), sem("kept")
        S0, W0, B0 = 0, NSEQ * (KC - 1), NSEQ * (KC - 1) + KC
        PER = 17
        w_view = io.w_in.rearrange("(k p) n -> p k n", p=P)
        sample = lambda slot: pre[:, slot, LP:].rearrange("p (b t) -> p b t", b=NSEQ)

        with nc.Block() as block:
            @block.sync
            def _(sp):
                sp.dma_start(small[0:W0, :], io.conv).then_inc(small_in, 16)
                sp.dma_start(small[W0:B0, :], io.conv_w).then_inc(small_in, 16)
                sp.dma_start(small[B0:NR, :], io.conv_b).then_inc(small_in, 16)
                for c in range(CONV // 512):
                    if c >= 2:
                        sp.wait_ge(ready, 4 * (c - 1))
                    sp.dma_start(w[:, c % 2], w_view[:, :, C_X + c * 512:C_X + (c + 1) * 512]).then_inc(w_in_[c % 2], 16)
                sp.wait_ge(last_out, NCT // 4)
                sp.dma_start(io.o_convp, last[0:KC - 1, :]).then_inc(stored, 16)
                sp.dma_start(io.o_convs, last[KC - 1:NO, :]).then_inc(stored, 16)
                sp.wait_ge(stored, 32)

            @block.gpsimd
            def _(pool):
                pool.memset(pre[:, :, 0:KC - 1], 0.0).then_inc(zeroed, 1)

            @block.tensor
            def _(pe):
                pe.wait_ge(small_in, 48)
                for m in range(NCT):
                    mm = pe.transpose(banks[:, 6 + m // PER, (m % PER) * NR:(m % PER + 1) * NR], small[:, m * P:(m + 1) * P], sb.const[0:NR, K_ID:K_ID + NR])
                mm.then_inc(small_ready, 1)
                for m in range(NCT):
                    c, b = m // 4, 2 * (m % 3)
                    pe.wait_ge(w_in_[c % 2], 16 * (c // 2 + 1))
                    if m >= 3:
                        pe.wait_ge(copied, m - 2)
                    for piece in range(2):
                        for k in range(KD):
                            mm = pe.matmul(banks[:, b + piece, 0:H2], w[:, c % 2, k, (m % 4) * P:(m % 4 + 1) * P],
                                           sb.xT[:, k, piece * H2:(piece + 1) * H2], start=(k == 0), stop=(k == KD - 1))
                    mm.then_inc(ready, 1)
                pe.wait_ge(kept, NCT)
                for u in range(NCT // 4):
                    if u == 0:
                        pe.wait_ge(copied, NCT)
                    for k in range(4):
                        mm = pe.transpose(banks[0:NO, u, k * P:(k + 1) * P], lastT[:, 4 * u + k, :], sb.const[:, K_ID:K_ID + P])
                    mm.then_inc(last_ready, 1)

            @block.scalar
            def _(act):
                def silu(m):
                    act.wait_ge(conved, m + 1)
                    act.activation(sb.xbcT[:, m, :], acc[:, m % 2, :], ACT.Silu).then_inc(done, 1)

                for m in range(NCT):
                    b, s = 2 * (m % 3), m % 3
                    act.wait_ge(ready, m + 1)
                    if m >= 3:
                        act.wait_ge(kept, m - 2)
                    act.activation(pre[:, s, KC - 1:KC - 1 + H2], banks[:, b, 0:H2], ACT.Copy)
                    act.activation(pre[:, s, KC - 1 + H2:LP], banks[:, b + 1, 0:SEQ - H2], ACT.Copy)
                    act.activation(sample(s)[:, :, KC - 1:LS], banks[:, b + 1, SEQ - H2:H2].rearrange("p (b t) -> p b t", b=NSEQ),
                                   ACT.Copy).then_inc(copied, 1)
                    if m >= 1:
                        silu(m - 1)
                silu(NCT - 1)

            @block.vector
            def _(dve):
                dve.wait_ge(small_ready, 1)
                dve.tensor_copy(smallT[:, 0:PER, :], banks[:, 6, 0:PER * NR].rearrange("p (m r) -> p m r", m=PER))
                dve.tensor_copy(smallT[:, PER:NCT, :], banks[:, 7, 0:(NCT - PER) * NR].rearrange("p (m r) -> p m r", m=NCT - PER)).then_inc(small_out, 1)
                dve.wait_ge(small_out, 1)
                dve.wait_ge(zeroed, 1)
                for m in range(NCT):
                    s = m % 3
                    if m >= 3:
                        dve.wait_ge(kept, m - 2)
                    dve.tensor_copy(sample(s)[:, :, 0:KC - 1], smallT[:, m, S0:W0].rearrange("p (b k) -> p b k", b=NSEQ)).then_inc(state_put, 1)
                    dve.wait_ge(state_put, m + 1)
                    dve.wait_ge(copied, m + 1)
                    if m >= 2:
                        dve.wait_ge(done, m - 1)
                    ap, as_ = acc[:, m % 2, 0:SEQ], acc[:, m % 2, SEQ:T].rearrange("p (b t) -> p b t", b=NSEQ)
                    for k in range(KC):
                        wk = smallT[:, m, W0 + k:W0 + k + 1]
                        xp, xs = pre[:, s, k:k + SEQ], sample(s)[:, :, k:k + TS]
                        if k == 0:
                            bias = smallT[:, m, B0:B0 + 1]
                            dve.tensor_scalar(ap, xp, wk, bias, ALU.mult, ALU.add)
                            dve.tensor_scalar(as_, xs, wk, bias, ALU.mult, ALU.add).then_inc(tap, 1)
                        else:
                            dve.wait_ge(tap, m * (KC - 1) + k)
                            dve.scalar_tensor_tensor(out=ap, in0=xp, scalar=wk, in1=ap, op0=ALU.mult, op1=ALU.add)
                            ins = dve.scalar_tensor_tensor(out=as_, in0=xs, scalar=wk, in1=as_, op0=ALU.mult, op1=ALU.add)
                            ins.then_inc(conved if k == KC - 1 else tap, 1)
                    dve.tensor_copy(lastT[:, m, 0:KC - 1], pre[:, s, SEQ:LP])
                    dve.tensor_copy(lastT[:, m, KC - 1:NO].rearrange("p (b k) -> p b k", b=NSEQ), sample(s)[:, :, TS:LS]).then_inc(kept, 1)
                for u in range(NCT // 4):
                    dve.wait_ge(last_ready, u + 1)
                    dve.tensor_copy(last[:, u * 512:(u + 1) * 512], banks[0:NO, u, :]).then_inc(last_out, 1)


def stage_ssd(nc, io, sb):
    with ExitStack() as ctx:
        sem = ctx.enter_context(signals(nc, "ssd"))
        buf = lambda n, s: ctx.enter_context(nc.sbuf_tensor(n, s, F32))
        K = sb.const
        dt_b, a_b, d_b = buf("dt_b", [P, SH]), buf("a_b", [P, SH]), buf("d_b", [P, SH])
        gn = buf("gn", [P, DI])
        t1, t2, t3 = (buf(n, [P, NT, SH]) for n in ("t1", "t2", "t3"))
        dta, acs, aend, e_acs, w_end, e_end = (buf(n, [P, NT, SH]) for n in ("dta", "acs", "aend", "e_acs", "w_end", "e_end"))
        wz = buf("wz", [P, 2, KD, GW])
        h0 = buf("h0", [P, 4, NSEQ, NST])
        h0T = buf("h0T", [NST, 2, GW])
        xs_t = buf("xs_t", [P, 2, GW])
        b_t = buf("b_t", [P, 2, NST])
        cb = buf("cb", [P, P])
        dec = buf("dec", [P, 2, HG, P])
        xdt, xend, xd = buf("xdt", [P, 2, GW]), buf("xend", [P, 2, GW]), buf("xd", [P, 2, GW])
        y = buf("y", [P, 2, GW])
        off = buf("off", [P, GW])
        zs = buf("zs", [P, GW])
        junk = zs
        ssq = buf("ssq6", [P, 2])
        stT = buf("stT", [NST, GW])
        c_of = buf("c_of", [P, NSEQ, NS])
        b_of = buf("b_of", [NS, NSEQ, NST])
        e_seq = buf("e_seq", [P, 4, NSEQ])
        st_out = buf("st_out", [P, 4, NST])
        banks = ctx.enter_context(nc.psum_tensor("banks6", [P, 8, 512], F32))
        N = G * NT
        unit = lambda k: divmod(k, NT)
        vec_in, wz_in = sem("vec_in"), [sem("wz_in0"), sem("wz_in1")]
        h_in, h_out, p_out = sem("h_in"), sem("h_stored"), sem("p_stored")
        prep_v, prep_a, sums_ready, sums_out = sem("prep_v"), sem("prep_a"), sem("sums_ready"), sem("sums_out")
        xs_ready, xs_out, cb_ready, cb_out, acs_ready, seg_out, dec_out, w_out = (sem(n) for n in (
            "xs_ready", "xs_out", "cb_ready", "cb_out", "acs_ready", "seg_out", "dec_out", "w_out"))
        scaled, of_seq, z_ready, z_out, y_ready, y_step, gated, squared, rooted, inverse, normed = (sem(n) for n in (
            "x_scaled", "of_seq", "z_ready", "z_out", "y_ready", "y_step", "gated", "squared6", "rooted6", "inverse", "normed6"))
        yt_ready, yt_out, st_ready, st_step, st_new = (sem(n) for n in ("yt_ready", "yt_out", "st_ready", "st_step", "st_new"))
        hT_ready, hT_out, off_part, fin_ready, fin_out, hs_ready, hs_out = (sem(n) for n in (
            "hT_ready", "hT_out", "off_part", "fin_ready", "fin_out", "hs_ready", "hs_out"))
        e_out, y_sum, mean_ready = sem("e_out"), sem("y_sum"), sem("mean_ready")
        heads = lambda t, n: t.rearrange("p (h d) -> p h d", h=HG)
        z_view = io.w_in.rearrange("(k p) n -> p k n", p=P)
        tri = lambda i, n: K[0:n, K_TRI:K_TRI + n] if i < 4 else K[0:n, K_BTRI:K_BTRI + n]

        with nc.Block() as block:
            @block.sync
            def _(sp):
                for t, src in ((dt_b, io.dt_bias), (a_b, io.a_log), (d_b, io.d_skip)):
                    sp.dma_start(t[:], src.broadcast_to((P, SH))).then_inc(vec_in, 16)
                sp.dma_start(gn[:], io.gn.broadcast_to((P, DI))).then_inc(vec_in, 16)
                for g in range(G):
                    if g >= 2:
                        sp.wait_ge(z_ready, NT * (g - 1))
                    sp.dma_start(wz[:, g % 2], z_view[:, :, C_Z + g * GW:C_Z + (g + 1) * GW]).then_inc(wz_in[g % 2], 16)
                    if g >= 1:
                        sp.wait_ge(fin_out, g)
                        sp.dma_start(io.o_ssmp[(g - 1) * GW:g * GW, :].rearrange("(q p) n -> p q n", p=P), st_out[:]).then_inc(p_out, 16)
                        sp.wait_ge(hs_out, 8 * g)
                        for q in range(4):
                            at = (g - 1) * GW + q * P
                            sp.dma_start(io.o_ssms[:, at:at + P, :].rearrange("b p n -> p b n"), h0[:, q]).then_inc(h_out, 16)
                        sp.wait_ge(h_out, 64 * g)
                    for q in range(4):
                        at = g * GW + q * P
                        sp.dma_start(h0[:, q], io.ssm[:, at:at + P, :].rearrange("b p n -> p b n")).then_inc(h_in, 16)
                sp.wait_ge(fin_out, G)
                sp.dma_start(io.o_ssmp[(G - 1) * GW:G * GW, :].rearrange("(q p) n -> p q n", p=P), st_out[:]).then_inc(p_out, 16)
                sp.wait_ge(hs_out, 8 * G)
                for q in range(4):
                    at = (G - 1) * GW + q * P
                    sp.dma_start(io.o_ssms[:, at:at + P, :].rearrange("b p n -> p b n"), h0[:, q]).then_inc(h_out, 16)
                sp.wait_ge(p_out, 16 * G)
                sp.wait_ge(h_out, 64 * G)

            @block.gpsimd
            def _(pool):
                pool.wait_ge(prep_v, 9)
                pool.wait_ge(vec_in, 64)
                for k in range(N):
                    g, i = unit(k)
                    n = ROWS[i]
                    pool.wait_ge(xs_out, k + 1)
                    if k >= 2:
                        pool.wait_ge(st_ready, k - 1)
                        pool.wait_ge(y_step, 2 * (k - 1))
                    x = heads(xs_t[0:n, k % 2], n)
                    for o, f in ((xdt, sb.dt[0:n, i]), (xend, w_end[0:n, i]), (xd, d_b[0:n])):
                        ins = pool.tensor_tensor(heads(o[0:n, k % 2], n), x, f[:, g * HG:(g + 1) * HG].unsqueeze(2).broadcast_to((n, HG, PD)), ALU.mult)
                    ins.then_inc(scaled, 1)
                    if i == NT - 1:
                        if g >= 1:
                            pool.wait_ge(hs_ready, 8 * g)
                        pool.tensor_tensor(c_of[:], sb.xbcT[:, 20 + g, SEQ:T].unsqueeze(1).broadcast_to((P, NSEQ, NS)),
                                           K[:, K_BCOL:K_BCOL + NSEQ * NS].rearrange("p (b n) -> p b n", b=NSEQ), ALU.mult)
                        pool.wait_ge(cb_out, k + 1)
                        pool.tensor_tensor(b_of[:], b_t[0:NS, k % 2, :].unsqueeze(1).broadcast_to((NS, NSEQ, NST)),
                                           K[0:NS, K_BROW:K_BROW + NSEQ].unsqueeze(2).broadcast_to((NS, NSEQ, NST)), ALU.mult).then_inc(of_seq, 1)

            @block.tensor
            def _(pe):
                pe.wait_ge(prep_v, 6)
                for i in range(NT):
                    n = ROWS[i]
                    pe.matmul(banks[0:n, 0, i * SH:(i + 1) * SH], tri(i, n), dta[0:n, i, :], start=True, stop=True)
                    last = K[0:n, K_ONE:K_ONE + n] if i < 4 else K[0:n, K_BALL:K_BALL + n]
                    mm = pe.matmul(banks[0:n, 1, i * SH:(i + 1) * SH], last, dta[0:n, i, :], start=True, stop=True)
                mm.then_inc(sums_ready, 1)
                pe.wait_ge(sums_out, 1)

                def inputs(k):
                    g, i = unit(k)
                    n = ROWS[i]
                    at = slice(P * i, P * i + n)
                    if k >= 1:
                        pe.wait_ge(xs_out, k)
                    if k >= 3:
                        pe.wait_ge(yt_out, k - 2)
                    for q in range(4):
                        mm = pe.transpose(banks[0:n, 0, q * P:(q + 1) * P], sb.xbcT[:, 4 * g + q, at], K[:, K_ID:K_ID + P])
                    mm.then_inc(xs_ready, 1)
                    if k >= 1:
                        pe.wait_ge(cb_out, k)
                        if unit(k - 1)[1] == NT - 1:
                            pe.wait_ge(e_out, unit(k - 1)[0] + 1)
                    pe.transpose(banks[0:n, 1, 0:P], sb.xbcT[:, 16 + g, at], K[:, K_ID:K_ID + P])
                    mm = pe.matmul(banks[0:n, 1, P:P + n], sb.xbcT[:, 16 + g, at], sb.xbcT[:, 20 + g, at], start=True, stop=True)
                    if i == NT - 1:
                        for h in range(HG):
                            q, half = h // 2, PD * (h % 2)
                            e_h = e_end[0:n, i, g * HG + h:g * HG + h + 1].broadcast_to((n, PD))
                            mm = pe.matmul(banks[half:half + PD, 1, 256 + q * NSEQ:256 + (q + 1) * NSEQ], e_h,
                                           K[0:n, K_BEND:K_BEND + NSEQ], start=True, stop=True)
                    mm.then_inc(cb_ready, 1)
                    if k >= 1:
                        pe.wait_ge(seg_out, k)
                    for h in range(HG):
                        mm = pe.matmul(banks[0:n, 2 + h // 4, (h % 4) * P:(h % 4) * P + n],
                                       dta[0:n, i, g * HG + h:g * HG + h + 1].broadcast_to((n, n)), tri(i, n), start=True, stop=True)
                    mm.then_inc(acs_ready, 1)

                def gate(k):
                    g, i = unit(k)
                    n = ROWS[i]
                    pe.wait_ge(wz_in[g % 2], 16 * (g // 2 + 1))
                    if k >= 1:
                        pe.wait_ge(z_out, k)
                    for q in range(KD):
                        mm = pe.matmul(banks[0:n, 7, :], sb.xT[:, q, P * i:P * i + n], wz[:, g % 2, q, :], start=(q == 0), stop=(q == KD - 1))
                    mm.then_inc(z_ready, 1)

                def outputs(k):
                    g, i = unit(k)
                    n = ROWS[i]
                    at = slice(P * i, P * i + n)
                    pe.wait_ge(w_out, k + 1)
                    pe.wait_ge(scaled, k + 1)
                    if k >= 1:
                        pe.wait_ge(y_step, 2 * k)
                    for h in range(HG):
                        pe.matmul(banks[0:n, 4, h * PD:(h + 1) * PD], dec[0:n, k % 2, h, 0:n], xdt[0:n, k % 2, h * PD:(h + 1) * PD], start=True, stop=True)
                    if i < NT - 1:
                        pe.wait_ge(st_new, NT * g + i + 1)
                        pe.matmul(banks[0:n, 5, :], sb.xbcT[:, 20 + g, at], stT[:], start=True, stop=True).then_inc(y_ready, 1)
                        if g >= 1 and i == 0:
                            pe.wait_ge(hs_out, 8 * g)
                        pe.matmul(banks[0:NST, 6, :], b_t[0:n, k % 2, :], xend[0:n, k % 2, :], start=True, stop=True).then_inc(st_ready, 1)
                        return
                    pe.wait_ge(st_new, NT * (g + 1))
                    for q in range(4):
                        mm = pe.transpose(banks[:, 6, q * P:(q + 1) * P], stT[:, q * P:(q + 1) * P], K[:, K_ID:K_ID + P])
                    mm.then_inc(fin_ready, 1)
                    pe.wait_ge(h_in, 64 * (g + 1))
                    pe.wait_ge(of_seq, g + 1)
                    for b in range(NSEQ):
                        m = NSEQ * g + b
                        if b == 0:
                            pe.wait_ge(fin_out, g + 1)
                        else:
                            pe.wait_ge(hT_out, m)
                        for q in range(4):
                            mm = pe.transpose(banks[:, 6, q * P:(q + 1) * P], h0[:, q, b, :], K[:, K_ID:K_ID + P])
                        mm.then_inc(hT_ready, 1)
                        pe.wait_ge(hT_out, m + 1)
                        mm = pe.matmul(banks[0:n, 5, :], c_of[:, b, :], h0T[:, b % 2, :], start=(b == 0), stop=(b == NSEQ - 1))
                        mm.then_inc(off_part, 1)
                        if b == NSEQ - 1:
                            pe.wait_ge(off_part, m + 1)
                            pe.sem_inc(y_ready, 1)
                    for u in range(8):
                        q, half = divmod(u, 2)
                        if u >= 1:
                            pe.wait_ge(hs_out, 8 * g + u)
                        mm = pe.matmul(banks[:, 6, :], xend[0:n, k % 2, q * P:(q + 1) * P], b_of[:, 4 * half:4 * half + 4, :],
                                       start=True, stop=True)
                        mm.then_inc(hs_ready, 1)
                    pe.wait_ge(hs_ready, 8 * g + 8)
                    pe.sem_inc(st_ready, 1)

                def turn(k):
                    g, i = unit(k)
                    n = ROWS[i]
                    pe.wait_ge(normed, k + 1)
                    pe.wait_ge(xs_out, min(k + 3, N))
                    if k + 3 > N and k >= 1:
                        pe.wait_ge(yt_out, k)
                    for q in range(4):
                        mm = pe.transpose(banks[:, 0, q * n:(q + 1) * n], y[0:n, k % 2, q * P:(q + 1) * P], K[0:n, K_ID:K_ID + n])
                    mm.then_inc(yt_ready, 1)

                for k in range(N + 2):
                    if k < N:
                        inputs(k)
                    if 1 <= k <= N:
                        gate(k - 1)
                        outputs(k - 1)
                    if k >= 2:
                        turn(k - 2)

            @block.scalar
            def _(act):
                act.wait_ge(prep_v, 3)
                act.activation(t2[:], t2[:], ACT.Exp).then_inc(prep_a, 1)
                act.wait_ge(vec_in, 64)
                act.activation(a_b[:], a_b[:], ACT.Exp).then_inc(prep_a, 1)
                act.wait_ge(prep_v, 4)
                act.activation(t3[:], acs[:], ACT.Ln).then_inc(prep_a, 1)
                act.wait_ge(sums_out, 1)
                act.activation(e_acs[:], acs[:], ACT.Exp)
                act.activation(e_end[:], aend[:], ACT.Exp).then_inc(prep_a, 1)
                act.wait_ge(prep_v, 8)
                act.activation(w_end[:], w_end[:], ACT.Exp).then_inc(prep_a, 1)
                for k in range(N + 2):
                    if k < N:
                        g, i = unit(k)
                        n = ROWS[i]
                        act.wait_ge(xs_ready, k + 1)
                        if k >= 2:
                            act.wait_ge(scaled, k - 1)
                        act.activation(xs_t[0:n, k % 2, :], banks[0:n, 0, :], ACT.Copy).then_inc(xs_out, 1)
                        act.wait_ge(seg_out, k + 1)
                        act.activation(dec[0:n, k % 2, :, 0:n], dec[0:n, k % 2, :, 0:n], ACT.Exp).then_inc(dec_out, 1)
                    if 1 <= k <= N:
                        j = k - 1
                        g, i = unit(j)
                        n = ROWS[i]
                        act.wait_ge(z_ready, j + 1)
                        if j >= 1:
                            act.wait_ge(gated, j)
                        act.activation(zs[0:n, :], banks[0:n, 7, :], ACT.Silu).then_inc(z_out, 1)
                        if i == NT - 1:
                            act.wait_ge(fin_ready, g + 1)
                            if g >= 1:
                                act.wait_ge(p_out, 16 * g)
                            act.activation(st_out[:].rearrange("p q n -> p (q n)"), banks[:, 6, :], ACT.Copy).then_inc(fin_out, 1)
                            for b in range(NSEQ):
                                m = NSEQ * g + b
                                act.wait_ge(hT_ready, m + 1)
                                if m >= 2:
                                    act.wait_ge(off_part, m - 1)
                                act.activation(h0T[:, b % 2, :], banks[:, 6, :], ACT.Copy).then_inc(hT_out, 1)
                        act.wait_ge(gated, j + 1)
                        if j >= 1:
                            act.wait_ge(squared, j)
                        act.activation(junk[0:n, :], y[0:n, j % 2, :], ACT.Square, accum_out=ssq[0:n, 0:1]).then_inc(squared, 1)
                        act.wait_ge(mean_ready, j + 1)
                        act.activation(ssq[0:n, 1:2], ssq[0:n, 1:2], ACT.Sqrt).then_inc(rooted, 1)
                    if k >= 2:
                        j = k - 2
                        g, i = unit(j)
                        n = ROWS[i]
                        act.wait_ge(yt_ready, j + 1)
                        act.activation(sb.yT[:, 4 * g:4 * g + 4, P * i:P * i + n], banks[:, 0, 0:4 * n].rearrange("p (q n) -> p q n", q=4),
                                       ACT.Copy).then_inc(yt_out, 1)

            @block.vector
            def _(dve):
                all_tiles = lambda t: t[:].unsqueeze(1).broadcast_to((P, NT, SH))
                dve.wait_ge(vec_in, 64)
                dve.tensor_tensor(t1[:], sb.dt[:], all_tiles(dt_b), ALU.add).then_inc(prep_v, 1)
                dve.wait_ge(prep_v, 1)
                dve.tensor_scalar(t2[:], t1[:], -1.0, None, ALU.mult).then_inc(prep_v, 1)
                dve.wait_ge(prep_v, 2)
                dve.tensor_tensor(t2[:], t2[:], t1[:], ALU.min).then_inc(prep_v, 1)
                dve.wait_ge(prep_a, 2)
                dve.tensor_scalar(acs[:], t2[:], 1.0, None, ALU.add).then_inc(prep_v, 1)
                dve.wait_ge(prep_v, 4)
                dve.reciprocal(aend[:], acs[:])
                dve.scalar_tensor_tensor(out=e_acs[:], in0=acs[:], scalar=-1.0, in1=t2[:], op0=ALU.add, op1=ALU.subtract)
                dve.tensor_scalar(t1[:], t1[:], 0.0, None, ALU.max)
                dve.tensor_scalar(a_b[:], a_b[:], -1.0, None, ALU.mult).then_inc(st_step, 1)
                dve.wait_ge(st_step, 1)
                dve.tensor_tensor(e_acs[:], e_acs[:], aend[:], ALU.mult).then_inc(st_step, 1)
                dve.wait_ge(st_step, 2)
                dve.wait_ge(prep_a, 3)
                dve.tensor_tensor(t3[:], t3[:], e_acs[:], ALU.subtract).then_inc(st_step, 1)
                dve.wait_ge(st_step, 3)
                dve.tensor_tensor(sb.dt[:], t3[:], t1[:], ALU.add).then_inc(prep_v, 1)
                dve.wait_ge(prep_v, 5)
                dve.tensor_tensor(dta[:], sb.dt[:], all_tiles(a_b), ALU.mult).then_inc(prep_v, 1)
                dve.wait_ge(prep_v, 6)
                dve.memset(acs[NS:P, NT - 1, :], 0.0)
                dve.memset(aend[NS:P, NT - 1, :], 0.0)
                dve.memset(stT[:], 0.0).then_inc(st_new, 1)
                dve.wait_ge(sums_ready, 1)
                for o, b in ((acs, 0), (aend, 1)):
                    dve.tensor_copy(o[:, 0:4, :], banks[:, b, 0:4 * SH].rearrange("p (i h) -> p i h", i=4))
                    ins = dve.tensor_copy(o[0:NS, 4, :], banks[0:NS, b, 4 * SH:5 * SH])
                ins.then_inc(sums_out, 1)
                dve.wait_ge(sums_out, 1)
                dve.wait_ge(prep_a, 3)
                dve.tensor_tensor(t1[:], aend[:], acs[:], ALU.subtract).then_inc(prep_v, 1)
                dve.wait_ge(prep_v, 7)
                dve.tensor_copy(w_end[:], t1[:]).then_inc(prep_v, 1)
                dve.wait_ge(prep_a, 5)
                dve.tensor_tensor(w_end[:], w_end[:], sb.dt[:], ALU.mult).then_inc(prep_v, 1)
                for k in range(N + 1):
                    if k < N:
                        g, i = unit(k)
                        n = ROWS[i]
                        dve.wait_ge(cb_ready, k + 1)
                        if k >= 2:
                            dve.wait_ge(st_ready, k - 1)
                        if k >= 1:
                            dve.wait_ge(w_out, k)
                        dve.tensor_copy(b_t[0:n, k % 2, :], banks[0:n, 1, 0:P])
                        ins = dve.tensor_tensor(cb[0:n, 0:n], banks[0:n, 1, P:P + n], tri(i, n), ALU.mult)
                        if i == NT - 1:
                            dve.tensor_copy(e_seq[:], banks[:, 1, 256:256 + 4 * NSEQ].rearrange("p (q b) -> p q b", q=4)).then_inc(e_out, 1)
                            dve.wait_ge(e_out, g + 1)
                            dve.sem_inc(cb_out, 1)
                        else:
                            ins.then_inc(cb_out, 1)
                        dve.wait_ge(acs_ready, k + 1)
                        if k >= 2:
                            dve.wait_ge(y_ready, k - 1)
                        for h in range(HG):
                            ins = dve.tensor_scalar(dec[0:n, k % 2, h, 0:n], banks[0:n, 2 + h // 4, (h % 4) * P:(h % 4) * P + n],
                                                    acs[0:n, i, g * HG + h:g * HG + h + 1], 0.0, ALU.subtract, ALU.min)
                        ins.then_inc(seg_out, 1)
                        dve.wait_ge(dec_out, k + 1)
                        dve.wait_ge(cb_out, k + 1)
                        dve.tensor_tensor(dec[0:n, k % 2, :, 0:n], dec[0:n, k % 2, :, 0:n], cb[0:n, 0:n].unsqueeze(1).broadcast_to((n, HG, n)), ALU.mult).then_inc(w_out, 1)
                    if k >= 1:
                        j = k - 1
                        g, i = unit(j)
                        n = ROWS[i]
                        hs = slice(g * HG, (g + 1) * HG)
                        dve.wait_ge(y_ready, j + 1)
                        dve.tensor_tensor(heads(off[0:n], n), heads(banks[0:n, 5, :], n), e_acs[0:n, i, hs].unsqueeze(2).broadcast_to((n, HG, PD)),
                                          ALU.mult).then_inc(y_step, 1)
                        dve.wait_ge(y_step, 2 * j + 1)
                        if j >= 2:
                            dve.wait_ge(yt_ready, j - 1)
                        dve.wait_ge(scaled, j + 1)
                        dve.tensor_tensor(y[0:n, j % 2, :], off[0:n], xd[0:n, j % 2, :], ALU.add).then_inc(y_sum, 1)
                        dve.wait_ge(y_sum, j + 1)
                        dve.tensor_tensor(y[0:n, j % 2, :], y[0:n, j % 2, :], banks[0:n, 4, :], ALU.add).then_inc(y_step, 1)
                        dve.wait_ge(y_step, 2 * j + 2)
                        dve.wait_ge(z_out, j + 1)
                        dve.tensor_tensor(y[0:n, j % 2, :], y[0:n, j % 2, :], zs[0:n, :], ALU.mult).then_inc(gated, 1)
                        if i < NT - 1:
                            dve.wait_ge(st_ready, j + 1)
                            dve.tensor_tensor(heads(stT[:], P), heads(stT[:], P), e_end[:, i, hs].unsqueeze(2).broadcast_to((P, HG, PD)), ALU.mult).then_inc(st_step, 1)
                            dve.wait_ge(st_step, 4 + (NT - 1) * g + i)
                            dve.tensor_tensor(stT[:], stT[:], banks[:, 6, :], ALU.add).then_inc(st_new, 1)
                        else:
                            for u in range(8):
                                q, half = divmod(u, 2)
                                dve.wait_ge(hs_ready, 8 * g + u + 1)
                                for b in range(4):
                                    s = 4 * half + b
                                    ins = dve.scalar_tensor_tensor(out=h0[:, q, s, :], in0=h0[:, q, s, :], scalar=e_seq[:, q, s:s + 1],
                                                                   in1=banks[:, 6, b * NST:(b + 1) * NST], op0=ALU.mult, op1=ALU.add)
                                ins.then_inc(hs_out, 1)
                            if g + 1 < G:
                                dve.memset(stT[:], 0.0).then_inc(st_new, 1)
                        dve.wait_ge(squared, j + 1)
                        dve.tensor_scalar(ssq[0:n, 1:2], ssq[0:n, 0:1], 1.0 / GW, RMS_EPS, ALU.mult, ALU.add).then_inc(mean_ready, 1)
                        dve.wait_ge(rooted, j + 1)
                        dve.reciprocal(ssq[0:n, 1:2], ssq[0:n, 1:2]).then_inc(inverse, 1)
                        dve.wait_ge(inverse, j + 1)
                        dve.scalar_tensor_tensor(out=y[0:n, j % 2, :], in0=y[0:n, j % 2, :], scalar=ssq[0:n, 1:2],
                                                 in1=gn[0:n, g * GW:(g + 1) * GW], op0=ALU.mult, op1=ALU.mult).then_inc(normed, 1)


def stage_out(nc, io, sb):
    with ExitStack() as ctx:
        sem = ctx.enter_context(signals(nc, "out"))
        buf = lambda n, s: ctx.enter_context(nc.sbuf_tensor(n, s, F32))
        w = buf("w_o", [P, 2, KD, 512])
        x_tok = buf("x_tok7", [P, NT, D])
        g_b, b_b = buf("g1_b", [P, D]), buf("b1_b", [P, D])
        stats = buf("stats7", [P, 2, 6])
        mv = buf("mv7", [P, NT, 2])
        banks = ctx.enter_context(nc.psum_tensor("banks7", [P, 8, 512], F32))
        w_in_, x_in, gb_in, mixed, summed, stat, mean, rooted, inverse, normed, scaled, done, stored = (sem(n) for n in (
            "w_in", "x_in", "gb_in", "mixed", "summed", "stat", "mean", "rooted", "inverse", "normed", "scaled", "done", "stored"))
        w_view = io.wo.rearrange("(k p) n -> p k n", p=P)
        h = sb.h

        with nc.Block() as block:
            @block.sync
            def _(sp):
                for c in range(2):
                    sp.dma_start(w[:, c], w_view[:, :, c * 512:(c + 1) * 512]).then_inc(w_in_, 16)
                for i in range(NT):
                    sp.dma_start(x_tok[0:ROWS[i], i, :], token_dram(io.xp, io.xs, i)).then_inc(x_in, 16)
                sp.dma_start(g_b[:], io.g1.broadcast_to((P, D))).then_inc(gb_in, 16)
                sp.dma_start(b_b[:], io.b1.broadcast_to((P, D))).then_inc(gb_in, 16)
                for i in range(NT):
                    sp.wait_ge(done, i + 1)
                    sp.dma_start(io.h_rows[P * i:P * i + ROWS[i], :], h[0:ROWS[i], i, :]).then_inc(stored, 16)
                sp.wait_ge(stored, 16 * NT)

            @block.tensor
            def _(pe):
                pe.wait_ge(w_in_, 32)
                for i in range(NT):
                    n = ROWS[i]
                    if i >= 4:
                        pe.wait_ge(summed, i - 3)
                    for c in range(2):
                        for k in range(KD):
                            mm = pe.matmul(banks[0:n, 2 * (i % 4) + c, :], sb.mergedT[:, k, P * i:P * i + n], w[:, c, k, :],
                                           start=(k == 0), stop=(k == KD - 1))
                    mm.then_inc(mixed, 1)

            @block.vector
            def _(dve):
                dve.memset(mv[:], 1.0).then_inc(inverse, 1)
                dve.wait_ge(inverse, 1)
                dve.wait_ge(x_in, 16 * NT)
                for i in range(NT):
                    n = ROWS[i]
                    dve.wait_ge(mixed, i + 1)
                    for c in range(2):
                        at = slice(c * 512, (c + 1) * 512)
                        ins = dve.scalar_tensor_tensor(out=h[0:n, i, at], in0=x_tok[0:n, i, at], scalar=ALPHA,
                                                       in1=banks[0:n, 2 * (i % 4) + c, :], op0=ALU.mult, op1=ALU.add)
                    ins.then_inc(summed, 1)
                    dve.wait_ge(summed, i + 1)
                    if i >= 1:
                        dve.wait_ge(mean, i)
                    for c in range(2):
                        ins = dve.bn_stats(stats[0:n, c, :], h[0:n, i, c * 512:(c + 1) * 512])
                    ins.then_inc(stat, 1)
                    dve.wait_ge(stat, i + 1)
                    dve.bn_aggr(mv[0:n, i, :], stats[0:n].rearrange("p c s -> p (c s)")).then_inc(mean, 1)
                dve.wait_ge(mean, NT)
                dve.tensor_scalar(mv[:, :, 1:2], mv[:, :, 1:2], LN_EPS, None, ALU.add).then_inc(inverse, 1)
                dve.wait_ge(rooted, 1)
                dve.reciprocal(mv[:, :, 1:2], mv[:, :, 1:2]).then_inc(inverse, 1)
                dve.wait_ge(inverse, 3)
                dve.wait_ge(gb_in, 32)
                for i in range(NT):
                    n = ROWS[i]
                    dve.tensor_scalar(h[0:n, i, :], h[0:n, i, :], mv[0:n, i, 0:1], mv[0:n, i, 1:2], ALU.subtract, ALU.mult).then_inc(normed, 1)
                    dve.wait_ge(normed, i + 1)
                    dve.tensor_tensor(h[0:n, i, :], h[0:n, i, :], g_b[0:n], ALU.mult).then_inc(scaled, 1)
                    dve.wait_ge(scaled, i + 1)
                    dve.tensor_tensor(h[0:n, i, :], h[0:n, i, :], b_b[0:n], ALU.add).then_inc(done, 1)

            @block.scalar
            def _(act):
                act.wait_ge(inverse, 2)
                act.activation(mv[:, :, 1:2], mv[:, :, 1:2], ACT.Sqrt).then_inc(rooted, 1)


def stage_route(nc, io, sb):
    with ExitStack() as ctx:
        sem = ctx.enter_context(signals(nc, "route"))
        buf = lambda n, s, d=F32: ctx.enter_context(nc.sbuf_tensor(n, s, d))
        K = sb.const
        hT = buf("hT8", [P, KD, T])
        wr = buf("wr", [P, KD, E])
        br = buf("br", [P, E])
        lg, gt, eq, run, sel, ex, place, pick, part = (buf(n, [P, NT, E]) for n in ("lg", "gt", "eq", "run", "sel", "ex", "place", "pick", "part"))
        top = buf("top", [P, NT, 8])
        few = buf("few", [P, NT])
        total = buf("total", [P, NT])
        slot_f = buf("slot_f", [P, NT, TOPK])
        pair = buf("pair", [P, NT * TOPK + 1, 2], I32)
        empty = buf("empty", [P, E * CAP // P, 2], I32)
        count = buf("count", [P, E])
        flag, nth, code, exp_of = (buf(n, [1, 4 * E]) for n in ("flag", "nth", "code", "exp_of"))
        match, found = buf("match", [1, NOVF + 1, 4 * E]), buf("found", [1, NOVF + 1, 4 * E])
        listed = buf("listed", [1, 2, NOVF + 1])
        banks = ctx.enter_context(nc.psum_tensor("banks8", [P, 8, 512], F32))
        wr_in, turned, turned_out, logit, vec, expd, ranked = (sem(n) for n in ("wr_in", "turned", "turned_out", "logit", "vec", "expd", "ranked"))
        chosen, slotted, listing, zeroed, cleared, scattered, tabled, listed_done = (sem(n) for n in (
            "chosen", "slotted", "listing", "zeroed", "cleared", "scattered", "tabled", "listed_done"))
        bc = lambda t: t.broadcast_to((P, NT, E))

        with nc.Block() as block:
            @block.sync
            def _(sp):
                sp.dma_start(wr[:], io.wr.rearrange("(k p) n -> p k n", p=P)).then_inc(wr_in, 16)
                sp.dma_start(br[:], io.br.broadcast_to((P, E))).then_inc(wr_in, 16)
                sp.wait_ge(zeroed, 2)
                sp.dma_start(io.slots.rearrange("(p c) a -> p c a", p=P), empty[:]).then_inc(cleared, 16)
                sp.wait_ge(scattered, 16 * NT * TOPK)
                first = io.slots.rearrange("(e c) a -> c e a", c=CAP)[0:P]
                with nc.allow_non_contiguous_dma(reason="a table of 8-byte pairs"):
                    sp.dma_start(sb.tok[:, 0:E, :], first).then_inc(tabled, 16)
                sp.wait_ge(listed_done, 3)
                for q in range(NOVF + 1):
                    s = sp.value_load(sb.item_slot[0:1, q:q + 1], min_val=0, max_val=E * CAP - P)
                    sp.dma_start(sb.tok[:, E + q, :], io.slots[bass.ds(s, P), :]).then_inc(tabled, 16)
                sp.wait_ge(tabled, 16 * (NOVF + 2))

            @block.gpsimd
            def _(pool):
                pool.tensor_copy(pair[:], K[:, K_PAIR:K_BASE].rearrange("p (n a) -> p n a", a=2)).then_inc(zeroed, 1)
                pool.wait_ge(zeroed, 1)
                pool.tensor_copy(empty[:], pair[:, NT * TOPK:, :].broadcast_to((P, E * CAP // P, 2))).then_inc(zeroed, 1)
                pool.wait_ge(cleared, 16)
                pool.wait_ge(zeroed, 2)
                pool.wait_ge(slotted, 1)
                for i in range(NT):
                    for k in range(TOPK):
                        n = ROWS[i]
                        pool.indirect_dma_start(out=io.slots, out_offset=bass.IndirectOffsetOnAxis(ap=sb.slot[0:n, i, k:k + 1].bitcast(U32), axis=0),
                                                in_=pair[0:n, i * TOPK + k, :], in_offset=None).then_inc(scattered, 16)

            @block.tensor
            def _(pe):
                for i in range(NT):
                    n = ROWS[i]
                    for h in range(2):
                        u = 2 * i + h
                        if u >= 4:
                            pe.wait_ge(turned_out, u - 3)
                        for k in range(4):
                            mm = pe.transpose(banks[:, u % 4, k * n:(k + 1) * n], sb.h[0:n, i, (4 * h + k) * P:(4 * h + k + 1) * P], K[0:n, K_ID:K_ID + n])
                        mm.then_inc(turned, 1)
                pe.wait_ge(wr_in, 32)
                for i in range(NT):
                    n = ROWS[i]
                    pe.wait_ge(turned_out, 2 * i + 2)
                    for k in range(KD):
                        mm = pe.matmul(banks[0:n, 4 + i % 2, 64 * i:64 * i + E], hT[:, k, P * i:P * i + n], wr[:, k, :], start=(k == 0), stop=(k == KD - 1))
                    mm.then_inc(logit, 1)
                pe.wait_ge(chosen, 1)
                for i in range(NT):
                    n = ROWS[i]
                    for j in range(i):
                        pe.matmul(banks[0:n, 6, i * E:(i + 1) * E], K[:, K_ONE:K_ONE + n], sel[:, j, :], start=(j == 0), stop=False)
                    pe.matmul(banks[0:n, 6, i * E:(i + 1) * E], K[0:n, K_STRICT:K_STRICT + n], sel[0:n, i, :], start=(i == 0), stop=True)
                for j in range(NT):
                    mm = pe.matmul(banks[:, 7, 0:E], K[:, K_ONE:K_ONE + P], sel[:, j, :], start=(j == 0), stop=(j == NT - 1))
                mm.then_inc(ranked, 1)

            @block.scalar
            def _(act):
                for u in range(2 * NT):
                    i, h = divmod(u, 2)
                    n = ROWS[i]
                    act.wait_ge(turned, u + 1)
                    act.activation(hT[:, 4 * h:4 * h + 4, P * i:P * i + n], banks[:, u % 4, 0:4 * n].rearrange("p (k n) -> p k n", k=4),
                                   ACT.Copy).then_inc(turned_out, 1)
                act.wait_ge(expd, 1)
                act.activation(ex[:], ex[:], ACT.Exp).then_inc(expd, 1)

            @block.vector
            def _(dve):
                done = [0]

                def then(ins):
                    done[0] += 1
                    ins.then_inc(vec, 1)
                    dve.wait_ge(vec, done[0])

                then(dve.memset(lg[NS:P, NT - 1, :], 0.0))
                dve.wait_ge(wr_in, 32)
                for i in range(NT):
                    n = ROWS[i]
                    dve.wait_ge(logit, NT)
                    ins = dve.tensor_tensor(lg[0:n, i, :], banks[0:n, 4 + i % 2, 64 * i:64 * i + E], br[0:n], ALU.add)
                then(ins)
                for i in range(NT):
                    ins = dve.max(out=top[:, i, :], in_=lg[:, i, :])
                then(ins)
                fourth = bc(top[:, :, TOPK - 1:TOPK])
                dve.tensor_tensor(gt[:], lg[:], fourth, ALU.is_gt)
                dve.tensor_tensor(eq[:], lg[:], fourth, ALU.is_equal)
                then(dve.tensor_tensor(ex[:], lg[:], bc(top[:, :, 0:1]), ALU.subtract))
                dve.sem_inc(expd, 1)
                for i in range(NT):
                    dve.tensor_tensor_scan(run[:, i, :], K[:, K_ONE:K_ONE + E], eq[:, i, :], 0.0, ALU.mult, ALU.add)
                then(dve.reduce_sum(few[:], gt[:], AX))
                then(dve.tensor_scalar(few[:], few[:], -1.0, float(TOPK), ALU.mult, ALU.add))
                then(dve.tensor_tensor(run[:], run[:], bc(few[:].unsqueeze(2)), ALU.is_le))
                then(dve.tensor_tensor(run[:], run[:], eq[:], ALU.mult))
                then(dve.tensor_tensor(sel[:], run[:], gt[:], ALU.add))
                dve.memset(sel[NS:P, NT - 1, :], 0.0).then_inc(chosen, 1)
                dve.wait_ge(chosen, 1)
                dve.wait_ge(expd, 2)
                for i in range(NT):
                    dve.tensor_tensor_scan(run[:, i, :], K[:, K_ONE:K_ONE + E], sel[:, i, :], 0.0, ALU.mult, ALU.add)
                then(dve.tensor_tensor(ex[:], ex[:], sel[:], ALU.mult))
                then(dve.reduce_sum(total[:], ex[:], AX))
                then(dve.tensor_scalar(total[:], total[:], 1e-30, None, ALU.max))
                then(dve.reciprocal(total[:], total[:]))
                then(dve.tensor_tensor(ex[:], ex[:], bc(total[:].unsqueeze(2)), ALU.mult))
                dve.wait_ge(ranked, 1)
                base = K[:, K_BASE:K_BASE + E]
                dve.tensor_tensor(place[:, 0:4, :], banks[:, 6, 0:4 * E].rearrange("p (i e) -> p i e", i=4),
                                  base.unsqueeze(1).broadcast_to((P, 4, E)), ALU.add)
                dve.memset(place[NS:P, 4, :], 0.0)
                dve.tensor_tensor(place[0:NS, 4, :], banks[0:NS, 6, 4 * E:5 * E], base[0:NS], ALU.add)
                then(dve.tensor_copy(count[:], banks[:, 7, 0:E]))
                for k in range(TOPK):
                    then(dve.scalar_tensor_tensor(out=pick[:], in0=run[:], scalar=float(k + 1), in1=sel[:], op0=ALU.is_equal, op1=ALU.mult))
                    then(dve.tensor_tensor(part[:], pick[:], place[:], ALU.mult))
                    dve.reduce_sum(slot_f[:, :, k:k + 1], part[:], AX)
                    then(dve.tensor_tensor(pick[:], pick[:], ex[:], ALU.mult))
                    then(dve.reduce_sum(sb.gate[:, :, k:k + 1], pick[:], AX))
                dve.tensor_copy(sb.slot[:], slot_f[:]).then_inc(slotted, 1)
                for j in range(4):
                    ins = dve.tensor_scalar(flag[:, j * E:(j + 1) * E], count[0:1, :], float(P * (j + 1)), None, ALU.is_gt)
                then(ins)
                dve.tensor_tensor(code[:], flag[:], K[0:1, K_CODE:K_CODE + 4 * E], ALU.mult)
                dve.tensor_tensor(exp_of[:], flag[:], K[0:1, K_EXP:K_EXP + 4 * E], ALU.mult)
                then(dve.tensor_tensor_scan(nth[:], K[0:1, K_ONE:K_ONE + P], flag[:], 0.0, ALU.mult, ALU.add))
                wide = lambda t: t.unsqueeze(1).broadcast_to((1, NOVF + 1, 4 * E))
                then(dve.tensor_tensor(match[:], wide(nth[:]), K[0:1, K_ITEM:K_ITEM + NOVF + 1].unsqueeze(2).broadcast_to((1, NOVF + 1, 4 * E)), ALU.is_equal))
                for o, c in ((0, code), (1, exp_of)):
                    then(dve.tensor_tensor(found[:], match[:], wide(c[:]), ALU.mult))
                    then(dve.reduce_sum(listed[:, o, :], found[:], AX))
                dve.tensor_copy(sb.item_slot[:], listed[:, 0, :]).then_inc(listed_done, 1)
                dve.tensor_copy(sb.item_expert[:], listed[:, 1, :]).then_inc(listed_done, 1)
                dve.tensor_copy(sb.n_over[:], nth[:, 4 * E - 1:4 * E]).then_inc(listed_done, 1)


def stage_experts(nc, io, sb):
    NW = 12
    HALF = 2 * FF // 2
    with ExitStack() as ctx:
        sem = ctx.enter_context(signals(nc, "experts"))
        buf = lambda n, s: ctx.enter_context(nc.sbuf_tensor(n, s, F32))
        K = sb.const
        w = buf("w_e", [P, NW, 2, HALF])
        b_gu, b_dn = buf("b_gu", [1, 2, 2 * FF]), buf("b_dn", [1, 2, D])
        room, room2 = sb.xT[:].rearrange("p k t -> p (k t)"), sb.mergedT[:].rearrange("p k t -> p (k t)")
        x_raw = room[:, 0:2 * D].rearrange("p (b n) -> p b n", b=2)
        y_out = room[:, 2 * D:4 * D].rearrange("p (b n) -> p b n", b=2)
        xT = room2[:, 0:2 * D].rearrange("p (b k n) -> p b k n", b=2, k=KD)
        hid = room2[:, 2 * D:2 * D + FF]
        hidT = room2[:, 3 * D:3 * D + FF].rearrange("p (k n) -> p k n", n=P)
        g_c, u_c, sg, prod = (buf(n, [P, FF // 2]) for n in ("g_c", "u_c", "sg", "prod9"))
        banks = ctx.enter_context(nc.psum_tensor("banks9", [P, 8, 512], F32))
        w_in_ = [sem(f"w_in{s}") for s in range(NW)]
        b_in = [sem("b_in0"), sem("b_in1")]
        x_in = [sem("x_in0"), sem("x_in1")]
        index = ctx.enter_context(nc.sbuf_tensor("index9", [P, 2, 2], I32))
        indexed = sem("indexed")
        y_free, carried = sem("y_free"), sem("carried")
        w_used, xT_ready, xT_out = sem("w_used"), sem("xT_ready"), sem("xT_out")
        gu_ready, gu_read, clamped, sig_out, hid_ready, hT_ready, hT_out, y_ready, y_copied, y_stored, multiplied = (sem(n) for n in (
            "gu_ready", "gu_read", "clamped", "sig_out", "hid_ready", "hT_ready", "hT_out", "y_ready", "y_copied", "y_stored", "multiplied"))

        def items(eng, body):
            with eng.Fori(0, E // 2) as i:
                body(i * 2, 0, i * 2)
                body(i * 2 + 1, 1, i * 2 + 1)
            n = eng.value_load(sb.n_over[0:1, 0:1], min_val=0, max_val=NOVF)
            with eng.Fori(0, (NOVF + 1) // 2) as i:
                for par in range(2):
                    q = i * 2 + par
                    with eng.If(q < n):
                        e = None
                        if eng is nc.sync:
                            e = eng.value_load(sb.item_expert[0:1, bass.ds(q, 1)], min_val=0, max_val=E - 1)
                        body(q + E, par, e)
            return n

        with nc.Block() as block:
            @block.sync
            def _(sp):
                def load(it, par, e):
                    def one(s, src):
                        sp.wait_ge(w_used, it * NW + s + 1)
                        sp.dma_start(w[:, s], src).then_inc(w_in_[s], 16)

                    gu = io.wgu[bass.ds(e, 1)].rearrange("a (s c p) n -> p s c (a n)", c=2, p=P)
                    dn = io.wdn[bass.ds(e, 1)].rearrange("a (s c p) n -> p s c (a n)", c=2, p=P)
                    for s in range(4):
                        one(s, gu[:, s, :, 0:HALF])
                        if s == 0:
                            sp.dma_start(b_gu[:, par, :], io.bgu[bass.ds(e, 1), :]).then_inc(b_in[par], 16)
                            sp.dma_start(b_dn[:, par, :], io.bdn[bass.ds(e, 1), :]).then_inc(b_in[par], 16)
                    for s in range(4):
                        one(4 + s, gu[:, s, :, HALF:2 * HALF])
                    for s in range(4):
                        one(8 + s, dn[:, s])

                items(sp, load)

            @block.gpsimd
            def _(pool):
                def gather(it, par):
                    if not isinstance(it, int):
                        pool.wait_ge(xT_ready, it * 2)
                    pool.sem_inc(carried, 1)
                    pool.indirect_dma_start(out=x_raw[:, par, :], out_offset=None, in_=io.h_rows,
                                            in_offset=bass.IndirectOffsetOnAxis(ap=index[:, par, 0:1].bitcast(U32), axis=0)).then_inc(x_in[par], 16)

                def run(it, par, _):
                    pool.wait_ge(x_in[par], it_sum(it, par))
                    pool.tensor_copy(index[:, 1 - par:2 - par, :], sb.tok[:, bass.ds(it + 1, 1), :]).then_inc(indexed, 1)
                    pool.wait_ge(indexed, it + 2)
                    gather(it + 1, 1 - par)
                    pool.wait_ge(y_copied, it + 2)
                    pool.sem_inc(carried, 1)
                    pool.indirect_dma_start(out=io.y_rows, out_offset=bass.IndirectOffsetOnAxis(ap=index[:, par, 1:2].bitcast(U32), axis=0),
                                            in_=y_out[:, par, :], in_offset=None).then_inc(y_stored, 16)
                    pool.wait_ge(y_stored, it * 16 + 16)
                    pool.sem_inc(y_free, 1)

                it_sum = lambda it, par: (it - par) * 8 + 16
                pool.sem_inc(y_free, 2)
                pool.tensor_copy(index[:, 0:1, :], sb.tok[:, 0:1, :]).then_inc(indexed, 1)
                pool.wait_ge(indexed, 1)
                gather(0, 0)
                n = items(pool, run)
                pool.wait_ge(y_stored, n * 16 + 16 * E)

            @block.tensor
            def _(pe):
                def turn_x(it, par):
                    pe.wait_ge(x_in[par], (it - par) * 8 + 16)
                    for h in range(2):
                        for k in range(4):
                            mm = pe.transpose(banks[:, 6 + h, k * P:(k + 1) * P], x_raw[:, par, (4 * h + k) * P:(4 * h + k + 1) * P], K[:, K_ID:K_ID + P])
                        mm.then_inc(xT_ready, 1)

                def turn_h(it, h):
                    pe.wait_ge(hid_ready, it * 2 + h + 2)
                    pe.wait_ge(xT_out, it * 2 + 4)
                    for k in range(4):
                        mm = pe.transpose(banks[:, 6 + h, k * P:(k + 1) * P], hid[:, (4 * h + k) * P:(4 * h + k + 1) * P], K[:, K_ID:K_ID + P])
                    mm.then_inc(hT_ready, 1)

                def run(it, par, _):
                    pe.wait_ge(b_in[par], (it - par) * 16 + 32)
                    pe.wait_ge(xT_out, it * 2 + 2)
                    for h in range(2):
                        pe.wait_ge(gu_read, it * 2 + h + 1)
                        for s in range(4):
                            pe.wait_ge(w_in_[4 * h + s], it * 16 + 16)
                            for j in range(2):
                                for c in range(2):
                                    mm = pe.matmul(banks[:, 2 * h + c, :], xT[:, par, 2 * s + j, :], w[:, 4 * h + s, j, c * 512:(c + 1) * 512],
                                                   start=(s == 0 and j == 0), stop=False)
                            mm.then_inc(w_used, 1)
                        for c in range(2):
                            at = h * HALF + c * 512
                            mm = pe.matmul(banks[:, 2 * h + c, :], K[0:1, K_ONE:K_ONE + P], b_gu[:, par, at:at + 512], start=False, stop=True)
                        mm.then_inc(gu_ready, 1)
                    turn_x(it + 1, 1 - par)
                    turn_h(it, 0)
                    pe.wait_ge(y_copied, it + 1)
                    for k in range(KD):
                        if k == 3:
                            turn_h(it, 1)
                        if k % 4 == 0:
                            pe.wait_ge(hT_out, it * 2 + k // 4 + 1)
                        if k % 2 == 0:
                            pe.wait_ge(w_in_[8 + k // 2], it * 16 + 16)
                        for c in range(2):
                            mm = pe.matmul(banks[:, 4 + c, :], hidT[:, k, :], w[:, 8 + k // 2, k % 2, c * 512:(c + 1) * 512], start=(k == 0), stop=False)
                        if k % 2 == 1:
                            mm.then_inc(w_used, 1)
                    for c in range(2):
                        mm = pe.matmul(banks[:, 4 + c, :], K[0:1, K_ONE:K_ONE + P], b_dn[:, par, c * 512:(c + 1) * 512], start=False, stop=True)
                    mm.then_inc(y_ready, 1)

                pe.sem_inc(w_used, NW)
                pe.sem_inc(xT_ready, 2)
                pe.sem_inc(hT_ready, 1)
                turn_x(0, 0)
                items(pe, run)

            @block.scalar
            def _(act):
                def copy_x(it, par):
                    for h in range(2):
                        act.wait_ge(xT_ready, it * 2 + h + 3)
                        act.activation(xT[:, par, 4 * h:4 * h + 4, :], banks[:, 6 + h, :].rearrange("p (k n) -> p k n", k=4), ACT.Copy).then_inc(xT_out, 1)

                def run(it, par, _):
                    for h in range(2):
                        act.wait_ge(clamped, it * 2 + h + 1)
                        act.activation(sg[:], g_c[:], ACT.Sigmoid, scale=SW_ALPHA).then_inc(sig_out, 1)
                    copy_x(it + 1, 1 - par)
                    for h in range(2):
                        act.wait_ge(hT_ready, it * 2 + h + 2)
                        act.activation(hidT[:, 4 * h:4 * h + 4, :], banks[:, 6 + h, :].rearrange("p (k n) -> p k n", k=4), ACT.Copy).then_inc(hT_out, 1)
                    act.wait_ge(y_ready, it + 1)
                    act.wait_ge(y_free, it + 1)
                    act.activation(y_out[:, par, :], banks[:, 4:6, :].rearrange("p c n -> p (c n)"), ACT.Copy).then_inc(y_copied, 1)

                act.sem_inc(y_copied, 1)
                copy_x(0, 0)
                items(act, run)

            @block.vector
            def _(dve):
                def run(it, par, _):
                    for h in range(2):
                        pair = banks[:, 2 * h:2 * h + 2, :].rearrange("p c (f t) -> p c f t", t=2)
                        two = lambda t: t.rearrange("p (c f) -> p c f", c=2)
                        dve.wait_ge(gu_ready, it * 2 + h + 1)
                        dve.wait_ge(hid_ready, it * 2 + h + 1)
                        dve.tensor_scalar(two(g_c[:]), pair[:, :, :, 0], SW_LIMIT, None, ALU.min).then_inc(clamped, 1)
                        dve.tensor_scalar(two(u_c[:]), pair[:, :, :, 1], SW_LIMIT, -SW_LIMIT, ALU.min, ALU.max).then_inc(gu_read, 1)
                        dve.wait_ge(gu_read, it * 2 + h + 3)
                        dve.scalar_tensor_tensor(out=prod[:], in0=u_c[:], scalar=1.0, in1=g_c[:], op0=ALU.add, op1=ALU.mult).then_inc(multiplied, 1)
                        dve.wait_ge(multiplied, it * 2 + h + 1)
                        dve.wait_ge(sig_out, it * 2 + h + 1)
                        dve.wait_ge(hT_ready, it * 2 + 1)
                        dve.tensor_tensor(hid[:, h * 512:(h + 1) * 512], prod[:], sg[:], ALU.mult).then_inc(hid_ready, 1)

                dve.sem_inc(gu_read, 2)
                dve.sem_inc(hid_ready, 1)
                items(dve, run)


def stage_combine(nc, io, sb):
    with ExitStack() as ctx:
        sem = ctx.enter_context(signals(nc, "combine"))
        buf = lambda n, s: ctx.enter_context(nc.sbuf_tensor(n, s, F32))
        rows = buf("rows10", [P, 3, TOPK, D])
        g_b, b_b = buf("g2_b", [P, D]), buf("b2_b", [P, D])
        stats = buf("stats10", [P, 2, 6])
        mv = buf("mv10", [P, NT, 2])
        row_in = [sem(f"row_in{i}") for i in range(3)]
        gb_in, summed, stat, mean, rooted, inverse, normed, scaled, done, stored, added = (sem(n) for n in (
            "gb_in", "summed", "stat", "mean", "rooted", "inverse", "normed", "scaled", "done", "stored", "added"))
        h = sb.h

        with nc.Block() as block:
            @block.sync
            def _(sp):
                def load(i):
                    src = io.y_rows[TOPK * P * i:TOPK * (P * i + ROWS[i]), :].rearrange("(t k) d -> t k d", k=TOPK)
                    sp.dma_start(rows[0:ROWS[i], i % 3], src).then_inc(row_in[i % 3], 16)

                for i in range(3):
                    load(i)
                sp.dma_start(g_b[:], io.g2.broadcast_to((P, D))).then_inc(gb_in, 16)
                sp.dma_start(b_b[:], io.b2.broadcast_to((P, D))).then_inc(gb_in, 16)
                for i in range(NT):
                    if i + 3 < NT:
                        sp.wait_ge(summed, i + 1)
                        load(i + 3)
                    sp.wait_ge(done, i + 1)
                    sp.dma_start(token_dram(io.o_yp, io.o_ys, i), h[0:ROWS[i], i, :]).then_inc(stored, 16)
                sp.wait_ge(stored, 16 * NT)

            @block.scalar
            def _(act):
                for i in range(NT):
                    n = ROWS[i]
                    act.wait_ge(mean, 2 * i + 2)
                    act.activation(mv[0:n, i, 1:2], mv[0:n, i, 1:2], ACT.Sqrt).then_inc(rooted, 1)

            @block.vector
            def _(dve):
                for i in range(NT):
                    n = ROWS[i]
                    x = h[0:n, i, :]
                    dve.tensor_scalar(x, x, ALPHA, None, ALU.mult).then_inc(added, 1)
                    dve.wait_ge(row_in[i % 3], 16 * (i // 3 + 1))
                    for k in range(TOPK):
                        dve.wait_ge(added, TOPK * i + k + 1)
                        dve.scalar_tensor_tensor(out=x, in0=rows[0:n, i % 3, k, :], scalar=sb.gate[0:n, i, k:k + 1], in1=x,
                                                 op0=ALU.mult, op1=ALU.add).then_inc(added if k < TOPK - 1 else summed, 1)
                    dve.wait_ge(summed, i + 1)
                    for c in range(2):
                        ins = dve.bn_stats(stats[0:n, c, :], h[0:n, i, c * 512:(c + 1) * 512])
                    ins.then_inc(stat, 1)
                    dve.wait_ge(stat, i + 1)
                    dve.bn_aggr(mv[0:n, i, :], stats[0:n].rearrange("p c s -> p (c s)")).then_inc(mean, 1)
                    dve.wait_ge(mean, 2 * i + 1)
                    dve.tensor_scalar(mv[0:n, i, 1:2], mv[0:n, i, 1:2], LN_EPS, None, ALU.add).then_inc(mean, 1)
                    dve.wait_ge(rooted, i + 1)
                    dve.reciprocal(mv[0:n, i, 1:2], mv[0:n, i, 1:2]).then_inc(inverse, 1)
                    dve.wait_ge(inverse, i + 1)
                    if i == 0:
                        dve.wait_ge(gb_in, 32)
                    dve.tensor_scalar(x, x, mv[0:n, i, 0:1], mv[0:n, i, 1:2], ALU.subtract, ALU.mult).then_inc(normed, 1)
                    dve.wait_ge(normed, i + 1)
                    dve.tensor_tensor(x, x, g_b[0:n], ALU.mult).then_inc(scaled, 1)
                    dve.wait_ge(scaled, i + 1)
                    dve.tensor_tensor(x, x, b_b[0:n], ALU.add).then_inc(done, 1)


class Tensors:
    pass


def program(nc, io):
    with ExitStack() as ctx:
        buf = lambda n, s: ctx.enter_context(nc.sbuf_tensor(n, s, F32))
        sb = Tensors()
        sb.const, sb.xT, sb.dt = buf("const", [P, K_W]), buf("xT", [P, KD, T]), buf("dt", [P, NT, SH])
        sb.mergedT = buf("mergedT", [P, KD, T])
        with ExitStack() as att:
            abuf = lambda n, s: att.enter_context(nc.sbuf_tensor(n, s, F32))
            sb.cT = abuf("cT", [P, 2, T])
            sb.krT = abuf("krT", [ROPE, T])
            sb.oT = abuf("oT", [P, HEADS, T])
            sb.wkv = abuf("wkv", [P, 2, HEADS * (NOPE + VH)])
            sb.qlS = abuf("qlS", [P, 2, HEADS, NS])
            sb.qrS = abuf("qrS", [ROPE, HEADS, NS])
            with ExitStack() as own:
                obuf = lambda n, s: own.enter_context(nc.sbuf_tensor(n, s, F32))
                sb.rope = obuf("rope", [P, 2, NT, ROPE // 2])
                sb.c_tok = obuf("c_tok", [P, NT, KVL])
                sb.kr_tok = obuf("kr_tok", [P, NT, ROPE])
                sb.qnT = obuf("qnT", [P, 2, T])
                stage_latents(nc, io, sb)
                stage_prompt_attention(nc, io, sb)
            stage_sample_attention(nc, io, sb)
            stage_turn_x(nc, io, sb)
            stage_merge(nc, io, sb, C_GB, io.wb, lambda k: sb.oT[:, k, :], HEADS, True, "_b")
        with ExitStack() as scan:
            sb.xbcT = scan.enter_context(nc.sbuf_tensor("xbcT", [P, NCT, T], F32))
            sb.yT = sb.xbcT[:, 0:DI // P, :]
            stage_conv(nc, io, sb)
            stage_ssd(nc, io, sb)
            stage_merge(nc, io, sb, C_GA, io.wa, lambda k: sb.yT[:, k, :], DI // P, False, "_a")
        with ExitStack() as moe:
            mbuf = lambda n, s, d=F32: moe.enter_context(nc.sbuf_tensor(n, s, d))
            sb.h = mbuf("h", [P, NT, D])
            sb.gate = mbuf("gate", [P, NT, TOPK])
            sb.slot = mbuf("slot", [P, NT, TOPK], I32)
            sb.tok = mbuf("tok", [P, ITEMS + 2, 2], I32)
            sb.item_expert = mbuf("item_expert", [1, NOVF + 1], I32)
            sb.item_slot = mbuf("item_slot", [1, NOVF + 1], I32)
            sb.n_over = mbuf("n_over", [1, 1], I32)
            stage_out(nc, io, sb)
            stage_route(nc, io, sb)
            stage_experts(nc, io, sb)
            stage_combine(nc, io, sb)


_INS = {'x_prompt': None, 'x_sample': None, 'cache_kv_latent': None, 'cache_k_rope': None, 'state_ssm': None,
        'state_conv': None, 'page_table': None, 'w_in': None, 'ssd_conv_w': None, 'ssd_conv_b': None,
        'ssd_dt_bias': None, 'ssd_a_log': None, 'ssd_d': None, 'ssd_norm_g': None, 'mla_q_norm_g': None,
        'w_q_b': None, 'mla_kv_norm_g': None, 'w_kv_b': None, 'w_branch_a': None, 'w_branch_b': None,
        'w_out': None, 'ln1_g': None, 'ln1_b': None, 'router_w': None, 'router_b': None, 'exp_w_gu': None,
        'exp_b_gu': None, 'exp_w_down': None, 'exp_b_down': None, 'ln2_g': None, 'ln2_b': None}
_OUTS = [(1, SEQ, D), (NSEQ, TS, D), (1, 1, SEQ, KVL), (1, 1, SEQ, ROPE), (1, 1, SH, PD, NST), (1, 1, KC - 1, CONV),
         (1, NSEQ, TS, KVL), (1, NSEQ, TS, ROPE), (1, NSEQ, SH, PD, NST), (1, NSEQ, KC - 1, CONV)]


def io_of(nc, ins, outs):
    scratch = lambda n, s, d=F32: nc.dram_tensor(n, s, d).ap()
    i = ins
    io = Tensors()
    io.xp = i['x_prompt'][0]
    io.xs = i['x_sample'].rearrange("b t d -> (b t) d")
    io.cache_c = i['cache_kv_latent'][0]
    io.cache_r = i['cache_k_rope'][0]
    io.ssm = i['state_ssm'][0].rearrange("b h p n -> b (h p) n")
    io.conv = i['state_conv'][0].rearrange("b k c -> (b k) c")
    io.pages = i['page_table']
    io.w_in = i['w_in'][0]
    io.conv_w = i['ssd_conv_w'][0]
    io.conv_b = i['ssd_conv_b']
    io.dt_bias = i['ssd_dt_bias']
    io.a_log = i['ssd_a_log']
    io.d_skip = i['ssd_d']
    io.gn = i['ssd_norm_g']
    io.gq = i['mla_q_norm_g']
    io.wq = i['w_q_b'][0]
    io.gkv = i['mla_kv_norm_g']
    io.wkv = i['w_kv_b'][0]
    io.wa = i['w_branch_a'][0]
    io.wb = i['w_branch_b'][0]
    io.wo = i['w_out'][0]
    io.g1 = i['ln1_g']
    io.b1 = i['ln1_b']
    io.wr = i['router_w'][0]
    io.br = i['router_b']
    io.wgu = i['exp_w_gu'][0]
    io.bgu = i['exp_b_gu'][0]
    io.wdn = i['exp_w_down'][0]
    io.bdn = i['exp_b_down'][0]
    io.g2 = i['ln2_g']
    io.b2 = i['ln2_b']
    io.consts = i['consts']
    io.rope = i['rope']
    io.o_yp = outs[0][0]
    io.o_ys = outs[1].rearrange("b t d -> (b t) d")
    io.o_cp = outs[2][0, 0]
    io.o_krp = outs[3][0, 0]
    io.o_ssmp = outs[4][0, 0].rearrange("h p n -> (h p) n")
    io.o_convp = outs[5][0, 0]
    io.o_cs = outs[6][0].rearrange("b t d -> (b t) d")
    io.o_krs = outs[7][0].rearrange("b t d -> (b t) d")
    io.o_ssms = outs[8][0].rearrange("b h p n -> b (h p) n")
    io.o_convs = outs[9][0].rearrange("b k c -> (b k) c")
    io.h_rows = scratch("h_rows", (T, D))
    io.slots = scratch("slots", (E * CAP, 2), I32)
    io.y_rows = scratch("y_rows", (T * TOPK + 1, D))
    return io


def kernel(**inputs):
    import concourse.bacc as _bacc
    from concourse.bass_utils import run_bass_kernel_spmd as _run

    nc = _bacc.Bacc("TRN2", target_bir_lowering=False, num_devices=1)
    arrays, ins = {}, {}
    given = {name: np.ascontiguousarray(inputs[name]) for name in _INS}
    given['consts'], given['rope'] = constants(), rope_tables()
    for name, a in given.items():
        arrays[f"in_{name}"] = a
        ins[name] = nc.dram_tensor(f"in_{name}", a.shape, mybir.dt.from_np(a.dtype), kind="ExternalInput").ap()
    outs = [nc.dram_tensor(f"out_{i}", s, F32, kind="ExternalOutput").ap() for i, s in enumerate(_OUTS)]
    program(nc, io_of(nc, ins, outs))
    r = _run(nc, [arrays], core_ids=[0])
    return tuple(r.results[0][f"out_{i}"] for i in range(len(_OUTS)))
```

```python
from contextlib import ExitStack, contextmanager

import numpy as np

import concourse.bass as bass
from concourse import mybir

F32 = mybir.dt.float32
F32R = mybir.dt.float32r
I32 = mybir.dt.int32
U32 = mybir.dt.uint32
ALU = mybir.AluOpType
ACT = mybir.ActivationFunctionType
AX = mybir.AxisListType.X

P = 128
D = 1024
SEQ = 512
NSEQ, TS = 8, 8
NS = NSEQ * TS
T = SEQ + NS
NT = 5
ROWS = [P, P, P, P, NS]
KD = D // P
PAST, PAGE = 4096, 128
NPAGE = PAST // PAGE
NPHYS = 320
HEADS, NOPE, ROPE, VH = 8, 128, 64, 128
QL = KVL = 256
QH = NOPE + ROPE
DI = 2048
G, HG, PD, NST = 4, 8, 64, 128
SH = G * HG
GW = HG * PD
CONV = DI + 2 * G * NST
KC = 4
NCT = CONV // P
FF = 1024
E = 32
TOPK = 4
CAP = 640
ITEMS = E + (T * TOPK - 1) // P
NOVF = ITEMS - E
ATT_SCALE = (NOPE + ROPE) ** -0.5
ALPHA = 2 ** 0.25
LN_EPS, RMS_EPS = 1e-5, 1e-6
SW_ALPHA, SW_LIMIT = 1.702, 7.0
MASKED = -1e30
H2 = T // 2

C_Q, C_KV, C_KR, C_Z = 0, QL, QL + KVL, QL + KVL + ROPE
C_X = C_Z + DI
C_DT = C_X + CONV
C_GA = C_DT + SH
C_GB = C_GA + D
C_ALL = C_GB + D

K_ID = 0
K_TRI = K_ID + P
K_STRICT = K_TRI + P
K_ONE = K_STRICT + P
K_CAUS = K_ONE + P
K_BTRI = K_CAUS + P
K_BALL = K_BTRI + NS
K_BEND = K_BALL + NS
K_BROW = K_BEND + NSEQ
K_BCOL = K_BROW + NSEQ
K_NEW = K_BCOL + NSEQ * NS
K_PAIR = K_NEW + TS
K_BASE = K_PAIR + 2 * (NT * TOPK + 1)
K_CODE = K_BASE + E
K_ITEM = K_CODE + 4 * E
K_EXP = K_ITEM + NOVF + 1
K_PICK = K_EXP + 4 * E
K_W = K_PICK + 6


def constants():
    c = np.zeros((P, K_W), np.float32)
    r = np.arange(P)[:, None]
    q = np.arange(P)[None, :]
    c[:, K_ID:K_ID + P] = r == q
    c[:, K_TRI:K_TRI + P] = r <= q
    c[:, K_STRICT:K_STRICT + P] = r < q
    c[:, K_ONE:K_ONE + P] = 1
    c[:, K_CAUS:K_CAUS + P] = np.where(q <= r, 0, MASKED)
    l = np.arange(NS)
    same = l[:, None] // TS == l[None, :] // TS
    c[:NS, K_BTRI:K_BTRI + NS] = same & (l[:, None] <= l[None, :])
    c[:NS, K_BALL:K_BALL + NS] = same
    s = np.arange(NSEQ)
    c[:NS, K_BEND:K_BEND + NSEQ] = l[:, None] == s[None, :] * TS + TS - 1
    c[:NS, K_BROW:K_BROW + NSEQ] = l[:, None] // TS == s[None, :]
    c[:, K_BCOL:K_BCOL + NSEQ * NS] = (s[:, None] == l[None, :] // TS).reshape(1, -1)
    t = np.arange(TS)
    c[:HEADS * TS, K_NEW:K_NEW + TS] = np.where(t[None, :] <= np.tile(t, HEADS)[:, None], 0, MASKED)
    pair = np.zeros((P, NT * TOPK + 1, 2))
    token = np.repeat(r + P * np.arange(NT)[None, :], TOPK, axis=1)
    pair[:, :-1, 0] = token
    pair[:, :-1, 1] = token * TOPK + np.tile(np.arange(TOPK), NT)[None, :]
    pair[:, -1, 1] = T * TOPK
    c[:, K_PAIR:K_BASE] = pair.reshape(P, -1)
    c[:, K_BASE:K_BASE + E] = CAP * np.arange(E)
    c[0, K_CODE:K_CODE + 4 * E] = (CAP * np.arange(E)[None, :] + P * np.arange(1, 5)[:, None]).reshape(-1)
    c[0, K_ITEM:K_ITEM + NOVF + 1] = np.arange(1, NOVF + 2)
    c[0, K_EXP:K_EXP + 4 * E] = np.tile(np.arange(E), 4)
    for j in range(6):
        c[[j, 32 + j], K_PICK + j] = 1
    return c


def rope_tables():
    half = ROPE // 2
    inv = np.float32(10000.0) ** (-np.arange(half, dtype=np.float32) / np.float32(half))
    pos = np.concatenate([np.arange(SEQ), np.tile(PAST + np.arange(TS), NSEQ)]).astype(np.float32)
    ang = np.zeros((NT * P, half), np.float32)
    ang[:T] = pos[:, None] * inv[None, :]
    both = np.stack([np.cos(ang), np.sin(ang)]).astype(np.float32)
    return np.ascontiguousarray(both.reshape(2, NT, P, half).transpose(2, 0, 1, 3))


@contextmanager
def signals(nc, stage):
    made = []

    def make(name):
        made.append(nc.alloc_semaphore(f"{stage}_{name}"))
        return made[-1]

    yield make
    nc.clear_and_free_semaphores(made)
    nc.all_engine_barrier()


def token_dram(prompt, sample, i):
    return prompt[P * i:P * (i + 1), :] if i < NT - 1 else sample


def stage_latents(nc, io, sb):
    with ExitStack() as ctx:
        sem = ctx.enter_context(signals(nc, "latents"))
        buf = lambda n, s: ctx.enter_context(nc.sbuf_tensor(n, s, F32))
        x_tok = buf("x_tok", [P, NT, D])
        w_lat = buf("w_lat", [P, KD, C_Z])
        w_dt = buf("w_dt", [P, KD, SH])
        lat = buf("lat", [P, NT, C_Z])
        qn = buf("qn", [P, NT, QL])
        gq = buf("gq", [P, QL])
        gkv = buf("gkv", [P, KVL])
        junk = buf("junk", [P, QL])
        ssq = buf("ssq", [P, 2, NT])
        rt = [buf(f"rt{i}", [P, NT, ROPE // 2]) for i in range(4)]
        banks = ctx.enter_context(nc.psum_tensor("banks", [P, 8, 512], F32))
        const_in, w_in_, g_in = sem("const_in"), sem("w_in_"), sem("g_in")
        x_in = [sem(f"x_in{i}") for i in range(NT)]
        turned, turned_out = sem("turned"), sem("turned_out")
        lat_ready, lat_out = sem("lat_ready"), sem("lat_out")
        zeroed, squared, rooted, vec = sem("zeroed"), sem("squared"), sem("rooted"), sem("vec")
        lat_done, lat_turned, stored = sem("lat_done"), sem("lat_turned"), sem("stored")
        K = sb.const
        w_view = io.w_in.rearrange("(k p) n -> p k n", p=P)

        with nc.Block() as block:
            @block.sync
            def _(sp):
                sp.dma_start(K[:], io.consts).then_inc(const_in, 16)
                for i in range(NT):
                    sp.dma_start(x_tok[0:ROWS[i], i, :], token_dram(io.xp, io.xs, i)).then_inc(x_in[i], 16)
                sp.dma_start(w_lat[:], w_view[:, :, 0:C_Z]).then_inc(w_in_, 16)
                sp.dma_start(w_dt[:], w_view[:, :, C_DT:C_GA]).then_inc(w_in_, 16)
                sp.dma_start(sb.rope[:], io.rope).then_inc(g_in, 16)
                sp.dma_start(gq[:], io.gq.broadcast_to((P, QL))).then_inc(g_in, 16)
                sp.dma_start(gkv[:], io.gkv.broadcast_to((P, KVL))).then_inc(g_in, 16)
                sp.wait_ge(lat_done, 2)
                for i in range(NT):
                    sp.dma_start(token_dram(io.o_cp, io.o_cs, i), sb.c_tok[0:ROWS[i], i, :]).then_inc(stored, 16)
                    sp.dma_start(token_dram(io.o_krp, io.o_krs, i), sb.kr_tok[0:ROWS[i], i, :]).then_inc(stored, 16)
                sp.wait_ge(stored, 16 * 2 * NT)

            @block.gpsimd
            def _(pool):
                pool.memset(lat[NS:P, NT - 1, :], 0.0).then_inc(zeroed, 1)
                pool.memset(sb.dt[NS:P, NT - 1, :], 0.0).then_inc(zeroed, 1)

            @block.tensor
            def _(pe):
                pe.wait_ge(const_in, 16)
                for i in range(NT):
                    n = ROWS[i]
                    pe.wait_ge(x_in[i], 16)
                    for h in range(2):
                        u = 2 * i + h
                        if u >= 4:
                            pe.wait_ge(turned_out, u - 3)
                        for k in range(4):
                            mm = pe.transpose(banks[:, u % 4, k * n:(k + 1) * n],
                                              x_tok[0:n, i, (4 * h + k) * P:(4 * h + k + 1) * P], K[0:n, K_ID:K_ID + n])
                        mm.then_inc(turned, 1)
                pe.wait_ge(w_in_, 32)
                pe.wait_ge(turned_out, 2 * NT)
                for i in range(NT):
                    n, b = ROWS[i], 4 + 2 * (i % 2)
                    if i >= 2:
                        pe.wait_ge(lat_out, i - 1)
                    xs = [sb.xT[:, k, P * i:P * i + n] for k in range(KD)]
                    for k in range(KD):
                        pe.matmul(banks[0:n, b, :], xs[k], w_lat[:, k, 0:512], start=(k == 0), stop=(k == KD - 1))
                    for k in range(KD):
                        pe.matmul(banks[0:n, b + 1, 0:ROPE], xs[k], w_lat[:, k, 512:C_Z], start=(k == 0), stop=(k == KD - 1))
                    for k in range(KD):
                        mm = pe.matmul(banks[0:n, b + 1, ROPE:ROPE + SH], xs[k], w_dt[:, k, :], start=(k == 0), stop=(k == KD - 1))
                    mm.then_inc(lat_ready, 1)
                pe.wait_ge(lat_done, 3)
                for i in range(NT):
                    n = ROWS[i]
                    if i >= 4:
                        pe.wait_ge(lat_turned, i - 3)
                    for c in range(2):
                        pe.transpose(banks[:, i % 4, c * n:(c + 1) * n], qn[0:n, i, c * P:(c + 1) * P], K[0:n, K_ID:K_ID + n])
                    for c in range(2):
                        pe.transpose(banks[:, 4 + i % 4, c * n:(c + 1) * n], sb.c_tok[0:n, i, c * P:(c + 1) * P], K[0:n, K_ID:K_ID + n])
                    pe.transpose(banks[0:ROPE, 4 + i % 4, 2 * n:3 * n], sb.kr_tok[0:n, i, :], K[0:n, K_ID:K_ID + n]).then_inc(turned, 1)

            @block.scalar
            def _(act):
                for i in range(NT):
                    n, b = ROWS[i], 4 + 2 * (i % 2)
                    act.wait_ge(lat_ready, i + 1)
                    act.activation(lat[0:n, i, 0:512], banks[0:n, b, :], ACT.Copy)
                    act.activation(lat[0:n, i, 512:C_Z], banks[0:n, b + 1, 0:ROPE], ACT.Copy)
                    act.activation(sb.dt[0:n, i, :], banks[0:n, b + 1, ROPE:ROPE + SH], ACT.Copy).then_inc(lat_out, 1)
                act.wait_ge(zeroed, 2)
                act.wait_ge(lat_out, NT)
                for j in range(2):
                    for i in range(NT):
                        if j or i:
                            act.wait_ge(squared, j * NT + i)
                        act.activation(junk[:], lat[:, i, j * QL:(j + 1) * QL], ACT.Square,
                                       accum_out=ssq[:, j, i:i + 1]).then_inc(squared, 1)
                act.wait_ge(vec, 1)
                act.activation(ssq[:], ssq[:], ACT.Sqrt).then_inc(rooted, 1)

            @block.vector
            def _(dve):
                for u in range(2 * NT):
                    i, h = divmod(u, 2)
                    n = ROWS[i]
                    dve.wait_ge(turned, u + 1)
                    dve.tensor_copy(sb.xT[:, 4 * h:4 * h + 4, P * i:P * i + n],
                                    banks[:, u % 4, 0:4 * n].rearrange("p (k n) -> p k n", k=4)).then_inc(turned_out, 1)
                dve.wait_ge(squared, 2 * NT)
                dve.tensor_scalar(ssq[:], ssq[:], 1.0 / QL, RMS_EPS, ALU.mult, ALU.add).then_inc(vec, 1)
                dve.wait_ge(g_in, 48)
                c, s = sb.rope[:, 0], sb.rope[:, 1]
                half = ROPE // 2
                k1, k2 = lat[:, :, 512:512 + half], lat[:, :, 512 + half:C_Z]
                for o, a, b in ((0, k1, c), (1, k2, s), (2, k2, c), (3, k1, s)):
                    ins = dve.tensor_tensor(rt[o][:], a, b, ALU.mult)
                ins.then_inc(vec, 1)
                dve.wait_ge(vec, 2)
                dve.tensor_tensor(sb.kr_tok[:, :, 0:half], rt[0][:], rt[1][:], ALU.subtract)
                dve.tensor_tensor(sb.kr_tok[:, :, half:ROPE], rt[2][:], rt[3][:], ALU.add).then_inc(lat_done, 1)
                dve.wait_ge(rooted, 1)
                dve.reciprocal(ssq[:], ssq[:]).then_inc(vec, 1)
                dve.wait_ge(vec, 3)
                for i in range(NT):
                    ins = dve.scalar_tensor_tensor(out=sb.c_tok[:, i, :], in0=lat[:, i, QL:QL + KVL], scalar=ssq[:, 1, i:i + 1],
                                                   in1=gkv[:], op0=ALU.mult, op1=ALU.mult)
                ins.then_inc(lat_done, 1)
                for i in range(NT):
                    ins = dve.scalar_tensor_tensor(out=qn[:, i, :], in0=lat[:, i, 0:QL], scalar=ssq[:, 0, i:i + 1],
                                                   in1=gq[:], op0=ALU.mult, op1=ALU.mult)
                ins.then_inc(lat_done, 1)
                for i in range(NT):
                    n = ROWS[i]
                    dve.wait_ge(turned, 2 * NT + i + 1)
                    dve.tensor_copy(sb.qnT[:, :, P * i:P * i + n], banks[:, i % 4, 0:2 * n].rearrange("p (c n) -> p c n", c=2))
                    dve.tensor_copy(sb.cT[:, :, P * i:P * i + n], banks[:, 4 + i % 4, 0:2 * n].rearrange("p (c n) -> p c n", c=2))
                    dve.tensor_copy(sb.krT[:, P * i:P * i + n], banks[0:ROPE, 4 + i % 4, 2 * n:3 * n]).then_inc(lat_turned, 1)


def stage_prompt_attention(nc, io, sb):
    with ExitStack() as ctx:
        sem = ctx.enter_context(signals(nc, "prompt_attention"))
        buf = lambda n, s: ctx.enter_context(nc.sbuf_tensor(n, s, F32))
        wq = buf("wq", [P, 2, HEADS * QH])
        wkT = buf("wkT", [P, HEADS, KVL])
        q_rot = buf("q_rot", [P, NT, HEADS, ROPE])
        rt = [buf(f"qrt{i}", [P, HEADS, ROPE // 2]) for i in range(4)]
        qn_h = buf("qn_h", [P, T])
        ql_h = buf("ql_h", [P, 2, 2, SEQ])
        qr_h = buf("qr_h", [ROPE, 2, SEQ])
        prob = buf("prob", [P, 2, SEQ])
        probT = buf("probT", [P, 2, 4, P])
        olT = buf("olT", [P, 2, 2, P])
        mx = buf("mx", [P, 2])
        neg = buf("neg", [P, 2])
        den = buf("den", [P, 2])
        banks = ctx.enter_context(nc.psum_tensor("banks2", [P, 8, 512], F32))
        K = sb.const
        wq_in, wkv_in = sem("wq_in"), sem("wkv_in")
        wk_ready, wk_out, rot_ready, rot_out, rot_vec = sem("wk_ready"), sem("wk_out"), sem("rot_ready"), sem("rot_out"), sem("rot_vec")
        prep_ready, prep_out = sem("prep_ready"), sem("prep_out")
        scored, maxed, vec, expd, normed = sem("scored"), sem("maxed"), sem("vec2"), sem("expd"), sem("normed")
        pt_ready, pt_out, pv_ready, pv_out, o_ready, o_out = (sem(n) for n in ("pt_ready", "pt_out", "pv_ready", "pv_out", "o_ready", "o_out"))
        wq_rot = wq[:].rearrange("p k (h d) -> p k h d", h=HEADS)[:, :, :, NOPE:QH]
        n_steps = HEADS * 4
        step = lambda i: divmod(i, 4)

        with nc.Block() as block:
            @block.sync
            def _(sp):
                sp.dma_start(wq[:], io.wq.rearrange("(k p) n -> p k n", p=P)).then_inc(wq_in, 16)
                sp.dma_start(sb.wkv[:], io.wkv.rearrange("(k p) n -> p k n", p=P)).then_inc(wkv_in, 16)

            @block.tensor
            def _(pe):
                pe.wait_ge(wq_in, 16)
                for i in range(NT):
                    n = ROWS[i]
                    if i >= 2:
                        pe.wait_ge(rot_out, i - 1)
                    for k in range(2):
                        mm = pe.matmul(banks[0:n, i % 2, :], sb.qnT[:, k, P * i:P * i + n], wq_rot[:, k], start=(k == 0), stop=(k == 1))
                    mm.then_inc(rot_ready, 1)
                pe.wait_ge(wkv_in, 16)
                for u in range(4):
                    for v in range(4):
                        h, r = 2 * u + v // 2, v % 2
                        mm = pe.transpose(banks[:, 2 + u, v * P:(v + 1) * P], sb.wkv[:, r, h * 256:h * 256 + NOPE], K[:, K_ID:K_ID + P])
                    mm.then_inc(wk_ready, 1)

                def prep(h, part):
                    m = 4 * h + part
                    if m >= 1:
                        pe.wait_ge(prep_out, m)
                    if part == 0:
                        for piece, b in ((0, 0), (1, 1)):
                            for k in range(2):
                                mm = pe.matmul(banks[:, b, 0:H2], wq[:, k, h * QH:h * QH + NOPE],
                                               sb.qnT[:, k, piece * H2:(piece + 1) * H2], start=(k == 0), stop=(k == 1))
                    elif part < 3:
                        r = part - 1
                        for piece in range(2):
                            mm = pe.matmul(banks[:, piece, 0:H2], wkT[:, h, r * P:(r + 1) * P],
                                           qn_h[:, piece * H2:(piece + 1) * H2], start=True, stop=True)
                    else:
                        for i in range(NT):
                            n = ROWS[i]
                            o = banks[0:ROPE, 0, P * i:P * i + n] if i < 4 else banks[0:ROPE, 1, 0:n]
                            mm = pe.transpose(o, q_rot[0:n, i, h, :], K[0:n, K_ID:K_ID + n])
                    mm.then_inc(prep_ready, 1)

                pe.wait_ge(rot_out, NT)
                pe.wait_ge(wk_out, 4)
                for part in range(4):
                    prep(0, part)
                for i in range(n_steps + 3):
                    if i < n_steps:
                        h, q = step(i)
                        pe.wait_ge(prep_out, 4 * h + 4)
                        if i >= 2:
                            pe.wait_ge(expd, i - 1)
                        n = (q + 1) * P
                        o = banks[:, 2 + i % 2, 0:n]
                        for r in range(2):
                            pe.matmul(o, ql_h[:, h % 2, r, q * P:(q + 1) * P], sb.cT[:, r, 0:n], start=(r == 0), stop=False)
                        pe.matmul(o, qr_h[:, h % 2, q * P:(q + 1) * P], sb.krT[:, 0:n], start=False, stop=True).then_inc(scored, 1)
                    if 1 <= i <= n_steps:
                        j = i - 1
                        pe.wait_ge(normed, j + 1)
                        if j >= 2:
                            pe.wait_ge(pt_out, j - 1)
                        for k in range(step(j)[1] + 1):
                            mm = pe.transpose(banks[:, 4 + 3 * (j % 2), k * P:(k + 1) * P], prob[:, j % 2, k * P:(k + 1) * P], K[:, K_ID:K_ID + P])
                        mm.then_inc(pt_ready, 1)
                    if 2 <= i <= n_steps + 1:
                        j = i - 2
                        pe.wait_ge(pt_out, j + 1)
                        if j >= 1:
                            pe.wait_ge(pv_out, j)
                        q = step(j)[1]
                        for r in range(2):
                            for k in range(q + 1):
                                mm = pe.matmul(banks[:, 5, r * P:(r + 1) * P], sb.c_tok[:, k, r * P:(r + 1) * P], probT[:, j % 2, k, :],
                                               start=(k == 0), stop=(k == q))
                        mm.then_inc(pv_ready, 1)
                    if 3 <= i:
                        j = i - 3
                        h = step(j)[0]
                        pe.wait_ge(pv_out, j + 1)
                        if j >= 1:
                            pe.wait_ge(o_out, j)
                        for r in range(2):
                            mm = pe.matmul(banks[:, 6, 0:P], sb.wkv[:, r, h * 256 + NOPE:(h + 1) * 256], olT[:, j % 2, r, :],
                                           start=(r == 0), stop=(r == 1))
                        mm.then_inc(o_ready, 1)
                    if i < n_steps and step(i)[0] + 1 < HEADS:
                        prep(step(i)[0] + 1, step(i)[1])

            @block.scalar
            def _(act):
                def prep_copy(h, part):
                    m = 4 * h + part
                    act.wait_ge(prep_ready, m + 1)
                    S1 = SEQ - H2
                    if part == 0:
                        act.activation(qn_h[:, 0:H2], banks[:, 0, 0:H2], ACT.Copy)
                        ins = act.activation(qn_h[:, H2:T], banks[:, 1, 0:H2], ACT.Copy)
                    elif part < 3:
                        r = part - 1
                        if h >= 2:
                            act.wait_ge(scored, 4 * h - 4)
                        act.activation(ql_h[:, h % 2, r, 0:H2], banks[:, 0, 0:H2], ACT.Copy)
                        act.activation(ql_h[:, h % 2, r, H2:SEQ], banks[:, 1, 0:S1], ACT.Copy)
                        ins = act.activation(sb.qlS[:, r, h, :], banks[:, 1, S1:H2], ACT.Copy)
                    else:
                        act.activation(qr_h[:, h % 2, :], banks[0:ROPE, 0, :], ACT.Copy)
                        ins = act.activation(sb.qrS[:, h, :], banks[0:ROPE, 1, 0:NS], ACT.Copy)
                    ins.then_inc(prep_out, 1)

                for part in range(4):
                    prep_copy(0, part)
                for i in range(n_steps + 1):
                    if i >= 1:
                        j = i - 1
                        n = step(j)[1] + 1
                        act.wait_ge(pt_ready, j + 1)
                        if j >= 2:
                            act.wait_ge(pv_ready, j - 1)
                        act.activation(probT[:, j % 2, 0:n, :], banks[:, 4 + 3 * (j % 2), 0:n * P].rearrange("p (k n) -> p k n", n=P),
                                       ACT.Copy).then_inc(pt_out, 1)
                    if i < n_steps:
                        h, q = step(i)
                        n = (q + 1) * P
                        act.wait_ge(maxed, i + 1)
                        if i >= 2:
                            act.wait_ge(pt_ready, i - 1)
                        act.activation(prob[:, i % 2, 0:n], banks[:, 2 + i % 2, 0:n], ACT.Exp, bias=neg[:, i % 2:i % 2 + 1],
                                       scale=ATT_SCALE, accum_out=den[:, i % 2:i % 2 + 1]).then_inc(expd, 1)
                        if h + 1 < HEADS:
                            prep_copy(h + 1, q)

            @block.vector
            def _(dve):
                half = ROPE // 2
                for i in range(NT):
                    n = ROWS[i]
                    dve.wait_ge(rot_ready, i + 1)
                    x = banks[0:n, i % 2, :].rearrange("p (h d) -> p h d", h=HEADS)
                    c = sb.rope[0:n, 0, i, :].unsqueeze(1).broadcast_to((n, HEADS, half))
                    s = sb.rope[0:n, 1, i, :].unsqueeze(1).broadcast_to((n, HEADS, half))
                    x1, x2 = x[:, :, 0:half], x[:, :, half:ROPE]
                    if i >= 1:
                        dve.wait_ge(rot_out, i)
                    for o, a, b in ((0, x1, c), (1, x2, s), (2, x2, c), (3, x1, s)):
                        ins = dve.tensor_tensor(rt[o][0:n], a, b, ALU.mult)
                    ins.then_inc(rot_vec, 1)
                    dve.wait_ge(rot_vec, i + 1)
                    dve.tensor_tensor(q_rot[0:n, i, :, 0:half], rt[0][0:n], rt[1][0:n], ALU.subtract)
                    dve.tensor_tensor(q_rot[0:n, i, :, half:ROPE], rt[2][0:n], rt[3][0:n], ALU.add).then_inc(rot_out, 1)
                for u in range(4):
                    dve.wait_ge(wk_ready, u + 1)
                    dve.tensor_copy(wkT[:, 2 * u:2 * u + 2, :], banks[:, 2 + u, :].rearrange("p (h r) -> p h r", h=2)).then_inc(wk_out, 1)
                for i in range(n_steps + 3):
                    if 1 <= i <= n_steps:
                        j = i - 1
                        n = (step(j)[1] + 1) * P
                        dve.wait_ge(expd, j + 1)
                        dve.reciprocal(den[:, j % 2:j % 2 + 1], den[:, j % 2:j % 2 + 1]).then_inc(vec, 1)
                        dve.wait_ge(vec, 3 * j + 3)
                        dve.tensor_scalar(prob[:, j % 2, 0:n], prob[:, j % 2, 0:n], den[:, j % 2:j % 2 + 1], None, ALU.mult).then_inc(normed, 1)
                    if i < n_steps:
                        q = step(i)[1]
                        dve.wait_ge(scored, i + 1)
                        diag = banks[:, 2 + i % 2, q * P:(q + 1) * P]
                        dve.tensor_tensor(diag, diag, K[:, K_CAUS:K_CAUS + P], ALU.add).then_inc(vec, 1)
                        dve.wait_ge(vec, 3 * i + 1)
                        dve.reduce_max(mx[:, i % 2:i % 2 + 1], banks[:, 2 + i % 2, 0:(q + 1) * P], AX).then_inc(vec, 1)
                        dve.wait_ge(vec, 3 * i + 2)
                        dve.tensor_scalar(neg[:, i % 2:i % 2 + 1], mx[:, i % 2:i % 2 + 1], -ATT_SCALE, None, ALU.mult).then_inc(maxed, 1)
                    if 2 <= i <= n_steps + 1:
                        j = i - 2
                        dve.wait_ge(pv_ready, j + 1)
                        if j >= 2:
                            dve.wait_ge(o_ready, j - 1)
                        dve.tensor_copy(olT[:, j % 2, :, :], banks[:, 5, 0:2 * P].rearrange("p (r n) -> p r n", r=2)).then_inc(pv_out, 1)
                    if 3 <= i:
                        j = i - 3
                        h, q = step(j)
                        dve.wait_ge(o_ready, j + 1)
                        dve.tensor_copy(sb.oT[:, h, q * P:(q + 1) * P], banks[:, 6, 0:P]).then_inc(o_out, 1)


def stage_sample_attention(nc, io, sb):
    NQ = HEADS * TS
    NKEY = PAST + TS
    NCH = 8
    with ExitStack() as ctx:
        sem = ctx.enter_context(signals(nc, "sample_attention"))
        buf = lambda n, s: ctx.enter_context(nc.sbuf_tensor(n, s, F32))
        page = ctx.enter_context(nc.sbuf_tensor("page", [1, NSEQ * NPAGE], I32))
        rows = buf("rows", [P, 2, NPAGE, KVL])
        rots = buf("rots", [P, 2, NPAGE, ROPE])
        spare = sb.mergedT[:].rearrange("p k t -> p (k t)")
        spare2 = sb.xT[:].rearrange("p k t -> p (k t)")
        keyT = spare[:, 0:3072].rearrange("p (a j n) -> p a j n", a=2, j=3)
        q_b = spare[:, 3072:3328].rearrange("p (a r n) -> p a r n", a=2, r=2)
        qr_b = spare[0:ROPE, 3328:3456].rearrange("p (a n) -> p a n", a=2)
        new_b = spare[0:TS, 3456:3968].rearrange("p (a r) -> p a r", a=2)
        score = buf("score", [NQ, 2, NKEY])
        mx = buf("mx3", [NQ, 2, NCH + 1])
        stat = buf("stat", [NQ, 2, 3])
        cT_b = spare[:, 3968:4000].rearrange("p (a r t) -> p a r t", a=2, r=2)
        krT_b = spare[0:ROPE, 4000:4016].rearrange("p (a t) -> p a t", a=2)
        probT = spare2[:, 0:NPAGE * NQ].rearrange("p (k n) -> p k n", k=NPAGE)
        probT_new = buf("probT_new", [TS, NQ])
        o_rows = spare2[0:NQ, NPAGE * NQ:NPAGE * NQ + NSEQ * KVL].rearrange("p (b r) -> p b r", b=NSEQ)
        olS = spare[:, 0:2 * HEADS * NS].rearrange("p (r h n) -> p r h n", r=2, h=HEADS)
        banks = ctx.enter_context(nc.psum_tensor("banks3", [P, 8, 512], F32))
        K = sb.const
        carried = sem("carried")
        page_in, new_in = sem("page_in"), [sem("new_in0"), sem("new_in1")]
        chunk_in = [[sem(f"chunk_in{p}{c}") for c in range(NCH)] for p in range(2)]
        rows_free, q_ready, q_free = sem("rows_free"), sem("q_ready"), sem("q_free")
        bank_full = [sem(f"bank_full{i}") for i in range(4)]
        bank_free = [sem(f"bank_free{i}") for i in range(4)]
        keys_v, keys_a, scored = sem("keys_v"), sem("keys_a"), sem("scored3")
        read_v, read_a, masked, maxed, negd, expd, vec = (sem(n) for n in ("read_v", "read_a", "masked", "maxed3", "negd", "expd3", "vec3"))
        scaled, new_scored, newT, newT_out, probs_out, pv_ready, pv_out = (sem(n) for n in (
            "scaled", "new_scored", "newT", "newT_out", "probs_out", "pv_ready3", "pv_out3"))
        o_ready, o_out, o_turned, ol_out = sem("o_ready3"), sem("o_out3"), sem("o_turned"), sem("ol_out")
        MID = 1
        EARLY = 3 * (MID + 2)

        def key_use(b, u):
            if isinstance(b, int) and b == 0:
                return u // 4
            return b * 7 + (u // 4 - (u < EARLY))

        def prob_use(b, u):
            return b * 7 + 6 + (0 if isinstance(b, int) and b == NSEQ - 1 else len(range(u % 4, EARLY, 4)))

        with nc.Block() as block:
            def over(eng, head, body, tail):
                head()
                with eng.Fori(0, NSEQ // 2 - 1) as i:
                    body(i * 2 + 1, 1)
                    body(i * 2 + 2, 0)
                tail(NSEQ - 1, 1)

            @block.sync
            def _(sp):
                sp.dma_start(page[:], io.pages.rearrange("(a b) n -> a (b n)", a=1)).then_inc(page_in, 16)
                sp.wait_ge(page_in, 16)

                def load(b, par):
                    sp.wait_ge(rows_free, b + 1)
                    for j in range(NPAGE):
                        n = sp.value_load(page[0:1, bass.ds(b * NPAGE + j, 1)], min_val=0, max_val=NPHYS - 1)
                        s = chunk_in[par][j // 4]
                        sp.dma_start(rows[:, par, j, :], io.cache_c[bass.ds(n, 1)].rearrange("a p r -> (a p) r")).then_inc(s, 16)
                        sp.dma_start(rots[:, par, j, :], io.cache_r[bass.ds(n, 1)].rearrange("a p r -> (a p) r")).then_inc(s, 16)

                with sp.Fori(0, NSEQ // 2) as i:
                    load(i * 2, 0)
                    load(i * 2 + 1, 1)

            @block.gpsimd
            def _(pool):
                def stage(b, par):
                    pool.wait_ge(q_free, b + 1)
                    pool.dma_start(new_b[:, par, :], io.o_cs[bass.ds(b * TS, TS), :]).then_inc(new_in[par], 16)
                    at, fresh = bass.ds(b * TS, TS), bass.ds(b * TS + SEQ, TS)
                    pool.tensor_copy(cT_b[:, par], sb.cT[:, :, fresh])
                    pool.tensor_copy(krT_b[:, par, :], sb.krT[:, fresh])
                    for r in range(2):
                        pool.tensor_copy(q_b[:, par, r, :].rearrange("p (h t) -> p h t", h=HEADS), sb.qlS[:, r, :, at])
                    pool.tensor_copy(qr_b[:, par, :].rearrange("p (h t) -> p h t", h=HEADS), sb.qrS[:, :, at]).then_inc(q_ready, 1)

                with pool.Fori(0, NSEQ // 2) as i:
                    stage(i * 2, 0)
                    stage(i * 2 + 1, 1)

            @block.tensor
            def _(pe):
                pe.sem_inc(rows_free, 2)
                pe.sem_inc(q_free, 2)

                def settle():
                    pe.sem_inc(carried, 1)

                def turn_keys(b, par, c):
                    for j in range(3):
                        u = 3 * c + j
                        if j == 0:
                            pe.wait_ge(chunk_in[par][c], (b - par) * 64 + 128)
                        pe.wait_ge(bank_free[u % 4], key_use(b, u) + 1)
                        if j == 2:
                            settle()
                        for k in range(4):
                            src = rows[:, par, 4 * c + k, j * P:(j + 1) * P] if j < 2 else rots[:, par, 4 * c + k, :]
                            mm = pe.transpose(banks[0:P if j < 2 else ROPE, u % 4, k * P:(k + 1) * P], src, K[:, K_ID:K_ID + P])
                        mm.then_inc(bank_full[u % 4], 1)

                def score_chunk(b, par, c):
                    pe.wait_ge(keys_v, b * NCH + c + 1)
                    pe.wait_ge(keys_a, b * NCH + c + 1)
                    pe.wait_ge(read_a, b * NCH + c + 1)
                    o = banks[0:NQ, 4 + c % 2, :]
                    for r in range(2):
                        pe.matmul(o, q_b[:, par, r, :], keyT[:, c % 2, r, :], start=(r == 0), stop=False)
                    pe.matmul(o, qr_b[:, par, :], keyT[0:ROPE, c % 2, 2, :], start=False, stop=True).then_inc(scored, 1)

                def scores(b, par, between):
                    pe.wait_ge(q_ready, b + 1)
                    turn_keys(b, par, 0)
                    for c in range(NCH):
                        if c + 1 < NCH:
                            turn_keys(b, par, c + 1)
                        score_chunk(b, par, c)
                        if c == MID:
                            between()
                    pe.wait_ge(masked, b + 1)
                    o = banks[0:NQ, 7, 0:TS]
                    for r in range(2):
                        pe.matmul(o, q_b[:, par, r, :], cT_b[:, par, r, :], start=(r == 0), stop=False)
                    pe.matmul(o, qr_b[:, par, :], krT_b[:, par, :], start=False, stop=True).then_inc(new_scored, 1)

                def values(b, par):
                    pe.wait_ge(scaled, b + 1)
                    for m in range(4):
                        u = 3 * NCH + m
                        pe.wait_ge(bank_free[u % 4], prob_use(b, u) + 1)
                        settle()
                        for k in range(8):
                            mm = pe.transpose(banks[:, u % 4, k * NQ:(k + 1) * NQ], score[:, par, (8 * m + k) * P:(8 * m + k + 1) * P], K[0:NQ, K_ID:K_ID + NQ])
                        mm.then_inc(bank_full[u % 4], 1)
                    pe.wait_ge(newT_out, b + 1)
                    pe.wait_ge(masked, b + 2)
                    settle()
                    pe.transpose(banks[0:TS, 7, 128:128 + NQ], score[:, par, PAST:NKEY], K[0:NQ, K_ID:K_ID + NQ]).then_inc(newT, 1)
                    pe.wait_ge(pv_out, b + 1)
                    o = banks[0:NQ, 6, 0:KVL]
                    for k in range(NPAGE):
                        if k % 8 == 0:
                            pe.wait_ge(probs_out, b * 4 + k // 8 + 1)
                        if k == NPAGE - 8:
                            pe.wait_ge(newT_out, b + 2)
                            pe.wait_ge(new_in[par], (b - par) * 8 + 16)
                        pe.matmul(o, probT[:, k, :], rows[:, par, k, :], start=(k == 0), stop=False)
                    pe.matmul(o, probT_new[:], new_b[:, par, :], start=False, stop=True).then_inc(pv_ready, 1)
                    pe.wait_ge(pv_ready, b + 1)
                    pe.sem_inc(rows_free, 1)
                    pe.sem_inc(q_free, 1)

                def body(b, par):
                    scores(b, par, lambda: values(b - 1, 1 - par))

                def tail(b, par):
                    body(b, par)
                    values(b, par)

                over(pe, lambda: scores(0, 0, lambda: None), body, tail)
                pe.wait_ge(pv_out, NSEQ + 1)
                for r in range(2):
                    for b in range(NSEQ):
                        mm = pe.transpose(banks[:, r, b * NQ:(b + 1) * NQ], o_rows[:, b, r * P:(r + 1) * P], K[0:NQ, K_ID:K_ID + NQ])
                    mm.then_inc(o_turned, 1)
                pe.wait_ge(ol_out, 2)
                for h in range(HEADS):
                    if h >= 2:
                        pe.wait_ge(o_out, h - 1)
                    for r in range(2):
                        mm = pe.matmul(banks[:, 4 + h % 2, 0:NS], sb.wkv[:, r, h * 256 + NOPE:(h + 1) * 256], olS[:, r, h, :],
                                       start=(r == 0), stop=(r == 1))
                    mm.then_inc(o_ready, 1)

            @block.scalar
            def _(act):
                act.sem_inc(read_a, 2)

                def chunk(b, par, c):
                    u = 3 * c + 1
                    act.wait_ge(bank_full[u % 4], key_use(b, u) + 1)
                    act.wait_ge(scored, b * NCH + c + 1)
                    act.activation(keyT[:, c % 2, 1, :], banks[:, u % 4, :], ACT.Copy).then_inc(keys_a, 1)
                    act.wait_ge(keys_a, b * NCH + c + 1)
                    act.sem_inc(bank_free[u % 4], 1)

                def copy_scores(b, par, c):
                    act.wait_ge(scored, b * NCH + c + 3)
                    act.activation(score[:, par, c * 512:(c + 1) * 512], banks[0:NQ, 4 + c % 2, :], ACT.Copy).then_inc(read_a, 1)

                def exponents(b, par):
                    act.wait_ge(negd, b + 1)
                    act.wait_ge(read_a, (b + 1) * NCH + 2)
                    act.activation(score[:, par, :], score[:, par, :], ACT.Exp, bias=stat[:, par, 1:2], scale=ATT_SCALE,
                                   accum_out=stat[:, par, 2:3]).then_inc(expd, 1)

                def chunks(b, par, between):
                    act.wait_ge(newT, b)
                    chunk(b, par, 0)
                    between()
                    for c in range(NCH):
                        if c + 1 < NCH:
                            chunk(b, par, c + 1)
                        copy_scores(b, par, c)

                def body(b, par):
                    chunks(b, par, lambda: exponents(b - 1, 1 - par))

                def tail(b, par):
                    body(b, par)
                    exponents(b, par)

                over(act, lambda: chunks(0, 0, lambda: None), body, tail)

            @block.vector
            def _(dve):
                dve.sem_inc(scored, 2)
                dve.sem_inc(masked, 1)
                dve.sem_inc(newT_out, 1)
                dve.sem_inc(newT, 1)
                dve.sem_inc(pv_out, 1)
                for s in bank_free:
                    dve.sem_inc(s, 1)

                def keys(b, par, c):
                    for j in (0, 2):
                        u = 3 * c + j
                        n = P if j < 2 else ROPE
                        dve.wait_ge(bank_full[u % 4], key_use(b, u) + 1)
                        if j == 0:
                            dve.wait_ge(scored, b * NCH + c + 1)
                        ins = dve.tensor_copy(keyT[0:n, c % 2, j, :], banks[0:n, u % 4, :])
                        if j == 0:
                            ins.then_inc(bank_free[u % 4], 1)
                        else:
                            ins.then_inc(keys_v, 1)
                            dve.wait_ge(keys_v, b * NCH + c + 1)
                            dve.sem_inc(bank_free[u % 4], 1)

                def chunk_max(b, par, c):
                    dve.wait_ge(read_a, b * NCH + c + 3)
                    dve.reduce_max(mx[:, par, c:c + 1], score[:, par, c * 512:(c + 1) * 512], AX).then_inc(read_v, 1)

                def chunks(b, par, early, between):
                    keys(b, par, 0)
                    for c in range(NCH):
                        if c + 1 < NCH:
                            keys(b, par, c + 1)
                        if c == 0:
                            early()
                        chunk_max(b, par, c)
                        if c == MID:
                            between()
                    dve.wait_ge(new_scored, b + 1)
                    fresh = score[:, par, PAST:NKEY]
                    dve.tensor_tensor(fresh, banks[0:NQ, 7, 0:TS], K[0:NQ, K_NEW:K_NEW + TS], ALU.add).then_inc(masked, 1)
                    dve.wait_ge(masked, b + 2)
                    dve.reduce_max(mx[:, par, NCH:NCH + 1], fresh, AX).then_inc(vec, 1)
                    dve.wait_ge(vec, b * 3 + 1)
                    dve.wait_ge(read_v, (b + 1) * NCH)
                    dve.reduce_max(stat[:, par, 0:1], mx[:, par, :], AX).then_inc(vec, 1)
                    dve.wait_ge(vec, b * 3 + 2)
                    dve.tensor_scalar(stat[:, par, 1:2], stat[:, par, 0:1], -ATT_SCALE, None, ALU.mult).then_inc(negd, 1)

                def scale(b, par):
                    dve.wait_ge(expd, b + 1)
                    dve.reciprocal(stat[:, par, 2:3], stat[:, par, 2:3]).then_inc(vec, 1)
                    dve.wait_ge(vec, b * 3 + 3)
                    dve.tensor_scalar(score[:, par, :], score[:, par, :], stat[:, par, 2:3], None, ALU.mult).then_inc(scaled, 1)

                def out(b, par):
                    for m in range(4):
                        u = 3 * NCH + m
                        dve.wait_ge(bank_full[u % 4], prob_use(b, u) + 1)
                        dve.tensor_copy(probT[:, 8 * m:8 * m + 8, :], banks[:, u % 4, :].rearrange("p (k n) -> p k n", k=8)).then_inc(probs_out, 1)
                        dve.wait_ge(probs_out, b * 4 + m + 1)
                        dve.sem_inc(bank_free[u % 4], 1)
                    dve.wait_ge(newT, b + 2)
                    dve.tensor_copy(probT_new[:], banks[0:TS, 7, 128:128 + NQ]).then_inc(newT_out, 1)
                    dve.wait_ge(pv_ready, b + 1)
                    dve.tensor_copy(o_rows[:, bass.ds(b, 1), :].rearrange("p b r -> p (b r)"), banks[0:NQ, 6, 0:KVL]).then_inc(pv_out, 1)

                def body(b, par):
                    chunks(b, par, lambda: scale(b - 1, 1 - par), lambda: out(b - 1, 1 - par))

                def tail(b, par):
                    body(b, par)
                    scale(b, par)
                    out(b, par)

                over(dve, lambda: chunks(0, 0, lambda: None, lambda: None), body, tail)
                for r in range(2):
                    dve.wait_ge(o_turned, r + 1)
                    dve.tensor_copy(olS[:, r].rearrange("p h (b t) -> p b h t", b=NSEQ),
                                    banks[:, r, :].rearrange("p (b h t) -> p b h t", b=NSEQ, h=HEADS)).then_inc(ol_out, 1)
                for h in range(HEADS):
                    dve.wait_ge(o_ready, h + 1)
                    dve.tensor_copy(sb.oT[:, h, SEQ:T], banks[:, 4 + h % 2, 0:NS]).then_inc(o_out, 1)


def stage_turn_x(nc, io, sb):
    with ExitStack() as ctx:
        sem = ctx.enter_context(signals(nc, "turn_x"))
        x_tok = ctx.enter_context(nc.sbuf_tensor("x_tok4", [P, NT, D], F32))
        banks = ctx.enter_context(nc.psum_tensor("banks4x", [P, 8, 512], F32))
        x_in = [sem(f"x_in4{i}") for i in range(NT)]
        turned, turned_out = sem("turned4"), sem("turned_out4")
        with nc.Block() as block:
            @block.sync
            def _(sp):
                for i in range(NT):
                    sp.dma_start(x_tok[0:ROWS[i], i, :], token_dram(io.xp, io.xs, i)).then_inc(x_in[i], 16)

            @block.tensor
            def _(pe):
                for i in range(NT):
                    n = ROWS[i]
                    pe.wait_ge(x_in[i], 16)
                    for h in range(2):
                        u = 2 * i + h
                        if u >= 8:
                            pe.wait_ge(turned_out, u - 7)
                        for k in range(4):
                            mm = pe.transpose(banks[:, u % 8, k * n:(k + 1) * n],
                                              x_tok[0:n, i, (4 * h + k) * P:(4 * h + k + 1) * P], sb.const[0:n, K_ID:K_ID + n])
                        mm.then_inc(turned, 1)

            @block.vector
            def _(dve):
                for u in range(2 * NT):
                    i, h = divmod(u, 2)
                    n = ROWS[i]
                    dve.wait_ge(turned, u + 1)
                    dve.tensor_copy(sb.xT[:, 4 * h:4 * h + 4, P * i:P * i + n],
                                    banks[:, u % 8, 0:4 * n].rearrange("p (k n) -> p k n", k=4)).then_inc(turned_out, 1)


def stage_merge(nc, io, sb, gate_col, w, x_of, nk, first, split_branch, tag):
    with ExitStack() as ctx:
        sem = ctx.enter_context(signals(nc, "merge" + tag))
        buf = lambda n, s, d=F32: ctx.enter_context(nc.sbuf_tensor(n + tag, s, d))
        ns = nk if split_branch else 0
        w_raw = buf("w_raw", [P, KD + ns, P])
        w_hi, w_lo = buf("w_mhi", [P, 2, KD + ns, P], F32R), buf("w_mlo", [P, 2, KD + ns, P], F32R)
        x_hi, x_lo = buf("x_mhi", [P, KD, T], F32R), buf("x_mlo", [P, KD, T], F32R)
        if split_branch:
            y_hi, y_lo = buf("y_mhi", [P, nk, T], F32R), buf("y_mlo", [P, nk, T], F32R)
        else:
            w_br = buf("w_br", [P, 2, nk, P])
            y_hi = y_lo = None
        sig = buf("sig", [P, 2, T])
        prod = None if first else buf("prod", [P, 2, T])
        banks = ctx.enter_context(nc.psum_tensor("banks" + tag, [P, 8, 512], F32))
        w_in_, br_in = sem("w_in"), [sem(f"br_in{i}") for i in range(2)]
        w_high, w_low, t_high, t_low = sem("w_high"), sem("w_low"), sem("t_high"), sem("t_low")
        gate_ready, y_ready, sig_out, prod_out, merged = sem("gate_ready"), sem("y_ready"), sem("sig_out"), sem("prod_out"), sem("merged")
        n_m = D // P
        gate_view = io.w_in.rearrange("(k p) n -> p k n", p=P)
        w_view = w.rearrange("(k p) n -> p k n", p=P)
        tiles = [(sb.xT[:, k, :], x_hi, x_lo, k) for k in range(KD)] + [(x_of(k), y_hi, y_lo, k) for k in range(ns)]

        with nc.Block() as block:
            @block.sync
            def _(sp):
                for m in range(n_m):
                    if m >= 1:
                        sp.wait_ge(w_low, m)
                    sp.dma_start(w_raw[:, 0:KD, :], gate_view[:, :, gate_col + m * P:gate_col + (m + 1) * P]).then_inc(w_in_, 16)
                    if split_branch:
                        sp.dma_start(w_raw[:, KD:KD + ns, :], w_view[:, :, m * P:(m + 1) * P]).then_inc(w_in_, 16)
                    else:
                        if m >= 2:
                            sp.wait_ge(y_ready, m - 1)
                        sp.dma_start(w_br[:, m % 2], w_view[:, :, m * P:(m + 1) * P]).then_inc(br_in[m % 2], 16)

            @block.tensor
            def _(pe):
                def products(m, k0, n, hi, lo, bank):
                    for k in range(n):
                        if m == 0:
                            pe.wait_ge(t_low, k0 + k + 1)
                        for wp, parts in ((w_hi, (hi, lo)), (w_lo, (hi,))):
                            for part in parts:
                                for piece in range(2):
                                    mm = pe.matmul(banks[:, bank + piece, 0:H2], wp[:, m % 2, k0 + k, :], part[:, k, piece * H2:(piece + 1) * H2],
                                                   start=(k == 0 and wp is w_hi and part is hi), stop=(k == n - 1 and wp is w_lo))
                    return mm

                for m in range(n_m):
                    b = 4 * (m % 2)
                    pe.wait_ge(w_low, m + 1)
                    if m >= 2:
                        pe.wait_ge(sig_out, m - 1)
                        pe.wait_ge(prod_out, m - 1)
                    products(m, 0, KD, x_hi, x_lo, b).then_inc(gate_ready, 1)
                    if split_branch:
                        products(m, KD, nk, y_hi, y_lo, b + 2).then_inc(y_ready, 1)
                        continue
                    pe.wait_ge(br_in[m % 2], 16 * (m // 2 + 1))
                    for piece in range(2):
                        for k in range(nk):
                            mm = pe.matmul(banks[:, b + 2 + piece, 0:H2], w_br[:, m % 2, k, :],
                                           x_of(k)[:, piece * H2:(piece + 1) * H2], start=(k == 0), stop=(k == nk - 1))
                    mm.then_inc(y_ready, 1)

            @block.scalar
            def _(act):
                def high(m):
                    act.wait_ge(w_in_, (32 if split_branch else 16) * (m + 1))
                    if m >= 2:
                        act.wait_ge(y_ready, m - 1)
                    act.activation(w_hi[:, m % 2], w_raw[:], ACT.Copy).then_inc(w_high, 1)

                high(0)
                for src, hi, _, k in tiles:
                    act.activation(hi[:, k, :], src, ACT.Copy).then_inc(t_high, 1)
                high(1)
                for m in range(n_m):
                    b = 4 * (m % 2)
                    if 1 <= m < n_m - 1:
                        high(m + 1)
                    act.wait_ge(gate_ready, m + 1)
                    if m >= 2:
                        act.wait_ge(prod_out, m - 1)
                    act.activation(sig[:, m % 2, :].rearrange("p (a n) -> p a n", a=2), banks[:, b:b + 2, 0:H2], ACT.Sigmoid).then_inc(sig_out, 1)

            @block.vector
            def _(dve):
                def low(m):
                    dve.wait_ge(w_high, m + 1)
                    dve.tensor_tensor(w_lo[:, m % 2], w_raw[:], w_hi[:, m % 2].bitcast(F32), ALU.subtract).then_inc(w_low, 1)

                low(0)
                for j, (src, hi, lo, k) in enumerate(tiles):
                    dve.wait_ge(t_high, j + 1)
                    dve.tensor_tensor(lo[:, k, :], src, hi[:, k, :].bitcast(F32), ALU.subtract).then_inc(t_low, 1)
                low(1)
                for m in range(n_m):
                    b = 4 * (m % 2)
                    if 1 <= m < n_m - 1:
                        low(m + 1)
                    dve.wait_ge(y_ready, m + 1)
                    dve.wait_ge(sig_out, m + 1)
                    if not first and m >= 2:
                        dve.wait_ge(merged, m - 1)
                    o = sb.mergedT[:, m, :] if first else prod[:, m % 2, :]
                    dve.tensor_tensor(o.rearrange("p (a n) -> p a n", a=2), banks[:, b + 2:b + 4, 0:H2],
                                      sig[:, m % 2, :].rearrange("p (a n) -> p a n", a=2), ALU.mult).then_inc(prod_out, 1)
                    if not first:
                        dve.wait_ge(prod_out, m + 1)
                        dve.tensor_tensor(sb.mergedT[:, m, :], sb.mergedT[:, m, :], prod[:, m % 2, :], ALU.add).then_inc(merged, 1)


def stage_conv(nc, io, sb):
    NR = NSEQ * (KC - 1) + KC + 1
    NO = (KC - 1) * (1 + NSEQ)
    LP = SEQ + KC - 1
    LS = TS + KC - 1
    with ExitStack() as ctx:
        sem = ctx.enter_context(signals(nc, "conv"))
        buf = lambda n, s: ctx.enter_context(nc.sbuf_tensor(n, s, F32))
        CW = 256
        NC = CONV // CW
        w = buf("w_x", [P, KD, CW])
        w_hi, w_lo = (ctx.enter_context(nc.sbuf_tensor(n, [P, 2, KD, CW], F32R)) for n in ("wx_hi", "wx_lo"))
        x_hi, x_lo = (ctx.enter_context(nc.sbuf_tensor(n, [P, KD, T], F32R)) for n in ("xc_hi", "xc_lo"))
        small = buf("small", [NR, CONV])
        smallT = buf("smallT", [P, NCT, NR])
        pre = buf("pre", [P, 3, LP + NSEQ * LS])
        acc = buf("acc", [P, 2, T])
        lastT = buf("lastT", [P, NCT, NO])
        last = small[0:NO, :]
        banks = ctx.enter_context(nc.psum_tensor("banks5", [P, 8, 512], F32))
        small_in, w_in_ = sem("small_in"), sem("w_x_in")
        x_high, x_low, w_high, w_low = sem("x_high"), sem("x_low"), sem("w_high"), sem("w_low")
        small_ready, small_out, zeroed = sem("small_ready"), sem("small_out"), sem("zeroed5")
        ready, copied, state_put, tap, conved, done = (sem(n) for n in ("x_ready", "x_copied", "state_put", "tap", "conved", "silu_done"))
        last_ready, last_out, stored, kept = sem("last_ready"), sem("last_out"), sem("stored5"), sem("kept")
        S0, W0, B0 = 0, NSEQ * (KC - 1), NSEQ * (KC - 1) + KC
        PER = 17
        w_view = io.w_in.rearrange("(k p) n -> p k n", p=P)
        sample = lambda slot: pre[:, slot, LP:].rearrange("p (b t) -> p b t", b=NSEQ)

        with nc.Block() as block:
            @block.sync
            def _(sp):
                sp.dma_start(small[0:W0, :], io.conv).then_inc(small_in, 16)
                sp.dma_start(small[W0:B0, :], io.conv_w).then_inc(small_in, 16)
                sp.dma_start(small[B0:NR, :], io.conv_b).then_inc(small_in, 16)
                for c in range(NC):
                    if c >= 1:
                        sp.wait_ge(w_low, c)
                    sp.dma_start(w[:], w_view[:, :, C_X + c * CW:C_X + (c + 1) * CW]).then_inc(w_in_, 16)
                sp.wait_ge(last_out, NCT // 4)
                sp.dma_start(io.o_convp, last[0:KC - 1, :]).then_inc(stored, 16)
                sp.dma_start(io.o_convs, last[KC - 1:NO, :]).then_inc(stored, 16)
                sp.wait_ge(stored, 32)

            @block.gpsimd
            def _(pool):
                pool.memset(pre[:, :, 0:KC - 1], 0.0).then_inc(zeroed, 1)

            @block.tensor
            def _(pe):
                pe.wait_ge(small_in, 48)
                for m in range(NCT):
                    mm = pe.transpose(banks[:, 6 + m // PER, (m % PER) * NR:(m % PER + 1) * NR], small[:, m * P:(m + 1) * P], sb.const[0:NR, K_ID:K_ID + NR])
                mm.then_inc(small_ready, 1)
                for m in range(NCT):
                    c, b, at = m // 2, 2 * (m % 3), (m % 2) * P
                    pe.wait_ge(w_low, c + 1)
                    if m >= 3:
                        pe.wait_ge(copied, m - 2)
                    for k in range(KD):
                        if m == 0:
                            pe.wait_ge(x_low, k + 1)
                        for wp, parts in ((w_hi, (x_hi, x_lo)), (w_lo, (x_hi,))):
                            for part in parts:
                                for piece in range(2):
                                    mm = pe.matmul(banks[:, b + piece, 0:H2], wp[:, c % 2, k, at:at + P], part[:, k, piece * H2:(piece + 1) * H2],
                                                   start=(k == 0 and wp is w_hi and part is x_hi), stop=(k == KD - 1 and wp is w_lo))
                    mm.then_inc(ready, 1)
                pe.wait_ge(kept, NCT)
                for u in range(NCT // 4):
                    if u == 0:
                        pe.wait_ge(copied, NCT)
                    for k in range(4):
                        mm = pe.transpose(banks[0:NO, u, k * P:(k + 1) * P], lastT[:, 4 * u + k, :], sb.const[:, K_ID:K_ID + P])
                    mm.then_inc(last_ready, 1)

            @block.scalar
            def _(act):
                def silu(m):
                    act.wait_ge(conved, m + 1)
                    act.activation(sb.xbcT[:, m, :], acc[:, m % 2, :], ACT.Silu).then_inc(done, 1)

                def high(c):
                    act.wait_ge(w_in_, 16 * (c + 1))
                    if c >= 2:
                        act.wait_ge(ready, 2 * (c - 1))
                    act.activation(w_hi[:, c % 2], w[:], ACT.Copy).then_inc(w_high, 1)

                high(0)
                for k in range(KD):
                    act.activation(x_hi[:, k, :], sb.xT[:, k, :], ACT.Copy).then_inc(x_high, 1)
                high(1)
                for m in range(NCT):
                    b, s = 2 * (m % 3), m % 3
                    if m % 2 == 0 and 2 <= m < NCT - 2:
                        high(m // 2 + 1)
                    act.wait_ge(ready, m + 1)
                    if m >= 3:
                        act.wait_ge(kept, m - 2)
                    act.activation(pre[:, s, KC - 1:KC - 1 + H2], banks[:, b, 0:H2], ACT.Copy)
                    act.activation(pre[:, s, KC - 1 + H2:LP], banks[:, b + 1, 0:SEQ - H2], ACT.Copy)
                    act.activation(sample(s)[:, :, KC - 1:LS], banks[:, b + 1, SEQ - H2:H2].rearrange("p (b t) -> p b t", b=NSEQ),
                                   ACT.Copy).then_inc(copied, 1)
                    if m >= 1:
                        silu(m - 1)
                silu(NCT - 1)

            @block.vector
            def _(dve):
                def low(c):
                    dve.wait_ge(w_high, c + 1)
                    dve.tensor_tensor(w_lo[:, c % 2], w[:], w_hi[:, c % 2].bitcast(F32), ALU.subtract).then_inc(w_low, 1)

                low(0)
                for k in range(KD):
                    dve.wait_ge(x_high, k + 1)
                    dve.tensor_tensor(x_lo[:, k, :], sb.xT[:, k, :], x_hi[:, k, :].bitcast(F32), ALU.subtract).then_inc(x_low, 1)
                low(1)
                dve.wait_ge(small_ready, 1)
                dve.tensor_copy(smallT[:, 0:PER, :], banks[:, 6, 0:PER * NR].rearrange("p (m r) -> p m r", m=PER))
                dve.tensor_copy(smallT[:, PER:NCT, :], banks[:, 7, 0:(NCT - PER) * NR].rearrange("p (m r) -> p m r", m=NCT - PER)).then_inc(small_out, 1)
                dve.wait_ge(small_out, 1)
                dve.wait_ge(zeroed, 1)
                for m in range(NCT):
                    s = m % 3
                    if m % 2 == 0 and 2 <= m < NCT - 2:
                        low(m // 2 + 1)
                    if m >= 3:
                        dve.wait_ge(kept, m - 2)
                    dve.tensor_copy(sample(s)[:, :, 0:KC - 1], smallT[:, m, S0:W0].rearrange("p (b k) -> p b k", b=NSEQ)).then_inc(state_put, 1)
                    dve.wait_ge(state_put, m + 1)
                    dve.wait_ge(copied, m + 1)
                    if m >= 2:
                        dve.wait_ge(done, m - 1)
                    ap, as_ = acc[:, m % 2, 0:SEQ], acc[:, m % 2, SEQ:T].rearrange("p (b t) -> p b t", b=NSEQ)
                    for k in range(KC):
                        wk = smallT[:, m, W0 + k:W0 + k + 1]
                        xp, xs = pre[:, s, k:k + SEQ], sample(s)[:, :, k:k + TS]
                        if k == 0:
                            bias = smallT[:, m, B0:B0 + 1]
                            dve.tensor_scalar(ap, xp, wk, bias, ALU.mult, ALU.add)
                            dve.tensor_scalar(as_, xs, wk, bias, ALU.mult, ALU.add).then_inc(tap, 1)
                        else:
                            dve.wait_ge(tap, m * (KC - 1) + k)
                            dve.scalar_tensor_tensor(out=ap, in0=xp, scalar=wk, in1=ap, op0=ALU.mult, op1=ALU.add)
                            ins = dve.scalar_tensor_tensor(out=as_, in0=xs, scalar=wk, in1=as_, op0=ALU.mult, op1=ALU.add)
                            ins.then_inc(conved if k == KC - 1 else tap, 1)
                    dve.tensor_copy(lastT[:, m, 0:KC - 1], pre[:, s, SEQ:LP])
                    dve.tensor_copy(lastT[:, m, KC - 1:NO].rearrange("p (b k) -> p b k", b=NSEQ), sample(s)[:, :, TS:LS]).then_inc(kept, 1)
                for u in range(NCT // 4):
                    dve.wait_ge(last_ready, u + 1)
                    dve.tensor_copy(last[:, u * 512:(u + 1) * 512], banks[0:NO, u, :]).then_inc(last_out, 1)


def stage_ssd(nc, io, sb):
    with ExitStack() as ctx:
        sem = ctx.enter_context(signals(nc, "ssd"))
        buf = lambda n, s: ctx.enter_context(nc.sbuf_tensor(n, s, F32))
        K = sb.const
        dt_b, a_b, d_b = buf("dt_b", [P, SH]), buf("a_b", [P, SH]), buf("d_b", [P, SH])
        gn = buf("gn", [P, DI])
        t1, t2, t3 = (buf(n, [P, NT, SH]) for n in ("t1", "t2", "t3"))
        dta, acs, aend, e_acs, w_end, e_end = (buf(n, [P, NT, SH]) for n in ("dta", "acs", "aend", "e_acs", "w_end", "e_end"))
        wz = buf("wz", [P, 2, KD, GW])
        h0 = buf("h0", [P, 4, NSEQ, NST])
        h0T = buf("h0T", [NST, 2, GW])
        xs_t = buf("xs_t", [P, 2, GW])
        b_t = buf("b_t", [P, 2, NST])
        cb = buf("cb", [P, P])
        dec = buf("dec", [P, 2, HG, P])
        xdt, xend, xd = buf("xdt", [P, 2, GW]), buf("xend", [P, 2, GW]), buf("xd", [P, 2, GW])
        y = buf("y", [P, 2, GW])
        off = buf("off", [P, GW])
        zs = buf("zs", [P, GW])
        junk = zs
        ssq = buf("ssq6", [P, 2])
        stT = buf("stT", [NST, GW])
        c_of = buf("c_of", [P, NSEQ, NS])
        b_of = buf("b_of", [NS, NSEQ, NST])
        e_seq = buf("e_seq", [P, 4, NSEQ])
        st_out = buf("st_out", [P, 4, NST])
        banks = ctx.enter_context(nc.psum_tensor("banks6", [P, 8, 512], F32))
        N = G * NT
        unit = lambda k: divmod(k, NT)
        vec_in, wz_in = sem("vec_in"), [sem("wz_in0"), sem("wz_in1")]
        h_in, h_out, p_out = sem("h_in"), sem("h_stored"), sem("p_stored")
        prep_v, prep_a, sums_ready, sums_out = sem("prep_v"), sem("prep_a"), sem("sums_ready"), sem("sums_out")
        xs_ready, xs_out, cb_ready, cb_out, acs_ready, seg_out, dec_out, w_out = (sem(n) for n in (
            "xs_ready", "xs_out", "cb_ready", "cb_out", "acs_ready", "seg_out", "dec_out", "w_out"))
        scaled, of_seq, z_ready, z_out, y_ready, y_step, gated, squared, rooted, inverse, normed = (sem(n) for n in (
            "x_scaled", "of_seq", "z_ready", "z_out", "y_ready", "y_step", "gated", "squared6", "rooted6", "inverse", "normed6"))
        yt_ready, yt_out, st_ready, st_step, st_new = (sem(n) for n in ("yt_ready", "yt_out", "st_ready", "st_step", "st_new"))
        hT_ready, hT_out, off_part, fin_ready, fin_out, hs_ready, hs_out = (sem(n) for n in (
            "hT_ready", "hT_out", "off_part", "fin_ready", "fin_out", "hs_ready", "hs_out"))
        e_out, y_sum, mean_ready = sem("e_out"), sem("y_sum"), sem("mean_ready")
        heads = lambda t, n: t.rearrange("p (h d) -> p h d", h=HG)
        z_view = io.w_in.rearrange("(k p) n -> p k n", p=P)
        tri = lambda i, n: K[0:n, K_TRI:K_TRI + n] if i < 4 else K[0:n, K_BTRI:K_BTRI + n]

        with nc.Block() as block:
            @block.sync
            def _(sp):
                for t, src in ((dt_b, io.dt_bias), (a_b, io.a_log), (d_b, io.d_skip)):
                    sp.dma_start(t[:], src.broadcast_to((P, SH))).then_inc(vec_in, 16)
                sp.dma_start(gn[:], io.gn.broadcast_to((P, DI))).then_inc(vec_in, 16)
                for g in range(G):
                    if g >= 2:
                        sp.wait_ge(z_ready, NT * (g - 1))
                    sp.dma_start(wz[:, g % 2], z_view[:, :, C_Z + g * GW:C_Z + (g + 1) * GW]).then_inc(wz_in[g % 2], 16)
                    if g >= 1:
                        sp.wait_ge(fin_out, g)
                        sp.dma_start(io.o_ssmp[(g - 1) * GW:g * GW, :].rearrange("(q p) n -> p q n", p=P), st_out[:]).then_inc(p_out, 16)
                        sp.wait_ge(hs_out, 8 * g)
                        for q in range(4):
                            at = (g - 1) * GW + q * P
                            sp.dma_start(io.o_ssms[:, at:at + P, :].rearrange("b p n -> p b n"), h0[:, q]).then_inc(h_out, 16)
                        sp.wait_ge(h_out, 64 * g)
                    for q in range(4):
                        at = g * GW + q * P
                        sp.dma_start(h0[:, q], io.ssm[:, at:at + P, :].rearrange("b p n -> p b n")).then_inc(h_in, 16)
                sp.wait_ge(fin_out, G)
                sp.dma_start(io.o_ssmp[(G - 1) * GW:G * GW, :].rearrange("(q p) n -> p q n", p=P), st_out[:]).then_inc(p_out, 16)
                sp.wait_ge(hs_out, 8 * G)
                for q in range(4):
                    at = (G - 1) * GW + q * P
                    sp.dma_start(io.o_ssms[:, at:at + P, :].rearrange("b p n -> p b n"), h0[:, q]).then_inc(h_out, 16)
                sp.wait_ge(p_out, 16 * G)
                sp.wait_ge(h_out, 64 * G)

            @block.gpsimd
            def _(pool):
                pool.wait_ge(prep_v, 9)
                pool.wait_ge(vec_in, 64)
                for k in range(N):
                    g, i = unit(k)
                    n = ROWS[i]
                    pool.wait_ge(xs_out, k + 1)
                    if k >= 2:
                        pool.wait_ge(st_ready, k - 1)
                        pool.wait_ge(y_step, 2 * (k - 1))
                    x = heads(xs_t[0:n, k % 2], n)
                    for o, f in ((xdt, sb.dt[0:n, i]), (xend, w_end[0:n, i]), (xd, d_b[0:n])):
                        ins = pool.tensor_tensor(heads(o[0:n, k % 2], n), x, f[:, g * HG:(g + 1) * HG].unsqueeze(2).broadcast_to((n, HG, PD)), ALU.mult)
                    ins.then_inc(scaled, 1)
                    if i == NT - 1:
                        if g >= 1:
                            pool.wait_ge(hs_ready, 8 * g)
                        pool.tensor_tensor(c_of[:], sb.xbcT[:, 20 + g, SEQ:T].unsqueeze(1).broadcast_to((P, NSEQ, NS)),
                                           K[:, K_BCOL:K_BCOL + NSEQ * NS].rearrange("p (b n) -> p b n", b=NSEQ), ALU.mult)
                        pool.wait_ge(cb_out, k + 1)
                        pool.tensor_tensor(b_of[:], b_t[0:NS, k % 2, :].unsqueeze(1).broadcast_to((NS, NSEQ, NST)),
                                           K[0:NS, K_BROW:K_BROW + NSEQ].unsqueeze(2).broadcast_to((NS, NSEQ, NST)), ALU.mult).then_inc(of_seq, 1)

            @block.tensor
            def _(pe):
                pe.wait_ge(prep_v, 6)
                for i in range(NT):
                    n = ROWS[i]
                    pe.matmul(banks[0:n, 0, i * SH:(i + 1) * SH], tri(i, n), dta[0:n, i, :], start=True, stop=True)
                    last = K[0:n, K_ONE:K_ONE + n] if i < 4 else K[0:n, K_BALL:K_BALL + n]
                    mm = pe.matmul(banks[0:n, 1, i * SH:(i + 1) * SH], last, dta[0:n, i, :], start=True, stop=True)
                mm.then_inc(sums_ready, 1)
                pe.wait_ge(sums_out, 1)

                def inputs(k):
                    g, i = unit(k)
                    n = ROWS[i]
                    at = slice(P * i, P * i + n)
                    if k >= 1:
                        pe.wait_ge(xs_out, k)
                    if k >= 3:
                        pe.wait_ge(yt_out, k - 2)
                    for q in range(4):
                        mm = pe.transpose(banks[0:n, 0, q * P:(q + 1) * P], sb.xbcT[:, 4 * g + q, at], K[:, K_ID:K_ID + P])
                    mm.then_inc(xs_ready, 1)
                    if k >= 1:
                        pe.wait_ge(cb_out, k)
                        if unit(k - 1)[1] == NT - 1:
                            pe.wait_ge(e_out, unit(k - 1)[0] + 1)
                    pe.transpose(banks[0:n, 1, 0:P], sb.xbcT[:, 16 + g, at], K[:, K_ID:K_ID + P])
                    mm = pe.matmul(banks[0:n, 1, P:P + n], sb.xbcT[:, 16 + g, at], sb.xbcT[:, 20 + g, at], start=True, stop=True)
                    if i == NT - 1:
                        for h in range(HG):
                            q, half = h // 2, PD * (h % 2)
                            e_h = e_end[0:n, i, g * HG + h:g * HG + h + 1].broadcast_to((n, PD))
                            mm = pe.matmul(banks[half:half + PD, 1, 256 + q * NSEQ:256 + (q + 1) * NSEQ], e_h,
                                           K[0:n, K_BEND:K_BEND + NSEQ], start=True, stop=True)
                    mm.then_inc(cb_ready, 1)
                    if k >= 1:
                        pe.wait_ge(seg_out, k)
                    for h in range(HG):
                        mm = pe.matmul(banks[0:n, 2 + h // 4, (h % 4) * P:(h % 4) * P + n],
                                       dta[0:n, i, g * HG + h:g * HG + h + 1].broadcast_to((n, n)), tri(i, n), start=True, stop=True)
                    mm.then_inc(acs_ready, 1)

                def gate(k):
                    g, i = unit(k)
                    n = ROWS[i]
                    pe.wait_ge(wz_in[g % 2], 16 * (g // 2 + 1))
                    if k >= 1:
                        pe.wait_ge(z_out, k)
                    if g >= 1 and i == 0:
                        pe.wait_ge(hs_out, 8 * g)
                    for q in range(KD):
                        mm = pe.matmul(banks[0:n, 7, :], sb.xT[:, q, P * i:P * i + n], wz[:, g % 2, q, :], start=(q == 0), stop=(q == KD - 1))
                    mm.then_inc(z_ready, 1)

                def outputs(k):
                    g, i = unit(k)
                    n = ROWS[i]
                    at = slice(P * i, P * i + n)
                    pe.wait_ge(w_out, k + 1)
                    pe.wait_ge(scaled, k + 1)
                    if k >= 1:
                        pe.wait_ge(y_step, 2 * k)
                    for h in range(HG):
                        pe.matmul(banks[0:n, 4, h * PD:(h + 1) * PD], dec[0:n, k % 2, h, 0:n], xdt[0:n, k % 2, h * PD:(h + 1) * PD], start=True, stop=True)
                    if i < NT - 1:
                        pe.wait_ge(st_new, NT * g + i + 1)
                        pe.matmul(banks[0:n, 5, :], sb.xbcT[:, 20 + g, at], stT[:], start=True, stop=True).then_inc(y_ready, 1)
                        if g >= 1 and i == 0:
                            pe.wait_ge(hs_out, 8 * g)
                        pe.matmul(banks[0:NST, 6, :], b_t[0:n, k % 2, :], xend[0:n, k % 2, :], start=True, stop=True).then_inc(st_ready, 1)
                        return
                    pe.wait_ge(st_new, NT * (g + 1))
                    for q in range(4):
                        mm = pe.transpose(banks[:, 6, q * P:(q + 1) * P], stT[:, q * P:(q + 1) * P], K[:, K_ID:K_ID + P])
                    mm.then_inc(fin_ready, 1)
                    pe.wait_ge(h_in, 64 * (g + 1))
                    pe.wait_ge(of_seq, g + 1)

                    def turn_state(b):
                        if b == 0:
                            pe.wait_ge(z_out, k + 1)
                        elif b == 1:
                            pe.wait_ge(fin_out, g + 1)
                        else:
                            pe.wait_ge(hT_out, NSEQ * g + b - 1)
                        for q in range(4):
                            mm = pe.transpose(banks[:, 7 - b % 2, q * P:(q + 1) * P], h0[:, q, b, :], K[:, K_ID:K_ID + P])
                        mm.then_inc(hT_ready, 1)

                    turn_state(0)
                    for b in range(NSEQ):
                        m = NSEQ * g + b
                        if b + 1 < NSEQ:
                            turn_state(b + 1)
                        pe.wait_ge(hT_out, m + 1)
                        mm = pe.matmul(banks[0:n, 5, :], c_of[:, b, :], h0T[:, b % 2, :], start=(b == 0), stop=(b == NSEQ - 1))
                        mm.then_inc(off_part, 1)
                        if b == NSEQ - 1:
                            pe.wait_ge(off_part, m + 1)
                            pe.sem_inc(y_ready, 1)
                    for u in range(8):
                        q, half = divmod(u, 2)
                        if u >= 2:
                            pe.wait_ge(hs_out, 8 * g + u - 1)
                        mm = pe.matmul(banks[:, 6 + u % 2, :], xend[0:n, k % 2, q * P:(q + 1) * P], b_of[:, 4 * half:4 * half + 4, :],
                                       start=True, stop=True)
                        mm.then_inc(hs_ready, 1)
                    pe.wait_ge(hs_ready, 8 * g + 8)
                    pe.sem_inc(st_ready, 1)

                def turn(k):
                    g, i = unit(k)
                    n = ROWS[i]
                    pe.wait_ge(normed, k + 1)
                    pe.wait_ge(xs_out, min(k + 3, N))
                    if k + 3 > N and k >= 1:
                        pe.wait_ge(yt_out, k)
                    for q in range(4):
                        mm = pe.transpose(banks[:, 0, q * n:(q + 1) * n], y[0:n, k % 2, q * P:(q + 1) * P], K[0:n, K_ID:K_ID + n])
                    mm.then_inc(yt_ready, 1)

                for k in range(N + 2):
                    if k < N:
                        inputs(k)
                    if 1 <= k <= N:
                        gate(k - 1)
                    if k >= 2:
                        turn(k - 2)
                    if 1 <= k <= N:
                        outputs(k - 1)

            @block.scalar
            def _(act):
                act.wait_ge(prep_v, 3)
                act.activation(t2[:], t2[:], ACT.Exp).then_inc(prep_a, 1)
                act.wait_ge(vec_in, 64)
                act.activation(a_b[:], a_b[:], ACT.Exp).then_inc(prep_a, 1)
                act.wait_ge(prep_v, 4)
                act.activation(t3[:], acs[:], ACT.Ln).then_inc(prep_a, 1)
                act.wait_ge(sums_out, 1)
                act.activation(e_acs[:], acs[:], ACT.Exp)
                act.activation(e_end[:], aend[:], ACT.Exp).then_inc(prep_a, 1)
                act.wait_ge(prep_v, 8)
                act.activation(w_end[:], w_end[:], ACT.Exp).then_inc(prep_a, 1)
                for k in range(N + 2):
                    if k < N:
                        g, i = unit(k)
                        n = ROWS[i]
                        act.wait_ge(xs_ready, k + 1)
                        if k >= 2:
                            act.wait_ge(scaled, k - 1)
                        act.activation(xs_t[0:n, k % 2, :], banks[0:n, 0, :], ACT.Copy).then_inc(xs_out, 1)
                        act.wait_ge(seg_out, k + 1)
                        act.activation(dec[0:n, k % 2, :, 0:n], dec[0:n, k % 2, :, 0:n], ACT.Exp).then_inc(dec_out, 1)
                    if 1 <= k <= N:
                        j = k - 1
                        g, i = unit(j)
                        n = ROWS[i]
                        act.wait_ge(z_ready, j + 1)
                        if j >= 1:
                            act.wait_ge(gated, j)
                        act.activation(zs[0:n, :], banks[0:n, 7, :], ACT.Silu).then_inc(z_out, 1)
                    if k >= 2:
                        j = k - 2
                        g, i = unit(j)
                        n = ROWS[i]
                        act.wait_ge(yt_ready, j + 1)
                        act.activation(sb.yT[:, 4 * g:4 * g + 4, P * i:P * i + n], banks[:, 0, 0:4 * n].rearrange("p (q n) -> p q n", q=4),
                                       ACT.Copy).then_inc(yt_out, 1)
                    if 1 <= k <= N:
                        j = k - 1
                        g, i = unit(j)
                        n = ROWS[i]
                        if i == NT - 1:
                            act.wait_ge(fin_ready, g + 1)
                            if g >= 1:
                                act.wait_ge(p_out, 16 * g)
                            act.activation(st_out[:].rearrange("p q n -> p (q n)"), banks[:, 6, :], ACT.Copy).then_inc(fin_out, 1)
                            for b in range(NSEQ):
                                m = NSEQ * g + b
                                act.wait_ge(hT_ready, m + 1)
                                if m >= 2:
                                    act.wait_ge(off_part, m - 1)
                                act.activation(h0T[:, b % 2, :], banks[:, 7 - b % 2, :], ACT.Copy).then_inc(hT_out, 1)
                        act.wait_ge(gated, j + 1)
                        if j >= 1:
                            act.wait_ge(squared, j)
                        act.activation(junk[0:n, :], y[0:n, j % 2, :], ACT.Square, accum_out=ssq[0:n, 0:1]).then_inc(squared, 1)
                        act.wait_ge(mean_ready, j + 1)
                        act.activation(ssq[0:n, 1:2], ssq[0:n, 1:2], ACT.Sqrt).then_inc(rooted, 1)

            @block.vector
            def _(dve):
                all_tiles = lambda t: t[:].unsqueeze(1).broadcast_to((P, NT, SH))
                dve.wait_ge(vec_in, 64)
                dve.tensor_tensor(t1[:], sb.dt[:], all_tiles(dt_b), ALU.add).then_inc(prep_v, 1)
                dve.wait_ge(prep_v, 1)
                dve.tensor_scalar(t2[:], t1[:], -1.0, None, ALU.mult).then_inc(prep_v, 1)
                dve.wait_ge(prep_v, 2)
                dve.tensor_tensor(t2[:], t2[:], t1[:], ALU.min).then_inc(prep_v, 1)
                dve.wait_ge(prep_a, 2)
                dve.tensor_scalar(acs[:], t2[:], 1.0, None, ALU.add).then_inc(prep_v, 1)
                dve.wait_ge(prep_v, 4)
                dve.reciprocal(aend[:], acs[:])
                dve.scalar_tensor_tensor(out=e_acs[:], in0=acs[:], scalar=-1.0, in1=t2[:], op0=ALU.add, op1=ALU.subtract)
                dve.tensor_scalar(t1[:], t1[:], 0.0, None, ALU.max)
                dve.tensor_scalar(a_b[:], a_b[:], -1.0, None, ALU.mult).then_inc(st_step, 1)
                dve.wait_ge(st_step, 1)
                dve.tensor_tensor(e_acs[:], e_acs[:], aend[:], ALU.mult).then_inc(st_step, 1)
                dve.wait_ge(st_step, 2)
                dve.wait_ge(prep_a, 3)
                dve.tensor_tensor(t3[:], t3[:], e_acs[:], ALU.subtract).then_inc(st_step, 1)
                dve.wait_ge(st_step, 3)
                dve.tensor_tensor(sb.dt[:], t3[:], t1[:], ALU.add).then_inc(prep_v, 1)
                dve.wait_ge(prep_v, 5)
                dve.tensor_tensor(dta[:], sb.dt[:], all_tiles(a_b), ALU.mult).then_inc(prep_v, 1)
                dve.wait_ge(prep_v, 6)
                dve.memset(acs[NS:P, NT - 1, :], 0.0)
                dve.memset(aend[NS:P, NT - 1, :], 0.0)
                dve.memset(stT[:], 0.0).then_inc(st_new, 1)
                dve.wait_ge(sums_ready, 1)
                for o, b in ((acs, 0), (aend, 1)):
                    dve.tensor_copy(o[:, 0:4, :], banks[:, b, 0:4 * SH].rearrange("p (i h) -> p i h", i=4))
                    ins = dve.tensor_copy(o[0:NS, 4, :], banks[0:NS, b, 4 * SH:5 * SH])
                ins.then_inc(sums_out, 1)
                dve.wait_ge(sums_out, 1)
                dve.wait_ge(prep_a, 3)
                dve.tensor_tensor(t1[:], aend[:], acs[:], ALU.subtract).then_inc(prep_v, 1)
                dve.wait_ge(prep_v, 7)
                dve.tensor_copy(w_end[:], t1[:]).then_inc(prep_v, 1)
                dve.wait_ge(prep_a, 5)
                dve.tensor_tensor(w_end[:], w_end[:], sb.dt[:], ALU.mult).then_inc(prep_v, 1)
                for k in range(N + 1):
                    if k < N:
                        g, i = unit(k)
                        n = ROWS[i]
                        dve.wait_ge(cb_ready, k + 1)
                        if k >= 2:
                            dve.wait_ge(st_ready, k - 1)
                        if k >= 1:
                            dve.wait_ge(w_out, k)
                        dve.tensor_copy(b_t[0:n, k % 2, :], banks[0:n, 1, 0:P])
                        ins = dve.tensor_tensor(cb[0:n, 0:n], banks[0:n, 1, P:P + n], tri(i, n), ALU.mult)
                        if i == NT - 1:
                            dve.tensor_copy(e_seq[:], banks[:, 1, 256:256 + 4 * NSEQ].rearrange("p (q b) -> p q b", q=4)).then_inc(e_out, 1)
                            dve.wait_ge(e_out, g + 1)
                            dve.sem_inc(cb_out, 1)
                        else:
                            ins.then_inc(cb_out, 1)
                        dve.wait_ge(acs_ready, k + 1)
                        if k >= 2:
                            dve.wait_ge(y_ready, k - 1)
                        for h in range(HG):
                            ins = dve.tensor_scalar(dec[0:n, k % 2, h, 0:n], banks[0:n, 2 + h // 4, (h % 4) * P:(h % 4) * P + n],
                                                    acs[0:n, i, g * HG + h:g * HG + h + 1], 0.0, ALU.subtract, ALU.min)
                        ins.then_inc(seg_out, 1)
                        dve.wait_ge(dec_out, k + 1)
                        dve.wait_ge(cb_out, k + 1)
                        dve.tensor_tensor(dec[0:n, k % 2, :, 0:n], dec[0:n, k % 2, :, 0:n], cb[0:n, 0:n].unsqueeze(1).broadcast_to((n, HG, n)), ALU.mult).then_inc(w_out, 1)
                    if k >= 1:
                        j = k - 1
                        g, i = unit(j)
                        n = ROWS[i]
                        hs = slice(g * HG, (g + 1) * HG)
                        dve.wait_ge(y_ready, j + 1)
                        dve.tensor_tensor(heads(off[0:n], n), heads(banks[0:n, 5, :], n), e_acs[0:n, i, hs].unsqueeze(2).broadcast_to((n, HG, PD)),
                                          ALU.mult).then_inc(y_step, 1)
                        dve.wait_ge(y_step, 2 * j + 1)
                        if j >= 2:
                            dve.wait_ge(yt_ready, j - 1)
                        dve.wait_ge(scaled, j + 1)
                        dve.tensor_tensor(y[0:n, j % 2, :], off[0:n], xd[0:n, j % 2, :], ALU.add).then_inc(y_sum, 1)
                        dve.wait_ge(y_sum, j + 1)
                        dve.tensor_tensor(y[0:n, j % 2, :], y[0:n, j % 2, :], banks[0:n, 4, :], ALU.add).then_inc(y_step, 1)
                        dve.wait_ge(y_step, 2 * j + 2)
                        dve.wait_ge(z_out, j + 1)
                        dve.tensor_tensor(y[0:n, j % 2, :], y[0:n, j % 2, :], zs[0:n, :], ALU.mult).then_inc(gated, 1)
                        if i < NT - 1:
                            dve.wait_ge(st_ready, j + 1)
                            dve.tensor_tensor(heads(stT[:], P), heads(stT[:], P), e_end[:, i, hs].unsqueeze(2).broadcast_to((P, HG, PD)), ALU.mult).then_inc(st_step, 1)
                            dve.wait_ge(st_step, 4 + (NT - 1) * g + i)
                            dve.tensor_tensor(stT[:], stT[:], banks[:, 6, :], ALU.add).then_inc(st_new, 1)
                        else:
                            for u in range(8):
                                q, half = divmod(u, 2)
                                dve.wait_ge(hs_ready, 8 * g + u + 1)
                                for b in range(4):
                                    s = 4 * half + b
                                    ins = dve.scalar_tensor_tensor(out=h0[:, q, s, :], in0=h0[:, q, s, :], scalar=e_seq[:, q, s:s + 1],
                                                                   in1=banks[:, 6 + u % 2, b * NST:(b + 1) * NST], op0=ALU.mult, op1=ALU.add)
                                ins.then_inc(hs_out, 1)
                            if g + 1 < G:
                                dve.memset(stT[:], 0.0).then_inc(st_new, 1)
                        dve.wait_ge(squared, j + 1)
                        dve.tensor_scalar(ssq[0:n, 1:2], ssq[0:n, 0:1], 1.0 / GW, RMS_EPS, ALU.mult, ALU.add).then_inc(mean_ready, 1)
                        dve.wait_ge(rooted, j + 1)
                        dve.reciprocal(ssq[0:n, 1:2], ssq[0:n, 1:2]).then_inc(inverse, 1)
                        dve.wait_ge(inverse, j + 1)
                        dve.scalar_tensor_tensor(out=y[0:n, j % 2, :], in0=y[0:n, j % 2, :], scalar=ssq[0:n, 1:2],
                                                 in1=gn[0:n, g * GW:(g + 1) * GW], op0=ALU.mult, op1=ALU.mult).then_inc(normed, 1)


def stage_out(nc, io, sb):
    with ExitStack() as ctx:
        sem = ctx.enter_context(signals(nc, "out"))
        buf = lambda n, s: ctx.enter_context(nc.sbuf_tensor(n, s, F32))
        w = buf("w_o", [P, 2, KD, 512])
        x_tok = buf("x_tok7", [P, NT, D])
        g_b, b_b = buf("g1_b", [P, D]), buf("b1_b", [P, D])
        stats = buf("stats7", [P, 2, 6])
        mv = buf("mv7", [P, NT, 2])
        banks = ctx.enter_context(nc.psum_tensor("banks7", [P, 8, 512], F32))
        w_in_, x_in, gb_in, mixed, summed, stat, mean, rooted, inverse, normed, scaled, done, stored = (sem(n) for n in (
            "w_in", "x_in", "gb_in", "mixed", "summed", "stat", "mean", "rooted", "inverse", "normed", "scaled", "done", "stored"))
        w_view = io.wo.rearrange("(k p) n -> p k n", p=P)
        h = sb.h

        with nc.Block() as block:
            @block.sync
            def _(sp):
                for c in range(2):
                    sp.dma_start(w[:, c], w_view[:, :, c * 512:(c + 1) * 512]).then_inc(w_in_, 16)
                for i in range(NT):
                    sp.dma_start(x_tok[0:ROWS[i], i, :], token_dram(io.xp, io.xs, i)).then_inc(x_in, 16)
                sp.dma_start(g_b[:], io.g1.broadcast_to((P, D))).then_inc(gb_in, 16)
                sp.dma_start(b_b[:], io.b1.broadcast_to((P, D))).then_inc(gb_in, 16)
                for i in range(NT):
                    sp.wait_ge(done, i + 1)
                    sp.dma_start(io.h_rows[P * i:P * i + ROWS[i], :], h[0:ROWS[i], i, :]).then_inc(stored, 16)
                sp.wait_ge(stored, 16 * NT)

            @block.tensor
            def _(pe):
                pe.wait_ge(w_in_, 32)
                for i in range(NT):
                    n = ROWS[i]
                    if i >= 4:
                        pe.wait_ge(summed, i - 3)
                    for c in range(2):
                        for k in range(KD):
                            mm = pe.matmul(banks[0:n, 2 * (i % 4) + c, :], sb.mergedT[:, k, P * i:P * i + n], w[:, c, k, :],
                                           start=(k == 0), stop=(k == KD - 1))
                    mm.then_inc(mixed, 1)

            @block.vector
            def _(dve):
                dve.memset(mv[:], 1.0).then_inc(inverse, 1)
                dve.wait_ge(inverse, 1)
                dve.wait_ge(x_in, 16 * NT)
                for i in range(NT):
                    n = ROWS[i]
                    dve.wait_ge(mixed, i + 1)
                    for c in range(2):
                        at = slice(c * 512, (c + 1) * 512)
                        ins = dve.scalar_tensor_tensor(out=h[0:n, i, at], in0=x_tok[0:n, i, at], scalar=ALPHA,
                                                       in1=banks[0:n, 2 * (i % 4) + c, :], op0=ALU.mult, op1=ALU.add)
                    ins.then_inc(summed, 1)
                    dve.wait_ge(summed, i + 1)
                    if i >= 1:
                        dve.wait_ge(mean, i)
                    for c in range(2):
                        ins = dve.bn_stats(stats[0:n, c, :], h[0:n, i, c * 512:(c + 1) * 512])
                    ins.then_inc(stat, 1)
                    dve.wait_ge(stat, i + 1)
                    dve.bn_aggr(mv[0:n, i, :], stats[0:n].rearrange("p c s -> p (c s)")).then_inc(mean, 1)
                dve.wait_ge(mean, NT)
                dve.tensor_scalar(mv[:, :, 1:2], mv[:, :, 1:2], LN_EPS, None, ALU.add).then_inc(inverse, 1)
                dve.wait_ge(rooted, 1)
                dve.reciprocal(mv[:, :, 1:2], mv[:, :, 1:2]).then_inc(inverse, 1)
                dve.wait_ge(inverse, 3)
                dve.wait_ge(gb_in, 32)
                for i in range(NT):
                    n = ROWS[i]
                    dve.tensor_scalar(h[0:n, i, :], h[0:n, i, :], mv[0:n, i, 0:1], mv[0:n, i, 1:2], ALU.subtract, ALU.mult).then_inc(normed, 1)
                    dve.wait_ge(normed, i + 1)
                    dve.tensor_tensor(h[0:n, i, :], h[0:n, i, :], g_b[0:n], ALU.mult).then_inc(scaled, 1)
                    dve.wait_ge(scaled, i + 1)
                    dve.tensor_tensor(h[0:n, i, :], h[0:n, i, :], b_b[0:n], ALU.add).then_inc(done, 1)

            @block.scalar
            def _(act):
                act.wait_ge(inverse, 2)
                act.activation(mv[:, :, 1:2], mv[:, :, 1:2], ACT.Sqrt).then_inc(rooted, 1)


NRAW = 8
AHEAD = 4


def expert_room(sb, w_more):
    room = sb.mergedT[:].rearrange("p k t -> p (k t)")
    slots = [room[:, 2 * D * j:2 * D * (j + 1)].rearrange("p (c n) -> p c n", c=2) for j in range(2)]
    return slots + [w_more[:, j] for j in range(NRAW - 2)]


def weight_slot(io, e, s):
    if s < 8:
        h, q = divmod(s, 4)
        src = io.wgu[bass.ds(e, 1), 2 * P * q:2 * P * (q + 1), h * FF:(h + 1) * FF]
    else:
        src = io.wdn[bass.ds(e, 1), 2 * P * (s - 8):2 * P * (s - 7), :]
    return src.rearrange("a (c p) n -> p c (a n)", p=P)


def stage_route(nc, io, sb):
    with ExitStack() as ctx:
        sem = ctx.enter_context(signals(nc, "route"))
        buf = lambda n, s, d=F32: ctx.enter_context(nc.sbuf_tensor(n, s, d))
        K = sb.const
        hT = buf("hT8", [P, KD, T])
        wr = buf("wr", [P, KD, E])
        br = buf("br", [P, E])
        lg, gt, eq, run, sel, ex, place, pick, part = (buf(n, [P, NT, E]) for n in ("lg", "gt", "eq", "run", "sel", "ex", "place", "pick", "part"))
        top = buf("top", [P, NT, 8])
        few = buf("few", [P, NT])
        total = buf("total", [P, NT])
        slot_f = buf("slot_f", [P, NT, TOPK])
        pair = buf("pair", [P, NT * TOPK + 1, 2], I32)
        empty = buf("empty", [P, E * CAP // P, 2], I32)
        count = buf("count", [P, E])
        flag, nth, code, exp_of = (buf(n, [1, 4 * E]) for n in ("flag", "nth", "code", "exp_of"))
        match, found = buf("match", [1, NOVF + 1, 4 * E]), buf("found", [1, NOVF + 1, 4 * E])
        listed = buf("listed", [1, 2, NOVF + 1])
        banks = ctx.enter_context(nc.psum_tensor("banks8", [P, 8, 512], F32))
        wr_in, turned, turned_out, logit, vec, expd, ranked = (sem(n) for n in ("wr_in", "turned", "turned_out", "logit", "vec", "expd", "ranked"))
        chosen, slotted, listing, zeroed, cleared, scattered, tabled, listed_done = (sem(n) for n in (
            "chosen", "slotted", "listing", "zeroed", "cleared", "scattered", "tabled", "listed_done"))
        first_in = sem("first_in")
        bc = lambda t: t.broadcast_to((P, NT, E))

        with nc.Block() as block:
            @block.sync
            def _(sp):
                sp.dma_start(wr[:], io.wr.rearrange("(k p) n -> p k n", p=P)).then_inc(wr_in, 16)
                sp.dma_start(br[:], io.br.broadcast_to((P, E))).then_inc(wr_in, 16)
                sp.wait_ge(zeroed, 2)
                sp.dma_start(io.slots.rearrange("(p c) a -> p c a", p=P), empty[:]).then_inc(cleared, 16)
                for s in range(AHEAD):
                    sp.dma_start(sb.w_raw[s], weight_slot(io, 0, s)).then_inc(first_in, 16)
                sp.wait_ge(scattered, 16 * NT * TOPK)
                first = io.slots.rearrange("(e c) a -> c e a", c=CAP)[0:P]
                with nc.allow_non_contiguous_dma(reason="a table of 8-byte pairs"):
                    sp.dma_start(sb.tok[:, 0:E, :], first).then_inc(tabled, 16)
                sp.wait_ge(listed_done, 3)
                for q in range(0, NOVF + 1, 2):
                    s = sp.value_load(sb.item_slot[0:1, q:q + 1], min_val=0, max_val=E * CAP - P)
                    sp.dma_start(sb.tok[:, E + q, :], io.slots[bass.ds(s, P), :]).then_inc(tabled, 16)
                sp.wait_ge(tabled, 16 * (NOVF + 2))
                sp.wait_ge(first_in, 16 * AHEAD)

            @block.gpsimd
            def _(pool):
                pool.tensor_copy(pair[:], K[:, K_PAIR:K_BASE].rearrange("p (n a) -> p n a", a=2)).then_inc(zeroed, 1)
                pool.wait_ge(zeroed, 1)
                pool.tensor_copy(empty[:], pair[:, NT * TOPK:, :].broadcast_to((P, E * CAP // P, 2))).then_inc(zeroed, 1)
                pool.wait_ge(cleared, 16)
                pool.wait_ge(zeroed, 2)
                pool.wait_ge(slotted, 1)
                for i in range(NT):
                    for k in range(TOPK):
                        n = ROWS[i]
                        pool.indirect_dma_start(out=io.slots, out_offset=bass.IndirectOffsetOnAxis(ap=sb.slot[0:n, i, k:k + 1].bitcast(U32), axis=0),
                                                in_=pair[0:n, i * TOPK + k, :], in_offset=None).then_inc(scattered, 16)

            @block.tensor
            def _(pe):
                for i in range(NT):
                    n = ROWS[i]
                    for h in range(2):
                        u = 2 * i + h
                        if u >= 4:
                            pe.wait_ge(turned_out, u - 3)
                        for k in range(4):
                            mm = pe.transpose(banks[:, u % 4, k * n:(k + 1) * n], sb.h[0:n, i, (4 * h + k) * P:(4 * h + k + 1) * P], K[0:n, K_ID:K_ID + n])
                        mm.then_inc(turned, 1)
                pe.wait_ge(wr_in, 32)
                for i in range(NT):
                    n = ROWS[i]
                    pe.wait_ge(turned_out, 2 * i + 2)
                    for k in range(KD):
                        mm = pe.matmul(banks[0:n, 4 + i % 2, 64 * i:64 * i + E], hT[:, k, P * i:P * i + n], wr[:, k, :], start=(k == 0), stop=(k == KD - 1))
                    mm.then_inc(logit, 1)
                pe.wait_ge(chosen, 1)
                for i in range(NT):
                    n = ROWS[i]
                    for j in range(i):
                        pe.matmul(banks[0:n, 6, i * E:(i + 1) * E], K[:, K_ONE:K_ONE + n], sel[:, j, :], start=(j == 0), stop=False)
                    pe.matmul(banks[0:n, 6, i * E:(i + 1) * E], K[0:n, K_STRICT:K_STRICT + n], sel[0:n, i, :], start=(i == 0), stop=True)
                for j in range(NT):
                    mm = pe.matmul(banks[:, 7, 0:E], K[:, K_ONE:K_ONE + P], sel[:, j, :], start=(j == 0), stop=(j == NT - 1))
                mm.then_inc(ranked, 1)

            @block.scalar
            def _(act):
                for u in range(2 * NT):
                    i, h = divmod(u, 2)
                    n = ROWS[i]
                    act.wait_ge(turned, u + 1)
                    act.activation(hT[:, 4 * h:4 * h + 4, P * i:P * i + n], banks[:, u % 4, 0:4 * n].rearrange("p (k n) -> p k n", k=4),
                                   ACT.Copy).then_inc(turned_out, 1)
                act.wait_ge(expd, 1)
                act.activation(ex[:], ex[:], ACT.Exp).then_inc(expd, 1)
                act.wait_ge(scattered, 16 * NT * TOPK)
                act.wait_ge(listed_done, 3)
                for q in range(1, NOVF + 1, 2):
                    s = act.value_load(sb.item_slot[0:1, q:q + 1], min_val=0, max_val=E * CAP - P)
                    act.dma_start(sb.tok[:, E + q, :], io.slots[bass.ds(s, P), :]).then_inc(tabled, 16)

            @block.vector
            def _(dve):
                done = [0]

                def then(ins):
                    done[0] += 1
                    ins.then_inc(vec, 1)
                    dve.wait_ge(vec, done[0])

                then(dve.memset(lg[NS:P, NT - 1, :], 0.0))
                dve.wait_ge(wr_in, 32)
                for i in range(NT):
                    n = ROWS[i]
                    dve.wait_ge(logit, NT)
                    ins = dve.tensor_tensor(lg[0:n, i, :], banks[0:n, 4 + i % 2, 64 * i:64 * i + E], br[0:n], ALU.add)
                then(ins)
                for i in range(NT):
                    ins = dve.max(out=top[:, i, :], in_=lg[:, i, :])
                then(ins)
                fourth = bc(top[:, :, TOPK - 1:TOPK])
                dve.tensor_tensor(gt[:], lg[:], fourth, ALU.is_gt)
                dve.tensor_tensor(eq[:], lg[:], fourth, ALU.is_equal)
                then(dve.tensor_tensor(ex[:], lg[:], bc(top[:, :, 0:1]), ALU.subtract))
                dve.sem_inc(expd, 1)
                for i in range(NT):
                    dve.tensor_tensor_scan(run[:, i, :], K[:, K_ONE:K_ONE + E], eq[:, i, :], 0.0, ALU.mult, ALU.add)
                then(dve.reduce_sum(few[:], gt[:], AX))
                then(dve.tensor_scalar(few[:], few[:], -1.0, float(TOPK), ALU.mult, ALU.add))
                then(dve.tensor_tensor(run[:], run[:], bc(few[:].unsqueeze(2)), ALU.is_le))
                then(dve.tensor_tensor(run[:], run[:], eq[:], ALU.mult))
                then(dve.tensor_tensor(sel[:], run[:], gt[:], ALU.add))
                dve.memset(sel[NS:P, NT - 1, :], 0.0).then_inc(chosen, 1)
                dve.wait_ge(chosen, 1)
                dve.wait_ge(expd, 2)
                for i in range(NT):
                    dve.tensor_tensor_scan(run[:, i, :], K[:, K_ONE:K_ONE + E], sel[:, i, :], 0.0, ALU.mult, ALU.add)
                then(dve.tensor_tensor(ex[:], ex[:], sel[:], ALU.mult))
                then(dve.reduce_sum(total[:], ex[:], AX))
                then(dve.tensor_scalar(total[:], total[:], 1e-30, None, ALU.max))
                then(dve.reciprocal(total[:], total[:]))
                then(dve.tensor_tensor(ex[:], ex[:], bc(total[:].unsqueeze(2)), ALU.mult))
                dve.wait_ge(ranked, 1)
                base = K[:, K_BASE:K_BASE + E]
                dve.tensor_tensor(place[:, 0:4, :], banks[:, 6, 0:4 * E].rearrange("p (i e) -> p i e", i=4),
                                  base.unsqueeze(1).broadcast_to((P, 4, E)), ALU.add)
                dve.memset(place[NS:P, 4, :], 0.0)
                dve.tensor_tensor(place[0:NS, 4, :], banks[0:NS, 6, 4 * E:5 * E], base[0:NS], ALU.add)
                then(dve.tensor_copy(count[:], banks[:, 7, 0:E]))
                for k in range(TOPK):
                    then(dve.scalar_tensor_tensor(out=pick[:], in0=run[:], scalar=float(k + 1), in1=sel[:], op0=ALU.is_equal, op1=ALU.mult))
                    then(dve.tensor_tensor(part[:], pick[:], place[:], ALU.mult))
                    dve.reduce_sum(slot_f[:, :, k:k + 1], part[:], AX)
                    then(dve.tensor_tensor(pick[:], pick[:], ex[:], ALU.mult))
                    then(dve.reduce_sum(sb.gate[:, :, k:k + 1], pick[:], AX))
                dve.tensor_copy(sb.slot[:], slot_f[:]).then_inc(slotted, 1)
                for j in range(4):
                    ins = dve.tensor_scalar(flag[:, j * E:(j + 1) * E], count[0:1, :], float(P * (j + 1)), None, ALU.is_gt)
                then(ins)
                dve.tensor_tensor(code[:], flag[:], K[0:1, K_CODE:K_CODE + 4 * E], ALU.mult)
                dve.tensor_tensor(exp_of[:], flag[:], K[0:1, K_EXP:K_EXP + 4 * E], ALU.mult)
                then(dve.tensor_tensor_scan(nth[:], K[0:1, K_ONE:K_ONE + P], flag[:], 0.0, ALU.mult, ALU.add))
                wide = lambda t: t.unsqueeze(1).broadcast_to((1, NOVF + 1, 4 * E))
                then(dve.tensor_tensor(match[:], wide(nth[:]), K[0:1, K_ITEM:K_ITEM + NOVF + 1].unsqueeze(2).broadcast_to((1, NOVF + 1, 4 * E)), ALU.is_equal))
                for o, c in ((0, code), (1, exp_of)):
                    then(dve.tensor_tensor(found[:], match[:], wide(c[:]), ALU.mult))
                    then(dve.reduce_sum(listed[:, o, :], found[:], AX))
                dve.tensor_copy(sb.item_slot[:], listed[:, 0, :]).then_inc(listed_done, 1)
                dve.tensor_copy(sb.item_expert[:, 0:E], K[0:1, K_EXP:K_EXP + E])
                dve.tensor_copy(sb.item_expert[:, E:E + NOVF + 1], listed[:, 1, :]).then_inc(listed_done, 1)
                dve.tensor_copy(sb.n_over[:], nth[:, 4 * E - 1:4 * E]).then_inc(listed_done, 1)


def stage_experts(nc, io, sb):
    NW = 12
    NHI = 4
    HALF = 2 * FF // 2
    NB = 3 * D // 512
    LROW = 32
    BR = LROW + NB
    POOL_SLOTS = (10, 11)
    VEC_SLOTS = tuple(s for s in range(NW) if s not in POOL_SLOTS)
    with ExitStack() as ctx:
        sem = ctx.enter_context(signals(nc, "experts"))
        buf = lambda n, s, d=F32: ctx.enter_context(nc.sbuf_tensor(n, s, d))
        K = sb.const
        room = sb.xT[:].rearrange("p k t -> p (k t)")
        w_hi, w_lo = buf("w_hi", [P, NHI, 2, HALF], F32R), buf("w_lo", [P, NHI, 2, HALF], F32R)
        b_raw = buf("b_raw", [BR, 2, 512])
        b_tmp = buf("b_tmp", [BR, 512], F32R)
        b_two = buf("b_two", [BR, 2, 512], F32R)
        pick = buf("pick9", [BR, NB, P], F32R)
        x_raw, y_out, hid = room[:, 0:D], room[:, D:2 * D], room[:, 2 * D:3 * D]
        g_c, u_c, sg = (room[:, 3 * D + 512 * j:3 * D + 512 * (j + 1)] for j in range(3))
        x_hi, x_lo, h_hi, h_lo = (buf(n, [P, KD, P], F32R) for n in ("x_hi", "x_lo", "h_hi", "h_lo"))
        banks = ctx.enter_context(nc.psum_tensor("banks9", [P, 8, 512], F32))
        index = buf("index9", [P, 2, 2], I32)
        w_in_ = [sem(f"w_in{s}") for s in range(NW)]
        b_in = [sem("b_in0"), sem("b_in1")]
        x_in, indexed, carried, b_part, b_split, picked = (sem(n) for n in ("x_in", "indexed", "carried", "b_part", "b_split", "picked"))
        w_used, hi_ready, lo_v, lo_p = (sem(n) for n in ("w_used", "hi_ready", "lo_v", "lo_p"))
        turned, turned_hi, turned_lo = (sem(n) for n in ("turned", "turned_hi", "turned_lo"))
        gu_ready, gu_read, clamped, sig_out, hid_ready, multiplied = (sem(n) for n in (
            "gu_ready", "gu_read", "clamped", "sig_out", "hid_ready", "multiplied"))
        y_ready, y_copied, y_stored, y_free = (sem(n) for n in ("y_ready", "y_copied", "y_stored", "y_free"))
        U_H0, U_X0, U_X1, U_H1 = range(4)

        def turns(it, unit):
            return unit if isinstance(it, int) else it * 4 + (unit - 1)

        def raw(s, par):
            return sb.w_raw[(par * NW + s) % NRAW]

        def wait_low(eng, it, s):
            for slots, made in ((POOL_SLOTS, lo_p), (VEC_SLOTS, lo_v)):
                if s in slots:
                    eng.wait_ge(made, it * len(slots) + (len(slots) + slots.index(s) + 1))

        def items(eng, body):
            with eng.Fori(0, E // 2) as i:
                body(i * 2, 0)
                body(i * 2 + 1, 1)
            n = eng.value_load(sb.n_over[0:1, 0:1], min_val=0, max_val=NOVF)
            with eng.Fori(0, (NOVF + 1) // 2) as i:
                for par in range(2):
                    q = i * 2 + par
                    with eng.If(q < n):
                        body(q + E, par)

        with nc.Block() as block:
            @block.sync
            def _(sp):
                def load(e, it, s, par):
                    if not isinstance(it, int):
                        if s < NRAW:
                            wait_low(sp, it - 1, s - NRAW + NW)
                        else:
                            wait_low(sp, it, s - NRAW)
                    sp.dma_start(raw(s, par), weight_slot(io, e, s)).then_inc(w_in_[s], 16)

                def biases(e, it, par):
                    sp.wait_ge(b_split, it + 1)
                    for p0 in (0, LROW):
                        sp.dma_start(b_raw[p0:p0 + 4, par, :], io.bgu[bass.ds(e, 1), :].rearrange("a (j n) -> (a j) n", j=4)).then_inc(b_in[par], 16)
                        sp.dma_start(b_raw[p0 + 4:p0 + 6, par, :], io.bdn[bass.ds(e, 1), :].rearrange("a (j n) -> (a j) n", j=2)).then_inc(b_in[par], 16)

                def expert(it):
                    return sp.value_load(sb.item_expert[0:1, bass.ds(it, 1)], min_val=0, max_val=E - 1)

                def run(it, par):
                    e, e_next = expert(it), expert(it + 1)
                    for s in range(AHEAD, NW):
                        load(e, it, s, par)
                        if s == 7:
                            biases(e_next, it + 1, 1 - par)
                    for s in range(AHEAD):
                        load(e_next, it + 1, s, 1 - par)

                biases(0, 0, 0)
                for s in range(AHEAD):
                    sp.sem_inc(w_in_[s], 16)
                sp.wait_ge(x_in, 16)
                items(sp, run)

            @block.gpsimd
            def _(pool):
                def gather(it, par):
                    pool.tensor_copy(index[:, par:par + 1, :], sb.tok[:, bass.ds(it, 1), :]).then_inc(indexed, 1)
                    pool.wait_ge(indexed, it + 1)
                    if not isinstance(it, int):
                        pool.wait_ge(turned, it * 4 - 2)
                    pool.sem_inc(carried, 1)
                    pool.indirect_dma_start(out=x_raw, out_offset=None, in_=io.h_rows,
                                            in_offset=bass.IndirectOffsetOnAxis(ap=index[:, par, 0:1].bitcast(U32), axis=0)).then_inc(x_in, 16)
                    pool.wait_ge(x_in, it * 16 + 16)

                def split_biases(it, par):
                    pool.wait_ge(b_in[par], (it - par) * 32 + 64)
                    if not isinstance(it, int):
                        pool.wait_ge(lo_p, (it + 1) * len(POOL_SLOTS))
                    pool.sem_inc(carried, 1)
                    pool.tensor_copy(b_two[0:NB, par, :], b_raw[0:NB, par, :]).then_inc(b_part, 1)
                    pool.tensor_copy(b_tmp[LROW:BR, :], b_raw[LROW:BR, par, :]).then_inc(b_part, 1)
                    pool.wait_ge(b_part, it * 2 + 2)
                    pool.tensor_tensor(b_two[LROW:BR, par, :], b_raw[LROW:BR, par, :], b_tmp[LROW:BR, :].bitcast(F32), ALU.subtract).then_inc(b_split, 1)
                    pool.wait_ge(b_split, it + 3)

                def low(it, s, par):
                    pool.wait_ge(hi_ready, it * NW + s + 1)
                    pool.tensor_tensor(w_lo[:, s % NHI], raw(s, par), w_hi[:, s % NHI].bitcast(F32), ALU.subtract).then_inc(lo_p, 1)

                def run(it, par):
                    gather(it + 1, 1 - par)
                    for s in POOL_SLOTS:
                        low(it, s, par)
                    split_biases(it + 1, 1 - par)
                    pool.wait_ge(y_copied, it + 2)
                    pool.sem_inc(carried, 1)
                    pool.indirect_dma_start(out=io.y_rows, out_offset=bass.IndirectOffsetOnAxis(ap=index[:, par, 1:2].bitcast(U32), axis=0),
                                            in_=y_out, in_offset=None).then_inc(y_stored, 16)
                    pool.wait_ge(y_stored, it * 16 + 16)
                    pool.sem_inc(y_free, 1)

                pool.sem_inc(b_split, 2)
                pool.sem_inc(y_free, 1)
                gather(0, 0)
                pool.wait_ge(picked, 2)
                split_biases(0, 0)
                items(pool, run)

            @block.tensor
            def _(pe):
                def turn(it, unit, src, k0):
                    if not isinstance(it, int):
                        pe.wait_ge(turned_lo, turns(it, unit) - 2)
                    for k in range(4):
                        mm = pe.transpose(banks[:, 6 + unit % 2, k * P:(k + 1) * P], src[:, (k0 + k) * P:(k0 + k + 1) * P], K[:, K_ID:K_ID + P])
                    mm.then_inc(turned, 1)

                def products(s, j, hi, lo, k, bank, start):
                    for x, parts in ((hi, (w_hi[:, s % NHI], w_lo[:, s % NHI])), (lo, (w_hi[:, s % NHI],))):
                        for part in parts:
                            for c in range(2):
                                mm = pe.matmul(banks[:, bank + c, :], x[:, k, :], part[:, j, c * 512:(c + 1) * 512], start=start, stop=False)
                            start = False
                    return mm

                def add_bias(par, bank, row):
                    for c in range(2):
                        mm = pe.matmul(banks[:, bank + c, :], pick[:, row + c, :], b_two[:, par, :], start=False, stop=True)
                    return mm

                def run(it, par):
                    pe.wait_ge(b_split, it + 3)
                    for h in range(2):
                        pe.wait_ge(gu_read, it * 2 + h + 1)
                        for q in range(4):
                            wait_low(pe, it, 4 * h + q)
                            for j in range(2):
                                mm = products(4 * h + q, j, x_hi, x_lo, 2 * q + j, 2 * h, q == 0 and j == 0)
                            mm.then_inc(w_used, 1)
                        add_bias(par, 2 * h, 2 * h).then_inc(gu_ready, 1)
                    pe.wait_ge(hid_ready, it * 2 + 2)
                    turn(it + 1, U_H0, hid, 0)
                    pe.wait_ge(x_in, it * 16 + 32)
                    turn(it + 1, U_X0, x_raw, 0)
                    pe.wait_ge(y_copied, it + 1)
                    for q in range(4):
                        if q == 1:
                            turn(it + 1, U_X1, x_raw, 4)
                            pe.wait_ge(hid_ready, it * 2 + 3)
                            turn(it + 1, U_H1, hid, 4)
                        if q == 2:
                            pe.wait_ge(turned_lo, turns(it + 1, U_H1))
                        if q == 0:
                            pe.wait_ge(turned_lo, turns(it + 1, U_H0))
                        wait_low(pe, it, 8 + q)
                        for j in range(2):
                            mm = products(8 + q, j, h_hi, h_lo, 2 * q + j, 4, q == 0 and j == 0)
                        mm.then_inc(w_used, 1)
                    add_bias(par, 4, 4).then_inc(y_ready, 1)

                pe.sem_inc(w_used, NW)
                pe.wait_ge(picked, 2)
                pe.wait_ge(x_in, 16)
                turn(0, U_X0, x_raw, 0)
                turn(0, U_X1, x_raw, 4)
                pe.wait_ge(turned_lo, 2)
                items(pe, run)

            @block.scalar
            def _(act):
                def high(it, s, par):
                    act.wait_ge(w_in_[s], it * 16 + 16)
                    if not (isinstance(it, int) and s < NHI):
                        act.wait_ge(w_used, it * NW + s + 1 + NW - NHI)
                    act.activation(w_hi[:, s % NHI], raw(s, par), ACT.Copy).then_inc(hi_ready, 1)

                def turned_high(it, unit, dst, k0):
                    act.wait_ge(turned, turns(it, unit))
                    act.activation(dst[:, k0:k0 + 4, :], banks[:, 6 + unit % 2, :].rearrange("p (k n) -> p k n", k=4), ACT.Copy).then_inc(turned_hi, 1)

                def sigmoid(it, h):
                    act.wait_ge(clamped, it * 2 + h + 1)
                    act.activation(sg, g_c, ACT.Sigmoid, scale=SW_ALPHA).then_inc(sig_out, 1)

                def run(it, par):
                    for s in range(AHEAD, 8):
                        high(it, s, par)
                    sigmoid(it, 0)
                    for s in range(8, NW - 1):
                        high(it, s, par)
                    turned_high(it + 1, U_H0, h_hi, 0)
                    sigmoid(it, 1)
                    turned_high(it + 1, U_X0, x_hi, 0)
                    high(it, NW - 1, par)
                    turned_high(it + 1, U_X1, x_hi, 4)
                    turned_high(it + 1, U_H1, h_hi, 4)
                    for s in range(AHEAD):
                        high(it + 1, s, 1 - par)
                    act.wait_ge(y_ready, it + 1)
                    act.wait_ge(y_free, it + 1)
                    act.activation(y_out, banks[:, 4:6, :].rearrange("p c n -> p (c n)"), ACT.Copy).then_inc(y_copied, 1)

                act.sem_inc(y_copied, 1)
                for s in range(AHEAD):
                    high(0, s, 0)
                turned_high(0, U_X0, x_hi, 0)
                turned_high(0, U_X1, x_hi, 4)
                items(act, run)

            @block.vector
            def _(dve):
                def low(it, s, par):
                    if s in POOL_SLOTS:
                        return
                    dve.wait_ge(hi_ready, it * NW + s + 1)
                    dve.tensor_tensor(w_lo[:, s % NHI], raw(s, par), w_hi[:, s % NHI].bitcast(F32), ALU.subtract).then_inc(lo_v, 1)

                def turned_low(it, unit, hi, lo, k0):
                    dve.wait_ge(turned_hi, turns(it, unit))
                    dve.tensor_tensor(lo[:, k0:k0 + 4, :], banks[:, 6 + unit % 2, :].rearrange("p (k n) -> p k n", k=4),
                                      hi[:, k0:k0 + 4, :].bitcast(F32), ALU.subtract).then_inc(turned_lo, 1)

                def clamp(it, h):
                    pair = banks[:, 2 * h:2 * h + 2, :].rearrange("p c (f t) -> p c f t", t=2)
                    two = lambda t: t.rearrange("p (c f) -> p c f", c=2)
                    dve.wait_ge(gu_ready, it * 2 + h + 1)
                    dve.wait_ge(hid_ready, it * 2 + h + 1)
                    dve.tensor_scalar(two(g_c), pair[:, :, :, 0], SW_LIMIT, None, ALU.min).then_inc(clamped, 1)
                    dve.tensor_scalar(two(u_c), pair[:, :, :, 1], SW_LIMIT, -SW_LIMIT, ALU.min, ALU.max).then_inc(gu_read, 1)

                def gate(it, h):
                    dve.wait_ge(clamped, it * 2 + h + 1)
                    dve.wait_ge(gu_read, it * 2 + h + 3)
                    dve.scalar_tensor_tensor(out=u_c, in0=u_c, scalar=1.0, in1=g_c, op0=ALU.add, op1=ALU.mult).then_inc(multiplied, 1)
                    dve.wait_ge(multiplied, it * 2 + h + 1)
                    dve.wait_ge(sig_out, it * 2 + h + 1)
                    dve.tensor_tensor(hid[:, h * 512:(h + 1) * 512], u_c, sg, ALU.mult).then_inc(hid_ready, 1)

                def run(it, par):
                    for s in range(AHEAD, 7):
                        low(it, s, par)
                    clamp(it, 0)
                    low(it, 7, par)
                    gate(it, 0)
                    low(it, 8, par)
                    low(it, 9, par)
                    clamp(it, 1)
                    turned_low(it + 1, U_H0, h_hi, h_lo, 0)
                    gate(it, 1)
                    turned_low(it + 1, U_X0, x_hi, x_lo, 0)
                    turned_low(it + 1, U_X1, x_hi, x_lo, 4)
                    low(it, 10, par)
                    turned_low(it + 1, U_H1, h_hi, h_lo, 4)
                    low(it, 11, par)
                    for s in range(AHEAD):
                        low(it + 1, s, 1 - par)

                dve.tensor_copy(b_two[:], K[0:BR, K_STRICT:K_STRICT + 1].unsqueeze(2).broadcast_to((BR, 2, 512))).then_inc(picked, 1)
                dve.tensor_copy(pick[:], K[0:BR, K_PICK:K_PICK + NB].unsqueeze(2).broadcast_to((BR, NB, P))).then_inc(picked, 1)
                dve.sem_inc(gu_read, 2)
                dve.sem_inc(lo_v, len(VEC_SLOTS))
                dve.sem_inc(lo_p, len(POOL_SLOTS))
                dve.sem_inc(hid_ready, 1)
                for s in range(AHEAD):
                    low(0, s, 0)
                turned_low(0, U_X0, x_hi, x_lo, 0)
                turned_low(0, U_X1, x_hi, x_lo, 4)
                items(dve, run)


def stage_combine(nc, io, sb):
    with ExitStack() as ctx:
        sem = ctx.enter_context(signals(nc, "combine"))
        buf = lambda n, s: ctx.enter_context(nc.sbuf_tensor(n, s, F32))
        rows = buf("rows10", [P, 3, TOPK, D])
        g_b, b_b = buf("g2_b", [P, D]), buf("b2_b", [P, D])
        stats = buf("stats10", [P, 2, 6])
        mv = buf("mv10", [P, NT, 2])
        row_in = [sem(f"row_in{i}") for i in range(3)]
        gb_in, summed, stat, mean, rooted, inverse, normed, scaled, done, stored, added = (sem(n) for n in (
            "gb_in", "summed", "stat", "mean", "rooted", "inverse", "normed", "scaled", "done", "stored", "added"))
        raised = sem("raised")
        h = sb.h

        with nc.Block() as block:
            @block.sync
            def _(sp):
                def load(i):
                    src = io.y_rows[TOPK * P * i:TOPK * (P * i + ROWS[i]), :].rearrange("(t k) d -> t k d", k=TOPK)
                    sp.dma_start(rows[0:ROWS[i], i % 3], src).then_inc(row_in[i % 3], 16)

                for i in range(3):
                    load(i)
                    if i == 0:
                        sp.dma_start(g_b[:], io.g2.broadcast_to((P, D))).then_inc(gb_in, 16)
                        sp.dma_start(b_b[:], io.b2.broadcast_to((P, D))).then_inc(gb_in, 16)
                for i in range(NT):
                    if i + 3 < NT:
                        sp.wait_ge(summed, i + 1)
                        load(i + 3)
                    sp.wait_ge(done, i + 1)
                    sp.dma_start(token_dram(io.o_yp, io.o_ys, i), h[0:ROWS[i], i, :]).then_inc(stored, 16)
                sp.wait_ge(stored, 16 * NT)

            @block.gpsimd
            def _(pool):
                pool.wait_ge(gb_in, 32)
                for i in range(NT):
                    x = h[0:ROWS[i], i, :]
                    pool.wait_ge(normed, i + 1)
                    pool.tensor_tensor(x, x, g_b[0:ROWS[i]], ALU.mult).then_inc(scaled, 1)
                    pool.wait_ge(scaled, i + 1)
                    pool.tensor_tensor(x, x, b_b[0:ROWS[i]], ALU.add).then_inc(done, 1)

            @block.scalar
            def _(act):
                for i in range(NT):
                    act.activation(h[0:ROWS[i], i, :], h[0:ROWS[i], i, :], ACT.Copy, scale=ALPHA).then_inc(raised, 1)
                for i in range(NT):
                    n = ROWS[i]
                    act.wait_ge(mean, 2 * i + 2)
                    act.activation(mv[0:n, i, 1:2], mv[0:n, i, 1:2], ACT.Sqrt).then_inc(rooted, 1)

            @block.vector
            def _(dve):
                for i in range(NT):
                    n = ROWS[i]
                    x = h[0:n, i, :]
                    dve.wait_ge(raised, i + 1)
                    dve.wait_ge(row_in[i % 3], 16 * (i // 3 + 1))
                    for k in range(TOPK):
                        if k >= 1:
                            dve.wait_ge(added, (TOPK - 1) * i + k)
                        dve.scalar_tensor_tensor(out=x, in0=rows[0:n, i % 3, k, :], scalar=sb.gate[0:n, i, k:k + 1], in1=x,
                                                 op0=ALU.mult, op1=ALU.add).then_inc(added if k < TOPK - 1 else summed, 1)
                    dve.wait_ge(summed, i + 1)
                    for c in range(2):
                        ins = dve.bn_stats(stats[0:n, c, :], h[0:n, i, c * 512:(c + 1) * 512])
                    ins.then_inc(stat, 1)
                    dve.wait_ge(stat, i + 1)
                    dve.bn_aggr(mv[0:n, i, :], stats[0:n].rearrange("p c s -> p (c s)")).then_inc(mean, 1)
                    dve.wait_ge(mean, 2 * i + 1)
                    dve.tensor_scalar(mv[0:n, i, 1:2], mv[0:n, i, 1:2], LN_EPS, None, ALU.add).then_inc(mean, 1)
                    dve.wait_ge(rooted, i + 1)
                    dve.reciprocal(mv[0:n, i, 1:2], mv[0:n, i, 1:2]).then_inc(inverse, 1)
                    dve.wait_ge(inverse, i + 1)
                    dve.tensor_scalar(x, x, mv[0:n, i, 0:1], mv[0:n, i, 1:2], ALU.subtract, ALU.mult).then_inc(normed, 1)


class Tensors:
    pass


def program(nc, io):
    with ExitStack() as ctx:
        buf = lambda n, s: ctx.enter_context(nc.sbuf_tensor(n, s, F32))
        sb = Tensors()
        sb.const, sb.xT, sb.dt = buf("const", [P, K_W]), buf("xT", [P, KD, T]), buf("dt", [P, NT, SH])
        sb.mergedT = buf("mergedT", [P, KD, T])
        with ExitStack() as att:
            abuf = lambda n, s: att.enter_context(nc.sbuf_tensor(n, s, F32))
            sb.cT = abuf("cT", [P, 2, T])
            sb.krT = abuf("krT", [ROPE, T])
            sb.oT = abuf("oT", [P, HEADS, T])
            sb.wkv = abuf("wkv", [P, 2, HEADS * (NOPE + VH)])
            sb.qlS = abuf("qlS", [P, 2, HEADS, NS])
            sb.qrS = abuf("qrS", [ROPE, HEADS, NS])
            with ExitStack() as own:
                obuf = lambda n, s: own.enter_context(nc.sbuf_tensor(n, s, F32))
                sb.rope = obuf("rope", [P, 2, NT, ROPE // 2])
                sb.c_tok = obuf("c_tok", [P, NT, KVL])
                sb.kr_tok = obuf("kr_tok", [P, NT, ROPE])
                sb.qnT = obuf("qnT", [P, 2, T])
                stage_latents(nc, io, sb)
                stage_prompt_attention(nc, io, sb)
            stage_sample_attention(nc, io, sb)
            stage_turn_x(nc, io, sb)
            stage_merge(nc, io, sb, C_GB, io.wb, lambda k: sb.oT[:, k, :], HEADS, True, True, "_b")
        with ExitStack() as scan:
            sb.xbcT = scan.enter_context(nc.sbuf_tensor("xbcT", [P, NCT, T], F32))
            sb.yT = sb.xbcT[:, 0:DI // P, :]
            stage_conv(nc, io, sb)
            stage_ssd(nc, io, sb)
            stage_merge(nc, io, sb, C_GA, io.wa, lambda k: sb.yT[:, k, :], DI // P, False, False, "_a")
        with ExitStack() as moe:
            mbuf = lambda n, s, d=F32: moe.enter_context(nc.sbuf_tensor(n, s, d))
            sb.h = mbuf("h", [P, NT, D])
            sb.gate = mbuf("gate", [P, NT, TOPK])
            sb.slot = mbuf("slot", [P, NT, TOPK], I32)
            sb.tok = mbuf("tok", [P, ITEMS + 2, 2], I32)
            sb.item_expert = mbuf("item_expert", [1, ITEMS + 2], I32)
            sb.item_slot = mbuf("item_slot", [1, NOVF + 1], I32)
            sb.n_over = mbuf("n_over", [1, 1], I32)
            stage_out(nc, io, sb)
            sb.w_raw = expert_room(sb, mbuf("w_raw", [P, NRAW - 2, 2, FF]))
            stage_route(nc, io, sb)
            stage_experts(nc, io, sb)
            stage_combine(nc, io, sb)


INPUTS = ('x_prompt', 'x_sample', 'cache_kv_latent', 'cache_k_rope', 'state_ssm',
        'state_conv', 'page_table', 'w_in', 'ssd_conv_w', 'ssd_conv_b',
        'ssd_dt_bias', 'ssd_a_log', 'ssd_d', 'ssd_norm_g', 'mla_q_norm_g',
        'w_q_b', 'mla_kv_norm_g', 'w_kv_b', 'w_branch_a', 'w_branch_b',
        'w_out', 'ln1_g', 'ln1_b', 'router_w', 'router_b', 'exp_w_gu',
        'exp_b_gu', 'exp_w_down', 'exp_b_down', 'ln2_g', 'ln2_b')
OUTPUTS = [(1, SEQ, D), (NSEQ, TS, D), (1, 1, SEQ, KVL), (1, 1, SEQ, ROPE), (1, 1, SH, PD, NST), (1, 1, KC - 1, CONV),
         (1, NSEQ, TS, KVL), (1, NSEQ, TS, ROPE), (1, NSEQ, SH, PD, NST), (1, NSEQ, KC - 1, CONV)]


def io_of(nc, ins, outs):
    scratch = lambda n, s, d=F32: nc.dram_tensor(n, s, d).ap()
    i = ins
    io = Tensors()
    io.xp = i['x_prompt'][0]
    io.xs = i['x_sample'].rearrange("b t d -> (b t) d")
    io.cache_c = i['cache_kv_latent'][0]
    io.cache_r = i['cache_k_rope'][0]
    io.ssm = i['state_ssm'][0].rearrange("b h p n -> b (h p) n")
    io.conv = i['state_conv'][0].rearrange("b k c -> (b k) c")
    io.pages = i['page_table']
    io.w_in = i['w_in'][0]
    io.conv_w = i['ssd_conv_w'][0]
    io.conv_b = i['ssd_conv_b']
    io.dt_bias = i['ssd_dt_bias']
    io.a_log = i['ssd_a_log']
    io.d_skip = i['ssd_d']
    io.gn = i['ssd_norm_g']
    io.gq = i['mla_q_norm_g']
    io.wq = i['w_q_b'][0]
    io.gkv = i['mla_kv_norm_g']
    io.wkv = i['w_kv_b'][0]
    io.wa = i['w_branch_a'][0]
    io.wb = i['w_branch_b'][0]
    io.wo = i['w_out'][0]
    io.g1 = i['ln1_g']
    io.b1 = i['ln1_b']
    io.wr = i['router_w'][0]
    io.br = i['router_b']
    io.wgu = i['exp_w_gu'][0]
    io.bgu = i['exp_b_gu'][0]
    io.wdn = i['exp_w_down'][0]
    io.bdn = i['exp_b_down'][0]
    io.g2 = i['ln2_g']
    io.b2 = i['ln2_b']
    io.consts = i['consts']
    io.rope = i['rope']
    io.o_yp = outs[0][0]
    io.o_ys = outs[1].rearrange("b t d -> (b t) d")
    io.o_cp = outs[2][0, 0]
    io.o_krp = outs[3][0, 0]
    io.o_ssmp = outs[4][0, 0].rearrange("h p n -> (h p) n")
    io.o_convp = outs[5][0, 0]
    io.o_cs = outs[6][0].rearrange("b t d -> (b t) d")
    io.o_krs = outs[7][0].rearrange("b t d -> (b t) d")
    io.o_ssms = outs[8][0].rearrange("b h p n -> b (h p) n")
    io.o_convs = outs[9][0].rearrange("b k c -> (b k) c")
    io.h_rows = scratch("h_rows", (T, D))
    io.slots = scratch("slots", (E * CAP, 2), I32)
    io.y_rows = scratch("y_rows", (T * TOPK + 1, D))
    return io


def kernel(**inputs):
    import concourse.bacc as _bacc
    from concourse.bass_utils import run_bass_kernel_spmd as _run

    nc = _bacc.Bacc("TRN2", target_bir_lowering=False, num_devices=1)
    arrays, ins = {}, {}
    given = {name: np.ascontiguousarray(inputs[name]) for name in INPUTS}
    given['consts'], given['rope'] = constants(), rope_tables()
    for name, a in given.items():
        arrays[f"in_{name}"] = a
        ins[name] = nc.dram_tensor(f"in_{name}", a.shape, mybir.dt.from_np(a.dtype), kind="ExternalInput").ap()
    outs = [nc.dram_tensor(f"out_{i}", s, F32, kind="ExternalOutput").ap() for i, s in enumerate(OUTPUTS)]
    program(nc, io_of(nc, ins, outs))
    r = _run(nc, [arrays], core_ids=[0])
    return tuple(r.results[0][f"out_{i}"] for i in range(len(OUTPUTS)))
```
